# Optimizing a Trainium2 kernel written in Bass

```python
import jax
import jax.numpy as jnp
from jax import lax
import numpy as np

D_MODEL = 1024
BATCH = 1
SEQ = 256
DEPTH = 2

GRID_W = 64
CTX_LEN = 256
EPS = 1e-6
NEG_INF = -1e30
D_A = 1024
K_A = 3
N_HEADS = 8
N_KV = 2
HEAD_DIM = 128
GROUP = N_HEADS // N_KV
Q_W = N_HEADS * HEAD_DIM
KV_W = N_KV * HEAD_DIM
WINDOW = 128
BLOCK = 128
ROPE_THETA = 10000.0
D_C = 1024
K_C = 4
LRU_BLOCKS = 8
LRU_BS = D_C // LRU_BLOCKS
LRU_C = 8.0
D_D = 1024
K_D = 31
N_BRANCH = 4
D_FF = -(-8 * D_MODEL // (3 * 256)) * 256
SPLIT_SIZES = (D_A, D_A, D_A, Q_W, KV_W, KV_W, D_C, D_C, D_D, D_D, N_BRANCH * D_MODEL)
N_IN = 3 * D_A + Q_W + 2 * KV_W + 2 * D_C + 2 * D_D + N_BRANCH * D_MODEL

kernel_name = 'hybrid_parallel_dit_block'

def _rmsnorm(x, g):
    x32 = x.astype(jnp.float32)
    y = x32 * lax.rsqrt(jnp.mean(jnp.square(x32), axis=-1, keepdims=True) + EPS)
    return (y * g.astype(jnp.float32)).astype(x.dtype)

def _layernorm(x, g, b):
    x32 = x.astype(jnp.float32)
    mu = jnp.mean(x32, axis=-1, keepdims=True)
    var = jnp.mean(jnp.square(x32 - mu), axis=-1, keepdims=True)
    y = (x32 - mu) * lax.rsqrt(var + EPS) * g.astype(jnp.float32) + b.astype(jnp.float32)
    return y.astype(x.dtype)

def _modulate(x, g, shift, scale):
    return _rmsnorm(x, g) * (1.0 + scale) + shift

def _dwconv(x, w):
    k = w.shape[0]
    left = k // 2
    return lax.conv_general_dilated(
        x, w[:, None, :].astype(x.dtype), window_strides=(1,),
        padding=[(left, k - 1 - left)],
        dimension_numbers=('NWC', 'WIO', 'NWC'),
        feature_group_count=x.shape[-1])

def _split_cols(p):
    cuts, acc = [], 0
    for s in SPLIT_SIZES[:-1]:
        acc += s
        cuts.append(acc)
    return jnp.split(p, cuts, axis=-1)

def _heads(t, n):
    return t.reshape(t.shape[0], t.shape[1], n, HEAD_DIM)

def _axial_rope(n_tok):
    rows = n_tok // GRID_W
    row = jnp.repeat(jnp.arange(rows), GRID_W).astype(jnp.float32)
    col = jnp.tile(jnp.arange(GRID_W), rows).astype(jnp.float32)
    half = HEAD_DIM // 2
    inv_freq = ROPE_THETA ** (-jnp.arange(0, half, 2, dtype=jnp.float32) / half)
    ang_r = row[:, None] * inv_freq[None, :]
    ang_c = col[:, None] * inv_freq[None, :]
    ang = jnp.concatenate([ang_r, ang_r, ang_c, ang_c], axis=-1)
    return jnp.cos(ang), jnp.sin(ang)

def _rotate(t, cos, sin):
    t1, t2, t3, t4 = jnp.split(t, 4, axis=-1)
    t_rot = jnp.concatenate([-t2, t1, -t4, t3], axis=-1)
    return (t * cos[:, None, :] + t_rot * sin[:, None, :]).astype(t.dtype)

def _band(t, nb):
    tb = t.reshape(t.shape[0], nb, BLOCK, t.shape[2], t.shape[3])
    tp = jnp.pad(tb, ((0, 0), (1, 1), (0, 0), (0, 0), (0, 0)))
    return jnp.concatenate([tp[:, :-2], tp[:, 1:-1], tp[:, 2:]], axis=2)

def _window_attention(q, k, v, kc, vc, sink):
    B, L = q.shape[0], q.shape[1]
    nb = L // BLOCK
    n_loc = 3 * BLOCK
    n_ctx = kc.shape[1]
    scale = HEAD_DIM ** -0.5
    qb = q.reshape(B, nb, BLOCK, N_KV, GROUP, HEAD_DIM)
    kb, vb = _band(k, nb), _band(v, nb)
    s_loc = jnp.einsum('bnqkgd,bnskd->bnkgqs', qb, kb, preferred_element_type=jnp.float32) * scale
    blk = jnp.arange(nb)[:, None]
    qpos = blk * BLOCK + jnp.arange(BLOCK)[None, :]
    kpos = (blk - 1) * BLOCK + jnp.arange(n_loc)[None, :]
    valid = ((jnp.abs(qpos[:, :, None] - kpos[:, None, :]) <= WINDOW)
             & (kpos[:, None, :] >= 0) & (kpos[:, None, :] < L))
    s_loc = jnp.where(valid[None, :, None, None], s_loc, NEG_INF)
    s_ctx = jnp.einsum('bnqkgd,bskd->bnkgqs', qb, kc, preferred_element_type=jnp.float32) * scale
    s_sink = jnp.broadcast_to(sink.astype(jnp.float32).reshape(1, 1, N_KV, GROUP, 1, 1), s_loc.shape[:-1] + (1,))
    p = jax.nn.softmax(jnp.concatenate([s_loc, s_ctx, s_sink], axis=-1), axis=-1).astype(v.dtype)
    o = (jnp.einsum('bnkgqs,bnskd->bnqkgd', p[..., :n_loc], vb)
         + jnp.einsum('bnkgqs,bskd->bnqkgd', p[..., n_loc:n_loc + n_ctx], vc))
    return o.reshape(B, L, Q_W)

def _context_attention(q, k, v, sink):
    B, Lc = q.shape[0], q.shape[1]
    qg = q.reshape(B, Lc, N_KV, GROUP, HEAD_DIM)
    s = jnp.einsum('bqkgd,bskd->bkgqs', qg, k, preferred_element_type=jnp.float32) * (HEAD_DIM ** -0.5)
    s_sink = jnp.broadcast_to(sink.astype(jnp.float32).reshape(1, N_KV, GROUP, 1, 1), s.shape[:-1] + (1,))
    p = jax.nn.softmax(jnp.concatenate([s, s_sink], axis=-1), axis=-1)[..., :Lc].astype(v.dtype)
    o = jnp.einsum('bkgqs,bskd->bqkgd', p, v)
    return o.reshape(B, Lc, Q_W)

def _linear_scan(a, b, reverse):
    def combine(e1, e2):
        a1, b1 = e1
        a2, b2 = e2
        return a1 * a2, a2 * b1 + b2
    return lax.associative_scan(combine, (a, b), axis=1, reverse=reverse)

def _rglru_gates(u, wa, ba, wx, bx, lam):
    B, L, C = u.shape
    ub = u.reshape(B, L, LRU_BLOCKS, LRU_BS)
    r = jax.nn.sigmoid(jnp.einsum('blnc,ncd->blnd', ub, wa, preferred_element_type=jnp.float32).reshape(B, L, C)
                       + ba.astype(jnp.float32))
    i = jax.nn.sigmoid(jnp.einsum('blnc,ncd->blnd', ub, wx, preferred_element_type=jnp.float32).reshape(B, L, C)
                       + bx.astype(jnp.float32))
    log_a = -LRU_C * jax.nn.softplus(-lam.astype(jnp.float32)) * r
    a = jnp.exp(log_a)
    b = jnp.sqrt(-jnp.expm1(2.0 * log_a)) * (i * u.astype(jnp.float32))
    return a, b

def _rglru_direction(uc, u, wa, ba, wx, bx, lam, reverse):
    ac, bc = _rglru_gates(uc, wa, ba, wx, bx, lam)
    _, hc = _linear_scan(ac, bc, reverse)
    h0 = hc[:, 0] if reverse else hc[:, -1]
    a, b = _rglru_gates(u, wa, ba, wx, bx, lam)
    a_cum, h = _linear_scan(a, b, reverse)
    return hc, h + a_cum * h0[:, None, :]

def _rglru_bidir(uc, u, wa, ba, wx, bx, lam):
    hc_f, h_f = _rglru_direction(uc, u, wa[0], ba[0], wx[0], bx[0], lam[0], False)
    hc_b, h_b = _rglru_direction(uc, u, wa[1], ba[1], wx[1], bx[1], lam[1], True)
    return (hc_f + hc_b).astype(u.dtype), (h_f + h_b).astype(u.dtype)

def _short_conv(b_gate, c_gate, u, w):
    return b_gate * _dwconv(c_gate * u, w)

def _conformer_conv(u_val, u_gate, w, bias, g, beta):
    z = _dwconv(u_val * jax.nn.sigmoid(u_gate), w) + bias
    return jax.nn.silu(_layernorm(z, g, beta))

def _merge(gate_logits, ys, w_out):
    B, L = gate_logits.shape[0], gate_logits.shape[1]
    g = jax.nn.sigmoid(gate_logits).reshape(B, L, N_BRANCH, D_MODEL)
    y = jnp.stack(ys, axis=2)
    return jnp.sum(g * y, axis=2) @ w_out

def _swiglu(h, w_in, w_out):
    gate, up = jnp.split(h @ w_in, 2, axis=-1)
    return (jax.nn.silu(gate) * up) @ w_out

def _mix_sublayer(h, hc, cos, sin, need_ctx, w_in, conv_a, sink, conv_c, conv_c_b, lru_wa, lru_ba,
                  lru_wx, lru_bx, lru_lam, conv_d, conv_d_b, ln_d_g, ln_d_b,
                  w_a_out, w_b_out, w_c_out, w_d_out, w_out):
    a_b, a_c, a_u, q, k, v, r_g, r_u, d_v, d_g, gl = _split_cols(h @ w_in)
    ca_b, ca_c, ca_u, cq, ck, cv, cr_g, cr_u, cd_v, cd_g, cgl = _split_cols(hc @ w_in)
    kc, vc = _heads(ck, N_KV), _heads(cv, N_KV)
    y_b = _window_attention(_rotate(_heads(q, N_HEADS), cos, sin), _rotate(_heads(k, N_KV), cos, sin),
                            _heads(v, N_KV), kc, vc, sink)
    u = _dwconv(r_u, conv_c) + conv_c_b
    uc = _dwconv(cr_u, conv_c) + conv_c_b
    rec_c, rec = _rglru_bidir(uc, u, lru_wa, lru_ba, lru_wx, lru_bx, lru_lam)
    ys = (_short_conv(a_b, a_c, a_u, conv_a) @ w_a_out,
          y_b @ w_b_out,
          (jax.nn.gelu(r_g) * rec) @ w_c_out,
          _conformer_conv(d_v, d_g, conv_d, conv_d_b, ln_d_g, ln_d_b) @ w_d_out)
    out = _merge(gl, ys, w_out)
    if not need_ctx:
        return out, None
    ys_c = (_short_conv(ca_b, ca_c, ca_u, conv_a) @ w_a_out,
            _context_attention(_heads(cq, N_HEADS), kc, vc, sink) @ w_b_out,
            (jax.nn.gelu(cr_g) * rec_c) @ w_c_out,
            _conformer_conv(cd_v, cd_g, conv_d, conv_d_b, ln_d_g, ln_d_b) @ w_d_out)
    return out, _merge(cgl, ys_c, w_out)

def setup_inputs(seed: int = 0) -> dict:
    key = jax.random.key(seed)
    ks = iter(jax.random.split(key, 40))
    f32 = jnp.float32

    def nrm(shape, scale):
        return jax.random.normal(next(ks), shape, f32) * scale

    u = jax.random.uniform(next(ks), (DEPTH, 2, D_C), f32, 0.9, 0.999)
    s = u ** (1.0 / LRU_C)
    lam = jnp.log(s) - jnp.log1p(-s)
    return {
        'x': nrm((BATCH, SEQ, D_MODEL), 1.0),
        'c': nrm((BATCH, D_MODEL), 1.0),
        'ctx': nrm((BATCH, CTX_LEN, D_MODEL), 1.0),
        'c_ctx': nrm((D_MODEL,), 1.0),
        'w_mod': nrm((DEPTH, D_MODEL, 6 * D_MODEL), 0.5 * D_MODEL ** -0.5),
        'b_mod': nrm((DEPTH, 6 * D_MODEL), 0.02),
        'g_mix': 1.0 + nrm((DEPTH, D_MODEL), 0.02),
        'w_in': nrm((DEPTH, D_MODEL, N_IN), D_MODEL ** -0.5),
        'conv_a': nrm((DEPTH, K_A, D_A), K_A ** -0.5),
        'sink': nrm((DEPTH, N_HEADS), 0.5),
        'conv_c': nrm((DEPTH, K_C, D_C), K_C ** -0.5),
        'conv_c_b': nrm((DEPTH, D_C), 0.02),
        'lru_wa': nrm((DEPTH, 2, LRU_BLOCKS, LRU_BS, LRU_BS), LRU_BS ** -0.5),
        'lru_ba': nrm((DEPTH, 2, D_C), 0.02),
        'lru_wx': nrm((DEPTH, 2, LRU_BLOCKS, LRU_BS, LRU_BS), LRU_BS ** -0.5),
        'lru_bx': nrm((DEPTH, 2, D_C), 0.02),
        'lru_lam': lam,
        'conv_d': nrm((DEPTH, K_D, D_D), K_D ** -0.5),
        'conv_d_b': nrm((DEPTH, D_D), 0.02),
        'ln_d_g': 1.0 + nrm((DEPTH, D_D), 0.02),
        'ln_d_b': nrm((DEPTH, D_D), 0.02),
        'w_a_out': nrm((DEPTH, D_A, D_MODEL), D_A ** -0.5),
        'w_b_out': nrm((DEPTH, Q_W, D_MODEL), Q_W ** -0.5),
        'w_c_out': nrm((DEPTH, D_C, D_MODEL), D_C ** -0.5),
        'w_d_out': nrm((DEPTH, D_D, D_MODEL), D_D ** -0.5),
        'w_out': nrm((DEPTH, D_MODEL, D_MODEL), D_MODEL ** -0.5),
        'g_ffn': 1.0 + nrm((DEPTH, D_MODEL), 0.02),
        'w_ffn_in': nrm((DEPTH, D_MODEL, 2 * D_FF), D_MODEL ** -0.5),
        'w_ffn_out': nrm((DEPTH, D_FF, D_MODEL), D_FF ** -0.5),
        'g_final': 1.0 + nrm((D_MODEL,), 0.02),
    }

def reference(x, c, ctx, c_ctx, w_mod, b_mod, g_mix, w_in, conv_a, sink, conv_c, conv_c_b, lru_wa, lru_ba,
              lru_wx, lru_bx, lru_lam, conv_d, conv_d_b, ln_d_g, ln_d_b, w_a_out, w_b_out, w_c_out, w_d_out,
              w_out, g_ffn, w_ffn_in, w_ffn_out, g_final):
    cos, sin = _axial_rope(x.shape[1])
    xc = ctx
    for l in range(DEPTH):
        need_ctx = l < DEPTH - 1
        m = jax.nn.silu(c) @ w_mod[l] + b_mod[l]
        mc = jax.nn.silu(c_ctx) @ w_mod[l] + b_mod[l]
        sh1, sc1, gt1, sh2, sc2, gt2 = jnp.split(m[:, None, :], 6, axis=-1)
        csh1, csc1, cgt1, csh2, csc2, cgt2 = jnp.split(mc[None, None, :], 6, axis=-1)
        o, oc = _mix_sublayer(
            _modulate(x, g_mix[l], sh1, sc1), _modulate(xc, g_mix[l], csh1, csc1), cos, sin, need_ctx,
            w_in[l], conv_a[l], sink[l], conv_c[l], conv_c_b[l], lru_wa[l], lru_ba[l], lru_wx[l], lru_bx[l],
            lru_lam[l], conv_d[l], conv_d_b[l], ln_d_g[l], ln_d_b[l], w_a_out[l], w_b_out[l], w_c_out[l],
            w_d_out[l], w_out[l])
        x = x + gt1 * o
        x = x + gt2 * _swiglu(_modulate(x, g_ffn[l], sh2, sc2), w_ffn_in[l], w_ffn_out[l])
        if need_ctx:
            xc = xc + cgt1 * oc
            xc = xc + cgt2 * _swiglu(_modulate(xc, g_ffn[l], csh2, csc2), w_ffn_in[l], w_ffn_out[l])
    return _rmsnorm(x, g_final)


_drawn_inputs = setup_inputs


def setup_inputs(seed=0):
    import zlib

    import numpy as np

    out = dict(_drawn_inputs(seed))
    spreads = {}
    factors = {'g_mix': 3.714,
     'sink': 8.0,
     'lru_ba': 48.656,
     'lru_bx': 37.798,
     'conv_d_b': 38.489,
     'ln_d_g': 64.0,
     'ln_d_b': 64.0,
     'g_ffn': 7.502,
     'g_final': 8.419,
     'conv_c_b': 3.563}
    for name, (base, spread) in spreads.items():
        noise = np.random.default_rng([zlib.crc32(name.encode()), seed]).standard_normal(out[name].shape)
        drawn = base * np.exp(spread * noise) if base else spread * noise
        out[name] = jnp.asarray(drawn.astype(out[name].dtype))
    for name, factor in factors.items():
        out[name] = (out[name] * factor).astype(out[name].dtype)
    return out
```

```python
from contextlib import ExitStack

import numpy as np
import concourse.bass as bass
from concourse import mybir

P = 128
F32 = mybir.dt.float32
F32R = mybir.dt.float32r
ALU = mybir.AluOpType
ACT = mybir.ActivationFunctionType
AX = mybir.AxisListType
ds = bass.ds

DEPTH = 2
D = 1024
KC = D // P
NX = 256
NC = 256
NT = NX + NC
HEADS, KVH, HD = 8, 2, 128
SCALE = float(HD) ** -0.5
EPS = 1e-6
FF_TILES = 22
FF_PARTS = (8, 8, 6)
TAPS_A, TAPS_C, TAPS_D = 3, 4, 31
PAD = 15
SEG = NX + 2 * PAD
GW = 2 * SEG
SLAB = KC * 2 * P
HALF = SLAB // 2
NMOD = 6 * KC // 2
GELU_C = 0.7978845608028654
NEG = -1e30

_cols, _at = {}, 0
for _name, _n in (("b_mod", 48), ("g_mix", 8), ("g_ffn", 8), ("conv_a", 24), ("conv_c", 32), ("conv_c_b", 8),
                  ("ba", 16), ("bx", 16), ("lam", 16), ("conv_d", 248), ("conv_d_b", 8), ("ln_g", 8), ("ln_b", 8),
                  ("g_final", 8), ("sink", 8)):
    _cols[_name] = _at
    _at += _n
NPRM = _at

STAGES = [("c_in", 8), ("c_out", 8), ("a_cu", 8), ("a_b", 4), ("a_out", 8), ("kv", 2), ("q", 4), ("d_in", 8),
          ("b_out", 8), ("d_out", 8), ("w_out", 4)]
for _f, _n in enumerate(FF_PARTS):
    STAGES += [(f"ff_in{_f}", _n), (f"ff_out{_f}", 4)]
LAYER_SLABS = sum(n for _, n in STAGES)


def pair_base(layer, stage):
    n = layer * LAYER_SLABS
    for name, k in STAGES:
        if name == stage:
            return n // 2
        n += k
    raise KeyError(stage)


class Steps:

    def __init__(self, sem, names):
        self.sem = sem
        self.names = names.split()

    def at(self, n, name):
        return n * len(self.names) + self.names.index(name) + 1


def build(nc, stream, modw, lruw, xT, cT, prm, rope, consts, outT):
    with ExitStack() as ctx:
        def sb(name, n, dt=F32):
            return ctx.enter_context(nc.sbuf_tensor(name, [P, n], dt))

        def sem(name):
            return ctx.enter_context(nc.semaphore(name))

        X = sb("X", KC * NT)
        HH = sb("HH", KC * NT, F32R)
        HL = sb("HL", KC * NT, F32R)
        ZH = sb("ZH", KC * NT, F32R)
        ZL = sb("ZL", KC * NT, F32R)
        S = sb("S", KC * NT)
        G = sb("G", KC * GW)
        CD = sb("CD", KC * NT)
        RAW = sb("RAW", 2 * SLAB)
        WH = sb("WH", 2 * SLAB, F32R)
        WL = sb("WL", 2 * SLAB, F32R)
        TMP = sb("TMP", 7 * NT)
        PRM = sb("PRM", DEPTH * NPRM)
        ROPE = sb("ROPE", 2 * NX)
        CST = sb("CST", 5 * P)
        MOD = sb("MOD", 2 * 48)
        AMP = sb("AMP", 2 * 2 * KC)
        SILC = sb("SILC", 2 * 2 * KC)
        SG = sb("SG", 2 * KC)
        LC = sb("LC", 3 * 16)
        LT = sb("LT", 5 * 16)
        EPST = sb("EPST", 1)
        SM = sb("SM", 14)
        PS = ctx.enter_context(nc.psum_tensor("PS", [P, 8, 512], F32))

        EPSC = EPST[:, 0:1]
        IDENT, ONES, ROT = CST[:, 0:P], CST[:, P:2 * P], CST[:, 2 * P:3 * P]
        TRI = [CST[:, 3 * P:4 * P], CST[:, 4 * P:5 * P]]
        COS, SIN = ROPE[:, 0:NX], ROPE[:, NX:2 * NX]

        def tmp(i, a=0, b=NT):
            return TMP[:, i * NT + a:i * NT + b]

        KT = [tmp(0), tmp(1)]
        VT = [[TMP[:, (2 + c // 2) * NT + (c % 2) * 256 + kv * P:(2 + c // 2) * NT + (c % 2) * 256 + kv * P + P]
               for c in range(4)] for kv in range(KVH)]
        PR, PT, QS = tmp(4), tmp(5), tmp(6)

        def par(l, name, i=0, n=1):
            return PRM[:, ds(i + (l * NPRM + _cols[name]), n)] if not isinstance(i, int) else \
                PRM[:, l * NPRM + _cols[name] + i:l * NPRM + _cols[name] + i + n]

        def row(t, j, w=NT, a=0):
            return t[:, j * NT + a:j * NT + a + w] if isinstance(j, int) else t[:, ds(j * NT + a, w)]

        def lc(j, n, d):
            return LC[:, ds(n + (16 * j + 8 * d), 1)]

        def bank(b, w=NT, a=0):
            return PS[:, b, a:a + w]

        def seqs(ap, c):
            return ap.rearrange("p (c t) -> p c t", c=c)

        def padded(j, c, shift=0):
            base = G[:, j * GW:j * GW + GW] if isinstance(j, int) else G[:, ds(j * GW, GW)]
            return base.rearrange("p (c t) -> p c t", c=2)[:, 0:c, PAD + shift:PAD + shift + NX]

        raw_loaded = [sem(f"raw_loaded{s}") for s in range(2)]
        hi_done = [sem(f"hi_done{s}") for s in range(2)]
        lo_done = [sem(f"lo_done{s}") for s in range(2)]
        tile_done = [sem(f"tile_done{s}") for s in range(2)]
        slab_out = [sem(f"slab_out{s}") for s in range(2)]
        mod_loaded = [sem(f"mod_loaded{s}") for s in range(2)]
        mod_used = [sem(f"mod_used{s}") for s in range(2)]
        in_loaded, par_loaded, lru_loaded = sem("in_loaded"), sem("par_loaded"), sem("lru_loaded")
        out_stored = sem("out_stored")
        eps_set, sigmoid_c, silu_c = sem("eps_set"), sem("sigmoid_c"), sem("silu_c")

        def stage_sems(l):
            a = {}

            def st(name, names=""):
                a[name] = Steps(sem(f"{name}_{l}"), names)

            st("lam_a", "abs exp")
            st("lam_v", "pos den inv z z2 p6 p5 p4 p3 p2 p1 p0 log sp c0 c1 c2")
            st("mod_v", "m0 m1 a0 a1 a2 a3")
            for nm in ("n1", "n2"):
                for eng in "apvh":
                    st(f"{nm}_{eng}")
            st("ci_a", "ru sq th r0 i0 r1 i1 t0 t1 a0 a1 e0 e1 s0 s1 zh")
            st("ci_v", "wc u0 u1 u2 u3 p0 p1 ge iu0 w0 iu1 w1 b0 b1 hc0 hx0 hc1 hx1 rec y")
            st("ci_p", "gates")
            st("ac_a", "c")
            st("ac_v", "g c0 c1")
            st("ab_a", "z0 z1")
            st("ab_v", "p0 p1 l0")
            for nm in ("co", "ao", "bo", "do"):
                st(f"{nm}_a", "sg")
            st("co_v")
            st("ao_v", "t")
            st("do_v", "t")
            st("bo_v", " ".join(f"k{k}" for k in range(TAPS_D)) + " t")
            st("kv_a", "c0 c1 x0 x1 v0")
            st("kv_v", "a0 a1 b0 s0 b1")
            st("kv_p", "r0 r1")
            st("q_a", "c0 c1 x0 x1" if l == 0 else "c0 c1")
            st("q_v", "a0 a1 b0 s0 b1")
            st("q_p", "r0 r1")
            ctx_unit = l == 0
            st("di_a", "qs p0 e0 t0 p1 e1 t1" + (" p2a p2 e2 t2" if ctx_unit else "") + " zh th")
            st("di_v", "k0 m0 s0 n0 f0 d0 r0 q0 k1 m1 s1 n1 f1 d1 r1 q1"
               + (" m2 s2 n2 f2 d2 r2 q2a q2" if ctx_unit else "") + " zl")
            st("di_p", "s0 t0 o0 s1 t1 o1" + (" s2 t2 o2" if ctx_unit else ""))
            tiles = range(KC)
            st("ln_v", " ".join([f"z{k}" for k in tiles] + ["mu"] + [f"c{k}" for k in tiles] + ["rstd", "n0", "v0"]
                                + [f"n{k} v{k} s{k - 1}" for k in tiles if k > 0] + [f"s{KC - 1}"]))
            st("ln_a", " ".join([f"q{k}" for k in tiles] + ["rms", "g0"]
                                + [f"g{k} h{k - 1}" for k in tiles if k > 0] + [f"h{KC - 1}"]))
            st("ln_p", " ".join(["mean"] + [f"q{k}" for k in tiles]))
            st("ln_l")
            st("ws_a")
            st("ws_v")
            st("wo_v", "x0 x1 x2" if l == 0 else "x0")
            for f in range(len(FF_PARTS)):
                st(f"fi{f}_a", "sg zh")
                st(f"fi{f}_v", "p z")
                st(f"fo{f}_v", "x0 x1 x2" if l == 0 else "x0")
            return a

        L = [stage_sems(l) for l in range(DEPTH)]
        fin_a, fin_p, fin_v = sem("fin_a"), sem("fin_p"), sem("fin_v")

        block = ctx.enter_context(nc.Block())

        def all_out(e, l, stage):
            for s in range(2):
                e.wait_ge(slab_out[s], pair_base(l, stage) + 1)

        def seqs_of(l):
            return 2 if l == 0 else 1

        @block.sync
        def _(sp):
            sp.dma_start(SILC[:, 0:2 * KC], cT).then_inc(in_loaded, 16)
            sp.dma_start(X[:, :], xT).then_inc(in_loaded, 16)
            sp.dma_start(PRM[:, :], prm).then_inc(par_loaded, 16)
            sp.dma_start(ROPE[:, :], rope).then_inc(par_loaded, 16)
            sp.dma_start(CST[:, :], consts).then_inc(par_loaded, 16)

            def load(n, s):
                sp.dma_start(RAW[:, s * SLAB:(s + 1) * SLAB], slab_of(stream, n)).then_inc(raw_loaded[s], 16)

            def load_mod(n, s):
                sp.dma_start(CD[:, s * SLAB:(s + 1) * SLAB], slab_of(modw, n)).then_inc(mod_loaded[s], 16)

            def slab_of(t, n):
                return t[n] if isinstance(n, int) else t[ds(n, 1)]

            for s in range(2):
                load_mod(s, s)
            for s in range(2):
                load(s, s)
            for l in range(DEPTH):
                if l > 0:
                    all_out(sp, l - 1, "w_out")
                    for s in range(2):
                        load_mod(l * NMOD + s, s)
                with sp.Fori(l * NMOD // 2 + 1, (l + 1) * NMOD // 2) as i:
                    for s in range(2):
                        sp.wait_ge(mod_used[s], i)
                        load_mod(2 * i + s, s)
                for s in range(2):
                    sp.wait_ge(mod_used[s], (l + 1) * NMOD // 2)
                sp.dma_start(CD[:, :], lruw[l]).then_inc(lru_loaded, 16)
                first = pair_base(l, "c_in") + 1
                with sp.Fori(first, min(first + LAYER_SLABS // 2, DEPTH * LAYER_SLABS // 2)) as i:
                    for s in range(2):
                        sp.wait_ge(lo_done[s], 2 * i)
                        load(2 * i + s, s)
            sp.wait_ge(fin_v, 1 + KC)
            sp.dma_start(outT, CD[:, 0:KC * NX]).then_inc(out_stored, 16)
            sp.wait_ge(out_stored, 16)

        @block.gpsimd
        def _(pool):
            def low(m, s, h):
                pool.wait_ge(hi_done[s], 2 * m + (h + 1))
                a, b = s * SLAB + h * HALF, s * SLAB + (h + 1) * HALF
                nc.gpsimd.tensor_tensor(WL[:, a:b], RAW[:, a:b], WH[:, a:b].bitcast(F32), ALU.subtract)\
                    .then_inc(lo_done[s], 1)

            with pool.Fori(0, LAYER_SLABS // 2 + 1) as m:
                for s in range(2):
                    for h in range(2):
                        low(m, s, h)
            with pool.Fori(LAYER_SLABS // 2 + 1, LAYER_SLABS) as m:
                for s in range(2):
                    low(m, s, 0)

        @block.tensor
        def _(pe):
            def mm(out, lhs, rhs, start, stop):
                return nc.tensor.matmul(out, lhs, rhs, start=start, stop=stop)

            def begin(m, s):
                pe.wait_ge(lo_done[s], 2 * m + 2)
                pe.wait_ge(slab_out[s], m + 1)

            def products(s, t, z, w, k, nk=KC):
                zh, zl = z
                out = bank(2 * s + t, w)
                a = s * SLAB + k * 2 * P + t * P
                wh, wl = WH[:, a:a + P], WL[:, a:a + P]
                mm(out, wh, row(zh, k, w), k == 0, False)
                mm(out, wh, row(zl, k, w), False, False)
                return mm(out, wl, row(zh, k, w), False, k == nk - 1)

            def slab(m, s, ops, nk=KC, before=None):
                begin(m, s)
                for t, (z, w) in enumerate(ops):
                    if before is not None and z is Z:
                        before()
                    for k in range(nk):
                        last = products(s, t, z, w, k, nk)
                    last.then_inc(tile_done[s], 1)

            def stage(l, name, ops, nk=KC, before=None):
                b = pair_base(l, name)
                with pe.Fori(0, dict(STAGES)[name] // 2) as i:
                    for s in range(2):
                        slab(i + b, s, ops, nk, before)

            H, Z = (HH, HL), (ZH, ZL)
            pe.wait_ge(par_loaded, 48)
            for l in range(DEPTH):
                a = L[l]
                W = seqs_of(l) * NX
                pe.wait_ge(silu_c, 1)
                with pe.Fori(0, NMOD // 2) as i:
                    for s in range(2):
                        pe.wait_ge(mod_loaded[s], i * 16 + 16 * (l * NMOD // 2 + 1))
                        for t in range(2):
                            for k in range(KC):
                                w0 = s * SLAB + k * 2 * P + t * P
                                last = mm(PS[:, 4, ds(i * 8 + (4 * s + 2 * t), 2)], CD[:, w0:w0 + P],
                                          SILC[:, 2 * KC + 2 * k:2 * KC + 2 * k + 2], k == 0, k == KC - 1)
                        last.then_inc(mod_used[s], 1)

                def squares(nm, w):
                    for k in range(KC):
                        pe.wait_ge(a[nm + "_a"].sem, k + 1)
                        last = mm(bank(5, w), ONES, row(S, k, w), k == 0, k == KC - 1)
                    last.then_inc(a[nm + "_p"].sem, 1)

                squares("n1", NT)
                pe.wait_ge(a["n1_h"].sem, 2 * KC)
                pe.wait_ge(a["mod_v"].sem, a["mod_v"].at(0, "m1"))

                b = pair_base(l, "c_in")
                with pe.Fori(0, KC // 2) as i:
                    for s in range(2):
                        slab(i + b, s, [(H, NT), (H, W)])
                        pe.wait_ge(a["ci_v"].sem, a["ci_v"].at(2 * i + s, "u3"))
                        for g in range(4):
                            last = mm(bank(4 + g), TMP[:, 5 * NT + g * P:5 * NT + (g + 1) * P], tmp(0), True, True)
                        last.then_inc(a["ci_p"].sem, 1)
                stage(l, "c_out", [(H, W), (Z, W)], before=lambda: all_out(pe, l, "c_out"))
                stage(l, "a_cu", [(H, W), (H, W)])
                stage(l, "a_b", [(H, W), (H, W)])
                stage(l, "a_out", [(H, W), (Z, W)], before=lambda: all_out(pe, l, "a_out"))

                def rotate(st_a, st_p, n, s):
                    for t in range(2):
                        pe.wait_ge(st_a.sem, st_a.at(n, f"c{t}"))
                        mm(bank(4 + 2 * s + t, NX), ROT, tmp(4 + t, 0, NX), True, True).then_inc(st_p.sem, 1)

                b = pair_base(l, "kv")
                slab(b, 0, [(H, NT), (H, NT)])
                rotate(a["kv_a"], a["kv_p"], 0, 0)
                begin(b, 1)
                for c in range(NT // P):
                    out = PS[:, 2 + c // 2, (c % 2) * 2 * P:(c % 2 + 1) * 2 * P]
                    for k in range(KC):
                        w0 = SLAB + k * 2 * P
                        h0 = k * NT + c * P
                        mm(out, HH[:, h0:h0 + P], WH[:, w0:w0 + 2 * P], k == 0, False)
                        mm(out, HH[:, h0:h0 + P], WL[:, w0:w0 + 2 * P], False, False)
                        last = mm(out, HL[:, h0:h0 + P], WH[:, w0:w0 + 2 * P], False, k == KC - 1)
                    if c % 2:
                        last.then_inc(tile_done[1], 1)
                b = pair_base(l, "q")
                with pe.Fori(0, 2) as i:
                    for s in range(2):
                        slab(i + b, s, [(H, W), (H, W)])
                        rotate(a["q_a"], a["q_p"], 2 * i + s, s)

                b = pair_base(l, "d_in")
                units = 3 if l == 0 else 2
                dv, da, dp = a["di_v"], a["di_a"], a["di_p"]

                def scores(n, u, kv):
                    if u == 0:
                        pe.wait_ge(da.sem, da.at(n, "qs"))
                    if u < 2:
                        last = mm(bank(5), QS[:, u * P:(u + 1) * P], KT[kv], True, True)
                    else:
                        for q in range(2):
                            last = mm(bank(5, NC, q * NC), QS[:, NX + q * P:NX + (q + 1) * P],
                                      KT[kv][:, NX:NT], True, True)
                    last.then_inc(dp.sem, 1)

                def turn(n, u):
                    pe.wait_ge(dv.sem, dv.at(n, f"q{u}"))
                    for q in range(4):
                        last = nc.tensor.transpose(bank(6, P, q * P), PR[:, q * P:(q + 1) * P], IDENT)
                    last.then_inc(dp.sem, 1)

                def weigh(n, u, kv):
                    pe.wait_ge(da.sem, da.at(n, f"t{u}"))
                    if u < 2:
                        for q in range(4):
                            last = mm(bank(7, P, u * P), VT[kv][q], PT[:, q * P:(q + 1) * P], q == 0, q == 3)
                    else:
                        for q in range(2):
                            for r in range(2):
                                last = mm(bank(7, P, NX + q * P), VT[kv][2 + r],
                                          PT[:, (2 * q + r) * P:(2 * q + r + 1) * P], r == 0, r == 1)
                    last.then_inc(dp.sem, 1)

                all_out(pe, l, "d_in")
                cuts = [(2 * KC * u) // (units + 1) for u in range(units + 2)]
                for kv in range(KVH):
                    with pe.Fori(0, 2) as i:
                        for s in range(2):
                            n = i * 2 + (kv * 4 + s)
                            begin(i + (b + 2 * kv), s)
                            for u in range(units + 1):
                                if u > 0:
                                    scores(n, u - 1, kv)
                                for step in range(cuts[u], cuts[u + 1]):
                                    t, k = divmod(step, KC)
                                    last = products(s, t, H, W, k)
                                    if k == KC - 1:
                                        last.then_inc(tile_done[s], 1)
                                if u > 0:
                                    turn(n, u - 1)
                                    weigh(n, u - 1, kv)
                stage(l, "b_out", [(H, W), (Z, W)], before=lambda: all_out(pe, l, "b_out"))
                lv, la, lp = a["ln_v"], a["ln_a"], a["ln_p"]
                for k in range(KC):
                    pe.wait_ge(lv.sem, lv.at(0, f"z{k}"))
                    last = mm(bank(4, W), ONES, row(CD, k, W), k == 0, k == KC - 1)
                last.then_inc(lp.sem, 1)
                for k in range(KC):
                    pe.wait_ge(la.sem, la.at(0, f"q{k}"))
                    mm(bank(5, W), ONES, tmp(1 + k % 4, 0, W), k == 0, k == KC - 1).then_inc(lp.sem, 1)
                stage(l, "d_out", [(H, W), (Z, W)], before=lambda: pe.wait_ge(a["ln_l"].sem, KC))
                stage(l, "w_out", [(Z, W), (Z, W)], before=lambda: pe.wait_ge(a["ws_v"].sem, KC))
                squares("n2", W)
                pe.wait_ge(a["n2_h"].sem, seqs_of(l) * KC)
                for f, nf in enumerate(FF_PARTS):
                    stage(l, f"ff_in{f}", [(H, W), (H, W)])
                    stage(l, f"ff_out{f}", [(Z, W), (Z, W)], nf, before=lambda f=f: all_out(pe, l, f"ff_out{f}"))
            for k in range(KC):
                pe.wait_ge(fin_a, k + 1)
                last = mm(bank(5, NX), ONES, row(S, k, NX), k == 0, k == KC - 1)
            last.then_inc(fin_p, 1)

        @block.scalar
        def _(act):
            def fn(out, in_, f, **kw):
                return nc.scalar.activation(out, in_, f, **kw)

            def high(m, s):
                act.wait_ge(raw_loaded[s], 16 * m + 16)
                for h in range(2):
                    x = slice(s * SLAB + h * HALF, s * SLAB + (h + 1) * HALF)
                    fn(WH[:, x], RAW[:, x], ACT.Copy).then_inc(hi_done[s], 1)

            def tiles(m, s, t=1):
                act.wait_ge(tile_done[s], 2 * m + (t + 1))

            def stage(l, name, body, high_first=True):
                b, pairs = pair_base(l, name), dict(STAGES)[name] // 2
                last = (l, name) == (DEPTH - 1, STAGES[-1][0])

                def one(i, s, more=True):
                    if high_first and more:
                        tiles(i + b, s)
                        high(i + (b + 1), s)
                    all_out(act, l, name)
                    body(2 * i + s, s, i + b)
                    if not high_first and more:
                        tiles(i + b, s)
                        high(i + (b + 1), s)

                with act.Fori(0, pairs - last) as i:
                    for s in range(2):
                        one(i, s)
                if last:
                    for s in range(2):
                        one(pairs - 1, s, more=False)

            act.wait_ge(in_loaded, 32)
            fn(SG[:, :], SILC[:, 0:2 * KC], ACT.Sigmoid).then_inc(sigmoid_c, 1)
            act.wait_ge(par_loaded, 48)
            for s in range(2):
                high(0, s)
            for l in range(DEPTH):
                a = L[l]
                C = seqs_of(l)
                W = C * NX

                def norm(nm, shift, c_all, stage_after):
                    na, nv, np_ = a[nm + "_a"].sem, a[nm + "_v"].sem, a[nm + "_p"].sem
                    all_out(act, l, stage_after)
                    for k in range(KC):
                        fn(row(S, k, c_all * NX), row(X, k, c_all * NX), ACT.Square).then_inc(na, 1)
                    act.wait_ge(np_, 1)
                    fn(tmp(0, 0, c_all * NX), bank(5, c_all * NX), ACT.Sqrt, scale=1.0 / D, bias=EPSC).then_inc(na, 1)
                    for k in range(KC):
                        for c in range(c_all):
                            act.wait_ge(nv, 1 + k * c_all + c + 1)
                            fn(row(HH, k, NX, c * NX), row(S, k, NX, c * NX), ACT.Identity,
                               bias=MOD[:, c * 48 + shift + k:c * 48 + shift + k + 1]).then_inc(na, 1)

                if l > 0:
                    all_out(act, l, "c_in")
                ls = a["lam_a"].sem
                fn(LT[:, 0:16], par(l, "lam", 0, 16), ACT.Abs).then_inc(ls, 1)
                act.wait_ge(ls, 1)
                fn(LT[:, 16:32], LT[:, 0:16], ACT.Exp, scale=-1.0).then_inc(ls, 1)
                norm("n1", 0, 2, "c_in")

                av, aa = a["ci_v"], a["ci_a"]

                def c_in(n, s, m):
                    fn(padded(n, 2), seqs(bank(2 * s), 2), ACT.Copy).then_inc(aa.sem, 1)
                    if s == 0:
                        act.wait_ge(slab_out[1], m + 1)
                    else:
                        act.wait_ge(slab_out[0], m + 2)
                    fn(tmp(1, 0, W), bank(2 * s + 1, W), ACT.Square).then_inc(aa.sem, 1)
                    act.wait_ge(av.sem, av.at(n, "p1"))
                    fn(tmp(3, 0, W), tmp(2, 0, W), ACT.Tanh, scale=GELU_C).then_inc(aa.sem, 1)
                    act.wait_ge(a["ci_p"].sem, n + 1)
                    for d in range(2):
                        fn(row(S, 2 * d), bank(4 + 2 * d), ACT.Sigmoid, bias=par(l, "ba", n + 8 * d)).then_inc(aa.sem, 1)
                        fn(row(S, 2 * d + 1), bank(5 + 2 * d), ACT.Sigmoid, bias=par(l, "bx", n + 8 * d)).then_inc(aa.sem, 1)
                    act.wait_ge(aa.sem, aa.at(n, "i1"))
                    for d in range(2):
                        fn(row(S, 4 + d), row(S, 2 * d), ACT.Tanh, scale=lc(2, n, d)).then_inc(aa.sem, 1)
                    for d in range(2):
                        fn(row(S, 6 + d), row(S, 2 * d), ACT.Exp, scale=lc(0, n, d)).then_inc(aa.sem, 1)
                    for d in range(2):
                        act.wait_ge(aa.sem, aa.at(n, f"a{d}"))
                        fn(row(S, 2 * d), row(S, 2 * d), ACT.Exp, scale=lc(1, n, d)).then_inc(aa.sem, 1)
                    for d in range(2):
                        act.wait_ge(av.sem, av.at(n, f"w{d}"))
                        fn(row(S, 2 * d), row(S, 2 * d), ACT.Sqrt).then_inc(aa.sem, 1)
                    act.wait_ge(av.sem, av.at(n, "y"))
                    fn(row(ZH, n, W), tmp(2, 0, W), ACT.Copy).then_inc(aa.sem, 1)

                stage(l, "c_in", c_in)

                def gate(which):
                    def body(n, s, m):
                        fn(tmp(s, 0, W), bank(2 * s, W), ACT.Sigmoid).then_inc(a[which + "_a"].sem, 1)
                    return body

                stage(l, "c_out", gate("co"))

                def a_cu(n, s, m):
                    fn(tmp(s, 0, W), bank(2 * s, W), ACT.Copy).then_inc(a["ac_a"].sem, 1)

                stage(l, "a_cu", a_cu)

                def a_b(n, s, m):
                    for t in range(2):
                        act.wait_ge(a["ab_v"].sem, a["ab_v"].at(n, f"p{t}"))
                        fn(row(ZH, 2 * n + t, W), tmp(2 * s + t, 0, W), ACT.Copy).then_inc(a["ab_a"].sem, 1)

                stage(l, "a_b", a_b)
                stage(l, "a_out", gate("ao"))

                b = pair_base(l, "kv")
                tiles(b, 0)
                high(b + 1, 0)
                all_out(act, l, "kv")
                ks = a["kv_a"].sem
                for t in range(2):
                    fn(tmp(4 + t, 0, NX), bank(t, NX), ACT.Copy).then_inc(ks, 1)
                for t in range(2):
                    fn(KT[t][:, NX:NT], bank(t, NC, NX), ACT.Copy).then_inc(ks, 1)
                tiles(b, 1)
                high(b + 1, 1)
                fn(tmp(2), bank(2), ACT.Copy).then_inc(ks, 1)

                def q_in(n, s, m):
                    qs = a["q_a"].sem
                    for t in range(2):
                        fn(tmp(4 + t, 0, NX), bank(2 * s + t, NX), ACT.Copy).then_inc(qs, 1)
                    if l == 0:
                        for t in range(2):
                            fn(row(CD, 2 * n + t, NC, NX), bank(2 * s + t, NC, NX), ACT.Copy).then_inc(qs, 1)

                stage(l, "q", q_in)

                dv, da, dp = a["di_v"], a["di_a"], a["di_p"]
                units = 3 if l == 0 else 2

                def d_in(n, s, m):
                    fn(QS[:, 0:W], row(CD, n, W), ACT.Copy).then_inc(da.sem, 1)
                    for u in range(units):
                        act.wait_ge(dv.sem, dv.at(n, f"n{u}"))
                        if u < 2:
                            fn(PR, bank(5), ACT.Exp, scale=SCALE, bias=SM[:, 4:5], accum_out=SM[:, 6:7]).then_inc(da.sem, 1)
                        else:
                            for q in range(2):
                                fn(PR[:, q * NC:(q + 1) * NC], bank(5, NC, q * NC), ACT.Exp, scale=SCALE,
                                   bias=SM[:, 4 + q:5 + q], accum_out=SM[:, 6 + q:7 + q]).then_inc(da.sem, 1)
                        act.wait_ge(dv.sem, dv.at(n, f"f{u}"))
                        q = 2 if u == 2 else 1
                        fn(SM[:, 8:8 + q], SM[:, 8:8 + q], ACT.Exp).then_inc(da.sem, 1)
                        act.wait_ge(dp.sem, dp.at(n, f"t{u}"))
                        fn(PT, bank(6), ACT.Copy).then_inc(da.sem, 1)
                    act.wait_ge(dp.sem, dp.at(n, f"o{units - 1}"))
                    fn(row(ZH, n, W), bank(7, W), ACT.Copy).then_inc(da.sem, 1)
                    tiles(m, s)
                    fn(padded(n, C), seqs(bank(2 * s + 1, W), C), ACT.Tanh, scale=0.5).then_inc(da.sem, 1)

                stage(l, "d_in", d_in, high_first=False)
                stage(l, "b_out", gate("bo"))

                lv, la, lp = a["ln_v"], a["ln_a"], a["ln_p"]
                for k in range(KC):
                    act.wait_ge(lv.sem, lv.at(0, f"c{k}"))
                    if k >= 4:
                        act.wait_ge(lp.sem, lp.at(0, f"q{k - 4}"))
                    fn(tmp(1 + k % 4, 0, W), row(CD, k, W), ACT.Square).then_inc(la.sem, 1)
                act.wait_ge(lp.sem, lp.at(0, f"q{KC - 1}"))
                fn(tmp(5, 0, W), bank(5, W), ACT.Sqrt, scale=1.0 / D, bias=EPSC).then_inc(la.sem, 1)

                def z_high(k):
                    act.wait_ge(lv.sem, lv.at(0, f"s{k}"))
                    fn(row(ZH, k, W), row(CD, k, W), ACT.Copy).then_inc(la.sem, 1)

                for k in range(KC):
                    act.wait_ge(lv.sem, lv.at(0, f"n{k}"))
                    if k >= 2:
                        act.wait_ge(lv.sem, lv.at(0, f"s{k - 2}"))
                    fn(tmp(1 + k % 2, 0, W), row(CD, k, W), ACT.Sigmoid, scale=par(l, "ln_g", k),
                       bias=par(l, "ln_b", k)).then_inc(la.sem, 1)
                    if k > 0:
                        z_high(k - 1)
                z_high(KC - 1)
                stage(l, "d_out", gate("do"))

                all_out(act, l, "w_out")
                for k in range(KC):
                    fn(row(ZH, k, W), row(S, k, W), ACT.Copy).then_inc(a["ws_a"].sem, 1)
                stage(l, "w_out", lambda n, s, m: None)
                norm("n2", 24, C, "ff_in0")
                for f in range(len(FF_PARTS)):
                    fa, fv = a[f"fi{f}_a"], a[f"fi{f}_v"]

                    def ff_in(n, s, m):
                        fn(tmp(s, 0, W), bank(2 * s, W), ACT.Sigmoid).then_inc(fa.sem, 1)
                        act.wait_ge(fv.sem, fv.at(n, "z"))
                        fn(row(ZH, n, W), tmp(4 + s, 0, W), ACT.Copy).then_inc(fa.sem, 1)

                    stage(l, f"ff_in{f}", ff_in)
                    stage(l, f"ff_out{f}", lambda n, s, m: None)
            for s in range(2):
                act.wait_ge(slab_out[s], DEPTH * LAYER_SLABS // 2 + 1)
            for k in range(KC):
                fn(row(S, k, NX), row(X, k, NX), ACT.Square).then_inc(fin_a, 1)
            act.wait_ge(fin_p, 1)
            fn(tmp(0, 0, NX), bank(5, NX), ACT.Sqrt, scale=1.0 / D, bias=EPSC).then_inc(fin_a, 1)

        @block.vector
        def _(dve):
            V = nc.vector

            def tt(out, x, y, op):
                return V.tensor_tensor(out, x, y, op)

            def stt(out, x, sc, y, op0, op1):
                return V.scalar_tensor_tensor(out, x, sc, y, op0, op1)

            def ts(out, x, s1, s2, op0, op1=None):
                return V.tensor_scalar(out, x, s1, s2, op0, op1) if op1 is not None else V.tensor_scalar(out, x, s1, None, op0)

            MUL, ADD, SUB, MAX = ALU.mult, ALU.add, ALU.subtract, ALU.max

            def stage(l, name, body):
                b, pairs = pair_base(l, name), dict(STAGES)[name] // 2
                last = (l, name) == (DEPTH - 1, STAGES[-1][0])

                def one(i, s, more=True):
                    dve.wait_ge(tile_done[s], 2 * (i + b) + 2)
                    body(2 * i + s, s, i + b)
                    if l == DEPTH - 1 and more:
                        low(i + (b + 1), s)

                with dve.Fori(0, pairs - last) as i:
                    for s in range(2):
                        one(i, s)
                if last:
                    for s in range(2):
                        one(pairs - 1, s, more=False)

            def low(m, s):
                dve.wait_ge(hi_done[s], 2 * m + 2)
                x = slice(s * SLAB + HALF, (s + 1) * SLAB)
                tt(WL[:, x], RAW[:, x], WH[:, x].bitcast(F32), SUB).then_inc(lo_done[s], 1)

            def z_low(n, w, src):
                return tt(row(ZL, n, w), src, row(ZH, n, w).bitcast(F32), SUB)

            V.memset(G[:, 0:GW * KC // 2], 0.0).then_inc(slab_out[0], 1)
            V.memset(G[:, GW * KC // 2:GW * KC], 0.0).then_inc(slab_out[1], 1)
            V.memset(EPSC, EPS).then_inc(eps_set, 1)
            dve.wait_ge(eps_set, 1)
            dve.wait_ge(sigmoid_c, 1)
            tt(SILC[:, 2 * KC:4 * KC], SILC[:, 0:2 * KC], SG[:, :], MUL).then_inc(silu_c, 1)
            dve.wait_ge(par_loaded, 48)
            for l in range(DEPTH):
                a = L[l]
                C = seqs_of(l)
                W = C * NX

                la, lv = a["lam_a"], a["lam_v"]
                k0, y, pos, z, z2 = (LT[:, 0:16], LT[:, 16:32], LT[:, 32:48], LT[:, 48:64], LT[:, 64:80])
                dve.wait_ge(la.sem, 2)
                ts(pos, par(l, "lam", 0, 16), -1.0, 0.0, MUL, MAX).then_inc(lv.sem, 1)
                ts(k0, y, 2.0, None, ADD).then_inc(lv.sem, 1)
                dve.wait_ge(lv.sem, lv.at(0, "den"))
                V.reciprocal(z, k0).then_inc(lv.sem, 1)
                dve.wait_ge(lv.sem, lv.at(0, "inv"))
                tt(z, z, y, MUL).then_inc(lv.sem, 1)
                dve.wait_ge(lv.sem, lv.at(0, "z"))
                tt(z2, z, z, MUL).then_inc(lv.sem, 1)
                dve.wait_ge(lv.sem, lv.at(0, "z2"))
                ts(k0, z2, 1.0 / 15, None, MUL).then_inc(lv.sem, 1)
                for j in range(6, 0, -1):
                    dve.wait_ge(lv.sem, lv.at(0, f"p{j}"))
                    stt(k0, k0, 1.0 / (2 * j + 1), z2, ADD, MUL).then_inc(lv.sem, 1)
                dve.wait_ge(lv.sem, lv.at(0, "p0"))
                stt(k0, k0, 1.0, z, ADD, MUL).then_inc(lv.sem, 1)
                dve.wait_ge(lv.sem, lv.at(0, "log"))
                stt(k0, k0, 2.0, pos, MUL, ADD).then_inc(lv.sem, 1)
                dve.wait_ge(lv.sem, lv.at(0, "sp"))
                for j, f in enumerate((-8.0, -16.0, 8.0)):
                    ts(LC[:, 16 * j:16 * j + 16], k0, f, None, MUL).then_inc(lv.sem, 1)
                dve.wait_ge(lv.sem, lv.at(0, "c2"))

                for s in range(2):
                    dve.wait_ge(mod_used[s], (l + 1) * NMOD // 2)
                mv = a["mod_v"]
                for c in range(2):
                    tt(MOD[:, c * 48:c * 48 + 48], PS[:, 4, 0:96].rearrange("p (n c) -> p c n", c=2)[:, c, :],
                       par(l, "b_mod", 0, 48), ADD).then_inc(mv.sem, 1)
                dve.wait_ge(mv.sem, mv.at(0, "m1"))
                for j, (g, off) in enumerate((("g_mix", 8), ("g_ffn", 32))):
                    for c in range(2):
                        stt(AMP[:, (2 * j + c) * KC:(2 * j + c + 1) * KC], MOD[:, c * 48 + off:c * 48 + off + KC], 1.0,
                            par(l, g, 0, KC), ADD, MUL).then_inc(mv.sem, 1)
                dve.wait_ge(mv.sem, mv.at(0, "a3"))

                def norm(nm, which, shift, c_all):
                    na, nv, nh = a[nm + "_a"].sem, a[nm + "_v"].sem, a[nm + "_h"].sem
                    dve.wait_ge(na, KC + 1)
                    V.reciprocal(tmp(1, 0, c_all * NX), tmp(0, 0, c_all * NX)).then_inc(nv, 1)
                    dve.wait_ge(nv, 1)

                    def scaled(k):
                        for c in range(c_all):
                            stt(row(S, k, NX, c * NX), row(X, k, NX, c * NX),
                                AMP[:, (2 * which + c) * KC + k:(2 * which + c) * KC + k + 1],
                                tmp(1, c * NX, (c + 1) * NX), MUL, MUL).then_inc(nv, 1)

                    def lows(k):
                        for c in range(c_all):
                            dve.wait_ge(na, KC + 1 + k * c_all + c + 1)
                            stt(row(HL, k, NX, c * NX), row(S, k, NX, c * NX),
                                MOD[:, c * 48 + shift + k:c * 48 + shift + k + 1],
                                row(HH, k, NX, c * NX).bitcast(F32), ADD, SUB).then_inc(nh, 1)

                    scaled(0)
                    for k in range(KC):
                        if k + 1 < KC:
                            scaled(k + 1)
                        lows(k)

                norm("n1", 0, 0, 2)

                def conv(out, n, c, name, taps, step, first_bias=None):
                    o = seqs(out, c)
                    for k in range(taps):
                        src, w = padded(n, c, k - taps // 2), par(l, name, n + 8 * k)
                        if k == 0 and first_bias is not None:
                            ins = ts(o, src, w, first_bias, MUL, ADD)
                        elif k == 0:
                            ins = ts(o, src, w, None, MUL)
                        else:
                            ins = stt(o, src, w, o, MUL, ADD)
                        step(k, ins)

                av, aa, ap = a["ci_v"], a["ci_a"], a["ci_p"]

                def c_in(n, s, m):
                    rg = bank(2 * s + 1, W)
                    V.tensor_copy(tmp(5), row(CD, n)).then_inc(av.sem, 1)
                    dve.wait_ge(aa.sem, aa.at(n, "ru"))

                    def tap(k, ins):
                        ins.then_inc(av.sem, 1)
                        dve.wait_ge(av.sem, av.at(n, f"u{k}"))

                    conv(tmp(0), n, 2, "conv_c", TAPS_C, tap, first_bias=par(l, "conv_c_b", n))
                    dve.wait_ge(aa.sem, aa.at(n, "sq"))
                    ts(tmp(2, 0, W), tmp(1, 0, W), 0.044715, 1.0, MUL, ADD).then_inc(av.sem, 1)
                    dve.wait_ge(av.sem, av.at(n, "p0"))
                    tt(tmp(2, 0, W), tmp(2, 0, W), rg, MUL).then_inc(av.sem, 1)
                    dve.wait_ge(aa.sem, aa.at(n, "th"))
                    stt(tmp(4, 0, W), tmp(3, 0, W), 1.0, rg, ADD, MUL).then_inc(av.sem, 1)
                    for d in range(2):
                        dve.wait_ge(aa.sem, aa.at(n, f"i{d}"))
                        tt(row(S, 2 * d + 1), row(S, 2 * d + 1), tmp(0), MUL).then_inc(av.sem, 1)
                        dve.wait_ge(aa.sem, aa.at(n, f"e{d}"))
                        stt(row(S, 2 * d), row(S, 2 * d), 1.0, row(S, 4 + d), ADD, MUL).then_inc(av.sem, 1)
                    for d in range(2):
                        dve.wait_ge(aa.sem, aa.at(n, f"s{d}"))
                        tt(row(S, 2 * d + 1), row(S, 2 * d + 1), row(S, 2 * d), MUL).then_inc(av.sem, 1)
                    dve.wait_ge(av.sem, av.at(n, "b1"))

                    def part(j, lo, hi, back):
                        v = S[:, j * NT + lo:j * NT + hi]
                        return v[:, ::-1] if back else v

                    for d in range(2):
                        h = 4 + d
                        end = h * NT + (NX if d else NT - 1)
                        V.tensor_tensor_scan(part(h, NX, NT, d), part(6 + d, NX, NT, d), part(2 * d + 1, NX, NT, d),
                                             0.0, MUL, ADD).then_inc(av.sem, 1)
                        dve.wait_ge(av.sem, av.at(n, f"hc{d}"))
                        V.tensor_tensor_scan(part(h, 0, NX, d), part(6 + d, 0, NX, d), part(2 * d + 1, 0, NX, d),
                                             S[:, end:end + 1], MUL, ADD).then_inc(av.sem, 1)
                    dve.wait_ge(av.sem, av.at(n, "hx1"))
                    tt(tmp(6, 0, W), row(S, 4, W), row(S, 5, W), ADD).then_inc(av.sem, 1)
                    dve.wait_ge(av.sem, av.at(n, "rec"))
                    stt(tmp(2, 0, W), tmp(6, 0, W), 0.5, tmp(4, 0, W), MUL, MUL).then_inc(av.sem, 1)
                    dve.wait_ge(aa.sem, aa.at(n, "zh"))
                    z_low(n, W, tmp(2, 0, W)).then_inc(slab_out[s], 1)

                dve.wait_ge(lru_loaded, 16 * (l + 1))
                stage(l, "c_in", c_in)

                def gated(which, first=False, before=None):
                    def body(n, s, m):
                        if before is not None:
                            before(n)
                        sa, sv = a[which + "_a"], a[which + "_v"]
                        dve.wait_ge(sa.sem, sa.at(n, "sg"))
                        if first:
                            tt(row(S, n, W), tmp(s, 0, W), bank(2 * s + 1, W), MUL).then_inc(slab_out[s], 1)
                        else:
                            tt(tmp(2 + s, 0, W), tmp(s, 0, W), bank(2 * s + 1, W), MUL).then_inc(sv.sem, 1)
                            dve.wait_ge(sv.sem, sv.at(n, "t"))
                            tt(row(S, n, W), row(S, n, W), tmp(2 + s, 0, W), ADD).then_inc(slab_out[s], 1)
                    return body

                stage(l, "c_out", gated("co", first=True))

                def a_cu(n, s, m):
                    sa, sv = a["ac_a"], a["ac_v"]
                    dve.wait_ge(sa.sem, sa.at(n, "c"))
                    tt(padded(n, C), seqs(tmp(s, 0, W), C), seqs(bank(2 * s + 1, W), C), MUL).then_inc(sv.sem, 1)
                    dve.wait_ge(sv.sem, sv.at(n, "g"))

                    def tap(k, ins):
                        if k < TAPS_A - 1:
                            ins.then_inc(sv.sem, 1)
                            dve.wait_ge(sv.sem, sv.at(n, f"c{k}"))
                        else:
                            ins.then_inc(slab_out[s], 1)

                    conv(row(CD, n, W), n, C, "conv_a", TAPS_A, tap)

                stage(l, "a_cu", a_cu)

                def a_b(n, s, m):
                    sa, sv = a["ab_a"], a["ab_v"]
                    for t in range(2):
                        tt(tmp(2 * s + t, 0, W), bank(2 * s + t, W), row(CD, 2 * n + t, W), MUL).then_inc(sv.sem, 1)
                    for t in range(2):
                        dve.wait_ge(sa.sem, sa.at(n, f"z{t}"))
                        z_low(2 * n + t, W, tmp(2 * s + t, 0, W)).then_inc(*((slab_out[s], 1) if t else (sv.sem, 1)))

                all_out(dve, l, "a_b")
                stage(l, "a_b", a_b)
                stage(l, "a_out", gated("ao"))

                def rotated(sa, sv, sp_, n, s, out):
                    for t in range(2):
                        dve.wait_ge(sa.sem, sa.at(n, f"x{t}" if "x0" in sa.names else f"c{t}"))
                        tt(out(t), bank(2 * s + t, NX), COS, MUL).then_inc(sv.sem, 1)
                    for t in range(2):
                        dve.wait_ge(sp_.sem, sp_.at(n, f"r{t}"))
                        tt(tmp(6, t * NX, t * NX + NX), bank(4 + 2 * s + t, NX), SIN, MUL).then_inc(sv.sem, 1)
                        dve.wait_ge(sv.sem, sv.at(n, f"b{t}"))
                        tt(out(t), out(t), tmp(6, t * NX, t * NX + NX), ADD)\
                            .then_inc(*((slab_out[s], 1) if t else (sv.sem, 1)))

                b = pair_base(l, "kv")
                all_out(dve, l, "kv")
                dve.wait_ge(tile_done[0], 2 * b + 2)
                rotated(a["kv_a"], a["kv_v"], a["kv_p"], 0, 0, lambda t: KT[t][:, 0:NX])
                if l == DEPTH - 1:
                    low(b + 1, 0)
                dve.wait_ge(tile_done[1], 2 * b + 2)
                dve.wait_ge(a["kv_a"].sem, a["kv_a"].at(0, "v0"))
                V.tensor_copy(tmp(3), bank(3)).then_inc(slab_out[1], 1)
                if l == DEPTH - 1:
                    low(b + 1, 1)
                stage(l, "q", lambda n, s, m: rotated(a["q_a"], a["q_v"], a["q_p"], n, s,
                                                      lambda t: row(CD, 2 * n + t, NX)))

                dv, da, dp = a["di_v"], a["di_a"], a["di_p"]
                units = 3 if l == 0 else 2

                def d_in_slab(n, s, m):
                    sink = par(l, "sink", n)
                    for u in range(units):
                        q = 2 if u == 2 else 1
                        mx, mm_, nm, dn, es, d2, rd = (SM[:, 2 * j:2 * j + q] for j in range(7))

                        def step(ins, name):
                            ins.then_inc(dv.sem, 1)
                            dve.wait_ge(dv.sem, dv.at(n, name))

                        dve.wait_ge(dp.sem, dp.at(n, f"s{u}"))
                        if u < 2:
                            far = bank(5, P, (1 - u) * P)
                            step(tt(far, far, TRI[u], ADD), f"k{u}")
                            step(V.reduce_max(mx, bank(5), AX.X), f"m{u}")
                        else:
                            step(V.reduce_max(mx, seqs(bank(5), 2), AX.X), "m2")
                        step(ts(mm_, mx, SCALE, sink, MUL, MAX), f"s{u}")
                        ts(nm, mm_, -1.0, None, MUL).then_inc(dv.sem, 1)
                        ts(es, mm_, -1.0, sink, MUL, ADD).then_inc(dv.sem, 1)
                        dve.wait_ge(da.sem, da.at(n, f"e{u}"))
                        step(tt(d2, dn, es, ADD), f"d{u}")
                        step(V.reciprocal(rd, d2), f"r{u}")
                        if u < 2:
                            ts(PR, PR, SM[:, 12:13], None, MUL).then_inc(dv.sem, 1)
                        else:
                            for j in range(2):
                                h = PR[:, j * NC:(j + 1) * NC]
                                ts(h, h, SM[:, 12 + j:13 + j], None, MUL).then_inc(dv.sem, 1)
                    dve.wait_ge(da.sem, da.at(n, "zh"))
                    z_low(n, W, bank(7, W)).then_inc(dv.sem, 1)
                    dve.wait_ge(tile_done[s], 2 * m + 2)
                    dve.wait_ge(da.sem, da.at(n, "th"))
                    stt(padded(n, C), padded(n, C), 1.0, seqs(bank(2 * s, W), C), ADD, MUL).then_inc(slab_out[s], 1)

                b = pair_base(l, "d_in")
                with dve.Fori(0, dict(STAGES)["d_in"] // 2) as i:
                    for s in range(2):
                        d_in_slab(2 * i + s, s, i + b)
                        if l == DEPTH - 1:
                            low(i + (b + 1), s)

                def conv_d(n):
                    sv = a["bo_v"]

                    def tap(k, ins):
                        ins.then_inc(sv.sem, 1)
                        dve.wait_ge(sv.sem, sv.at(n, f"k{k}"))

                    conv(row(CD, n, W), n, C, "conv_d", TAPS_D, tap)

                all_out(dve, l, "b_out")
                stage(l, "b_out", gated("bo", before=conv_d))

                lv, la, lp = a["ln_v"], a["ln_a"], a["ln_p"]
                for k in range(KC):
                    ts(row(CD, k, W), row(CD, k, W), 0.5, par(l, "conv_d_b", k), MUL, ADD).then_inc(lv.sem, 1)
                dve.wait_ge(lp.sem, lp.at(0, "mean"))
                ts(tmp(0, 0, W), bank(4, W), 1.0 / D, None, MUL).then_inc(lv.sem, 1)
                dve.wait_ge(lv.sem, lv.at(0, "mu"))
                for k in range(KC):
                    tt(row(CD, k, W), row(CD, k, W), tmp(0, 0, W), SUB).then_inc(lv.sem, 1)
                dve.wait_ge(la.sem, la.at(0, "rms"))
                V.reciprocal(tmp(6, 0, W), tmp(5, 0, W)).then_inc(lv.sem, 1)
                dve.wait_ge(lv.sem, lv.at(0, "rstd"))

                def ln_low(k):
                    dve.wait_ge(la.sem, la.at(0, f"h{k}"))
                    z_low(k, W, row(CD, k, W)).then_inc(a["ln_l"].sem, 1)

                def ln_gate(k):
                    dve.wait_ge(la.sem, la.at(0, f"g{k}"))
                    tt(row(CD, k, W), tmp(3 + k % 2, 0, W), tmp(1 + k % 2, 0, W), MUL).then_inc(lv.sem, 1)

                for k in range(KC):
                    tt(row(CD, k, W), row(CD, k, W), tmp(6, 0, W), MUL).then_inc(lv.sem, 1)
                    dve.wait_ge(lv.sem, lv.at(0, f"n{k}"))
                    ts(tmp(3 + k % 2, 0, W), row(CD, k, W), par(l, "ln_g", k), par(l, "ln_b", k), MUL, ADD)\
                        .then_inc(lv.sem, 1)
                    if k > 0:
                        ln_gate(k - 1)
                    if k > 1:
                        ln_low(k - 2)
                dve.wait_ge(lv.sem, lv.at(0, f"v{KC - 1}"))
                ln_gate(KC - 1)
                ln_low(KC - 2)
                ln_low(KC - 1)
                stage(l, "d_out", gated("do"))

                all_out(dve, l, "w_out")
                for k in range(KC):
                    dve.wait_ge(a["ws_a"].sem, k + 1)
                    z_low(k, W, row(S, k, W)).then_inc(a["ws_v"].sem, 1)

                def residual(which, gt):
                    def body(n, s, m):
                        for t in range(2):
                            for c in range(C):
                                x = row(X, 2 * n + t, NX, c * NX)
                                g = MOD[:, ds(2 * n + (t + gt + 48 * c), 1)] if not isinstance(n, int) else \
                                    MOD[:, 2 * n + t + gt + 48 * c:2 * n + t + gt + 48 * c + 1]
                                stt(x, bank(2 * s + t, NX, c * NX), g, x, MUL, ADD)\
                                    .then_inc(*((slab_out[s], 1) if (t, c) == (1, C - 1) else (a[which + "_v"].sem, 1)))
                    return body

                stage(l, "w_out", residual("wo", 16))
                norm("n2", 1, 24, C)
                for f in range(len(FF_PARTS)):
                    fa, fv = a[f"fi{f}_a"], a[f"fi{f}_v"]

                    def ff_in(n, s, m):
                        dve.wait_ge(fa.sem, fa.at(n, "sg"))
                        tt(tmp(2 + s, 0, W), tmp(s, 0, W), bank(2 * s, W), MUL).then_inc(fv.sem, 1)
                        dve.wait_ge(fv.sem, fv.at(n, "p"))
                        tt(tmp(4 + s, 0, W), tmp(2 + s, 0, W), bank(2 * s + 1, W), MUL).then_inc(fv.sem, 1)
                        dve.wait_ge(fa.sem, fa.at(n, "zh"))
                        z_low(n, W, tmp(4 + s, 0, W)).then_inc(slab_out[s], 1)

                    stage(l, f"ff_in{f}", ff_in)
                    all_out(dve, l, f"ff_out{f}")
                    stage(l, f"ff_out{f}", residual(f"fo{f}", 40))
                    if (l, f) != (DEPTH - 1, len(FF_PARTS) - 1):
                        all_out(dve, l, f"ff_in{f + 1}") if f + 1 < len(FF_PARTS) else all_out(dve, l + 1, "c_in")
            dve.wait_ge(fin_a, KC + 1)
            V.reciprocal(tmp(1, 0, NX), tmp(0, 0, NX)).then_inc(fin_v, 1)
            dve.wait_ge(fin_v, 1)
            for k in range(KC):
                stt(CD[:, k * NX:(k + 1) * NX], row(X, k, NX), par(0, "g_final", k), tmp(1, 0, NX), MUL, MUL)\
                    .then_inc(fin_v, 1)


def slab_tiles(w, c0, c1=None, r0=0):
    cols = [c0, c0 + P if c1 is None else c1]
    rows = min(w.shape[0] - r0, D)
    out = np.zeros((P, KC, 2, P), np.float32)
    for t, c in enumerate(cols):
        out[:, :rows // P, t, :] = w[r0:r0 + rows, c:c + P].reshape(rows // P, P, P).transpose(1, 0, 2)
    return out.reshape(P, SLAB)


def layer_stream(w_in, w_a, w_b, w_c, w_d, w_out, w_fi, w_fo):
    at = dict(zip(("a_b", "a_c", "a_u", "q", "k", "v", "r_g", "r_u", "d_v", "d_g", "gl"),
                  np.cumsum([0, D, D, D, D, 256, 256, D, D, D, D])))
    ff = FF_TILES * P
    s = []

    def two(x, y):
        s.extend(slab_tiles(w_in, at[x] + j * P, at[y] + j * P) for j in range(KC))

    def branch(w, n):
        for j in range(KC):
            c = at["gl"] + n * D + j * P
            g, y = (slab_tiles(x, a, a).reshape(P, KC, 2, P)[:, :, 0] for x, a in ((w_in, c), (w, j * P)))
            s.append(np.stack([g, y], axis=2).reshape(P, SLAB))

    two("r_u", "r_g")
    branch(w_c, 2)
    two("a_c", "a_u")
    s.extend(slab_tiles(w_in, at["a_b"] + 2 * j * P) for j in range(KC // 2))
    branch(w_a, 0)
    s.append(slab_tiles(w_in, at["k"]))
    s.append(slab_tiles(w_in, at["v"]))
    s.extend(slab_tiles(w_in, at["q"] + 2 * j * P) for j in range(KC // 2))
    two("d_v", "d_g")
    branch(w_b, 1)
    branch(w_d, 3)
    s.extend(slab_tiles(w_out, 2 * j * P) for j in range(KC // 2))
    first = 0
    for n in FF_PARTS:
        s.extend(slab_tiles(w_fi, (first + j) * P, ff + (first + j) * P) for j in range(n))
        s.extend(slab_tiles(w_fo[first * P:(first + n) * P], 2 * j * P) for j in range(KC // 2))
        first += n
    return s


def constants():
    half = HD // 2
    inv = (10000.0 ** (-np.arange(0, half, 2, dtype=np.float32) / half)).astype(np.float32)
    tok = np.arange(NX)
    row_, col = (tok // 64).astype(np.float32), (tok % 64).astype(np.float32)
    ar, ac = row_[:, None] * inv, col[:, None] * inv
    ang = np.concatenate([ar, ar, ac, ac], axis=-1).astype(np.float32)
    q = HD // 4
    sign = np.repeat(np.array([-1, 1, -1, 1], np.float32), q)
    rope = np.concatenate([np.cos(ang).T, (np.sin(ang) * sign).T], axis=1).astype(np.float32)
    swap = np.concatenate([np.arange(q) + q, np.arange(q), np.arange(q) + 3 * q, np.arange(q) + 2 * q])
    rot = np.zeros((P, P), np.float32)
    rot[swap, np.arange(P)] = 1.0
    i, j = np.arange(P)[:, None], np.arange(P)[None, :]
    tri0 = np.where(j <= i, 0.0, NEG).astype(np.float32)
    tri1 = np.where(j >= i, 0.0, NEG).astype(np.float32)
    return rope, np.concatenate([np.eye(P, dtype=np.float32), np.ones((P, P), np.float32), rot, tri0, tri1], axis=1)


def columns(v):
    return np.asarray(v).reshape(-1, P).T


def kernel(**inputs):
    import concourse.bacc as bacc
    from concourse.bass_utils import run_bass_kernel_spmd

    w = {k: np.asarray(v) for k, v in inputs.items()}
    stream, modw, lruw, prm = [], [], [], []
    for l in range(DEPTH):
        stream += layer_stream(*(w[k][l] for k in ("w_in", "w_a_out", "w_b_out", "w_c_out", "w_d_out", "w_out",
                                                   "w_ffn_in", "w_ffn_out")))
        modw += [slab_tiles(w["w_mod"][l], 2 * j * P) for j in range(NMOD)]
        gates = np.stack([w["lru_wa"][l, 0], w["lru_wx"][l, 0], w["lru_wa"][l, 1], w["lru_wx"][l, 1]])
        lruw.append(gates.transpose(2, 1, 0, 3).reshape(P, KC * NT))
        prm.append(np.concatenate(
            [columns(w[k][l]) for k in ("b_mod", "g_mix", "g_ffn", "conv_a", "conv_c", "conv_c_b", "lru_ba", "lru_bx",
                                        "lru_lam", "conv_d", "conv_d_b", "ln_d_g", "ln_d_b")]
            + [columns(w["g_final"]), np.broadcast_to(w["sink"][l], (P, HEADS))], axis=1))
    tokens = np.concatenate([w["x"][0], w["ctx"][0]], axis=0)
    xT = tokens.T.reshape(KC, P, NT).transpose(1, 0, 2).reshape(P, KC * NT)
    cT = np.stack([w["c"][0], w["c_ctx"]], axis=-1).reshape(KC, P, 2).transpose(1, 0, 2).reshape(P, 2 * KC)
    rope, consts = constants()
    arrays = {"stream": np.stack(stream), "modw": np.stack(modw), "lruw": np.stack(lruw), "xT": xT, "cT": cT,
              "prm": np.concatenate(prm, axis=1), "rope": rope, "consts": consts}
    arrays = {k: np.ascontiguousarray(v) for k, v in arrays.items()}

    nc = bacc.Bacc("TRN2", target_bir_lowering=False, num_devices=1)
    args = [nc.dram_tensor("in_" + k, v.shape, F32, kind="ExternalInput").ap() for k, v in arrays.items()]
    out = nc.dram_tensor("outT", (P, KC * NX), F32, kind="ExternalOutput").ap()
    build(nc, *args, out)
    r = run_bass_kernel_spmd(nc, [{"in_" + k: v for k, v in arrays.items()}], core_ids=[0])
    y = np.asarray(r.results[0]["outT"]).reshape(P, KC, NX)
    return y.transpose(2, 1, 0).reshape(1, NX, D)
```

```python
from contextlib import ExitStack

import numpy as np
import concourse.bass as bass
from concourse import mybir

P = 128
F32 = mybir.dt.float32
F32R = mybir.dt.float32r
ALU = mybir.AluOpType
ACT = mybir.ActivationFunctionType
AX = mybir.AxisListType
ds = bass.ds

DEPTH = 2
D = 1024
KC = D // P
NX = 256
NC = 256
NT = NX + NC
HEADS, KVH, HD = 8, 2, 128
SCALE = float(HD) ** -0.5
EPS = 1e-6
TAPS_A, TAPS_C, TAPS_D = 3, 4, 31
FF_TILES = 22
FF_PARTS = (8, 8, 6)
PAD = 15
SEG = NX + 2 * PAD
GW = 2 * SEG
SLAB = KC * 2 * P
HALF = SLAB // 2
NMOD = 6 * KC // 2
MOD_FIRST = 2 * KC // 2
MOD_IN = {(0, "d_out"): (2, MOD_FIRST // 2), (0, "ff_in0"): (2, NMOD // 2), (0, "ff_in1"): (1, NMOD // 2 + KC)}
D_TAPS = {"b_out": range(0, 13), "a_cu": range(13, 24), "a_b": range(24, TAPS_D)}
GELU_C = 0.7978845608028654
NEG = -1e30

_cols, _at = {}, 0
for _name, _n in (("b_mod", 48), ("g_mix", 8), ("g_ffn", 8), ("conv_a", 24), ("conv_c", 32), ("conv_c_b", 8),
                  ("ba", 16), ("bx", 16), ("lam", 16), ("conv_d", 248), ("conv_d_b", 8), ("ln_g", 8), ("ln_b", 8),
                  ("g_final", 8), ("sink", 8)):
    _cols[_name] = _at
    _at += _n
NPRM = _at

STAGES = [("c_in", 8), ("c_out", 8), ("kv", 2), ("q", 4), ("d_in", 8), ("b_out", 8), ("a_cu", 8), ("a_b", 4),
          ("a_out", 8), ("d_out", 8), ("w_out", 4)]
for _f, _n in enumerate(FF_PARTS):
    STAGES += [(f"ff_in{_f}", _n), (f"ff_out{_f}", 4)]
LAYER_SLABS = sum(n for _, n in STAGES)


def pair_base(layer, stage):
    n = layer * LAYER_SLABS
    for name, k in STAGES:
        if name == stage:
            return n // 2
        n += k
    raise KeyError(stage)


class Steps:

    def __init__(self, sem, names):
        self.sem = sem
        self.names = names.split()

    def at(self, n, name):
        return n * len(self.names) + self.names.index(name) + 1


def build(nc, stream, modw, lruw, xT, cT, prm, rope, consts, outT):
    with ExitStack() as ctx:
        def sb(name, n, dt=F32):
            return ctx.enter_context(nc.sbuf_tensor(name, [P, n], dt))

        def sem(name):
            return ctx.enter_context(nc.semaphore(name))

        X = sb("X", KC * NT)
        HH = sb("HH", KC * NT, F32R)
        HL = sb("HL", KC * NT, F32R)
        ZH = sb("ZH", KC * NT, F32R)
        ZL = sb("ZL", KC * NT, F32R)
        S = sb("S", KC * NT)
        G = sb("G", KC * GW)
        CD = sb("CD", KC * NT)
        PADA = sb("PADA", 2 * GW)
        RAW = sb("RAW", 2 * SLAB)
        WH = sb("WH", 2 * SLAB, F32R)
        WL = sb("WL", 2 * SLAB, F32R)
        TMP = sb("TMP", 7 * NT)
        PRM = sb("PRM", DEPTH * NPRM)
        ROPE = sb("ROPE", 2 * NX)
        CST = sb("CST", 5 * P + 2)
        MOD = sb("MOD", 2 * 48)
        AMP = sb("AMP", 2 * 2 * KC)
        CIN = sb("CIN", 2 * KC)
        SILC = sb("SILC", 32 * KC)
        SG = sb("SG", 2 * KC)
        LC = sb("LC", 3 * 16)
        LT = sb("LT", 5 * 16)
        EPST = sb("EPST", 2)
        BD2 = sb("BD2", KC)
        SM = sb("SM", 14)
        PS = ctx.enter_context(nc.psum_tensor("PS", [P, 8, 512], F32))

        EPSC, EPS4 = EPST[:, 0:1], EPST[:, 1:2]
        IDENT, ONES, ROT = CST[:, 0:P], CST[:, P:2 * P], CST[:, 2 * P:3 * P]
        TRI = [CST[:, 3 * P:4 * P], CST[:, 4 * P:5 * P]]
        SEL = CST[:, 5 * P:5 * P + 2]
        COS, SIN = ROPE[:, 0:NX], ROPE[:, NX:2 * NX]

        def tmp(i, a=0, b=NT):
            return TMP[:, i * NT + a:i * NT + b]

        KT = [tmp(0), tmp(1)]
        VT = [[TMP[:, (2 + c // 2) * NT + (c % 2) * 256 + kv * P:(2 + c // 2) * NT + (c % 2) * 256 + kv * P + P]
               for c in range(4)] for kv in range(KVH)]
        PR, PT, QS = tmp(4), tmp(5), tmp(6)

        MROW = [tmp(6, 0, NX), tmp(6, NX, NT)]

        def par(l, name, i=0, n=1):
            return PRM[:, ds(i + (l * NPRM + _cols[name]), n)] if not isinstance(i, int) else \
                PRM[:, l * NPRM + _cols[name] + i:l * NPRM + _cols[name] + i + n]

        def row(t, j, w=NT, a=0):
            return t[:, j * NT + a:j * NT + a + w] if isinstance(j, int) else t[:, ds(j * NT + a, w)]

        def lc(j, n, d):
            return LC[:, ds(n + (16 * j + 8 * d), 1)]

        def bank(b, w=NT, a=0):
            return PS[:, b, a:a + w]

        def seqs(ap, c):
            return ap.rearrange("p (c t) -> p c t", c=c)

        def padded(j, c, shift=0):
            base = G[:, j * GW:j * GW + GW] if isinstance(j, int) else G[:, ds(j * GW, GW)]
            return base.rearrange("p (c t) -> p c t", c=2)[:, 0:c, PAD + shift:PAD + shift + NX]

        raw_loaded = [sem(f"raw_loaded{s}") for s in range(2)]
        hi_done = [sem(f"hi_done{s}") for s in range(2)]
        lo_done = [sem(f"lo_done{s}") for s in range(2)]
        tile_done = [sem(f"tile_done{s}") for s in range(2)]
        slab_out = [sem(f"slab_out{s}") for s in range(2)]
        mod_loaded = [sem(f"mod_loaded{s}") for s in range(2)]
        mod_used = [sem(f"mod_used{s}") for s in range(2)]
        mod_copied = [sem(f"mod_copied{s}") for s in range(2)]
        mod_cols = sem("mod_cols")
        in_loaded, par_loaded, lru_loaded = sem("in_loaded"), sem("par_loaded"), sem("lru_loaded")
        out_stored = sem("out_stored")
        eps_set, sigmoid_c, silu_c = sem("eps_set"), sem("sigmoid_c"), sem("silu_c")

        def stage_sems(l):
            a = {}

            def st(name, names=""):
                a[name] = Steps(sem(f"{name}_{l}"), names)

            st("lam_a", "abs exp")
            st("lam_v", "pos den inv z z2 p6 p5 p4 p3 p2 p1 p0 log sp c0 c1 c2")
            st("mod_v", "b2 m0 m1 a0 a1 m2 m3 a2 a3")
            for nm in ("n1", "n2"):
                for eng in "apvh":
                    st(f"{nm}_{eng}")
            st("ci_a", "ru sq th r0 i0 r1 i1 t0 t1 a0 a1 e0 e1 s0 s1 zh")
            st("ci_v", "wc u0 u1 u2 u3 p0 p1 ge iu0 w0 iu1 w1 b0 b1 hc0 hx0 hc1 hx1 rec y")
            st("ci_p", "gates")
            st("ac_a", "c zh")
            st("ac_v", "g c0 c1 c2 " + " ".join(f"k{k}" for k in D_TAPS["a_cu"]))
            st("ab_a", "z0 z1")
            st("ab_v", "e0 e1 p0 p1 " + " ".join(f"k{k}_{t}" for k in D_TAPS["a_b"] for t in range(2)) + " l0")
            for nm in ("co", "ao", "bo", "do"):
                st(f"{nm}_a", "sg")
            st("co_v")
            st("ao_v", "t")
            st("do_v", "t")
            st("bo_v", " ".join(f"k{k}" for k in D_TAPS["b_out"]) + " t")
            st("kv_a", "c0 c1 x0 x1 v0")
            st("kv_v", "a0 a1 b0 s0 b1")
            st("kv_p", "r0 r1")
            st("q_a", "c0 c1 x0 x1" if l == 0 else "c0 c1")
            st("q_v", "a0 a1 b0 s0 b1")
            st("q_p", "r0 r1")
            ctx_unit = l == 0
            st("di_a", "qs p0 e0 t0 p1 e1 t1" + (" p2a p2 e2 t2" if ctx_unit else "") + " zh th")
            st("di_v", "k0 m0 s0 n0 f0 d0 r0 q0 k1 m1 s1 n1 f1 d1 r1 q1"
               + (" m2 s2 n2 f2 d2 r2 q2a q2" if ctx_unit else "") + " zl")
            st("di_p", "s0 t0 o0 s1 t1 o1" + (" s2 t2 o2" if ctx_unit else ""))
            tiles = range(KC)
            st("ln_v", " ".join(["mu"] + [f"c{k}" for k in tiles] + ["rstd", "n0"]
                                + [f"n{k} s{k - 1}" for k in tiles if k > 0] + [f"s{KC - 1}"]))
            st("ln_a", " ".join([f"q{k}" for k in tiles] + ["rms"] + [f"g{k}" for k in tiles]))
            st("ln_p", "mean var")
            st("ln_h")
            st("ln_l")
            st("pad_v")
            st("ws_a")
            st("ws_v")
            st("wo_v", "x0 x1 x2" if l == 0 else "x0")
            for f in range(len(FF_PARTS)):
                st(f"fi{f}_a", "sg zh")
                st(f"fi{f}_v", "p z")
                st(f"fo{f}_v", "x0 x1 x2" if l == 0 else "x0")
            return a

        L = [stage_sems(l) for l in range(DEPTH)]
        fin_a, fin_p, fin_v = sem("fin_a"), sem("fin_p"), sem("fin_v")

        block = ctx.enter_context(nc.Block())

        def all_out(e, l, stage):
            for s in range(2):
                e.wait_ge(slab_out[s], pair_base(l, stage) + 1)

        def seqs_of(l):
            return 2 if l == 0 else 1

        @block.sync
        def _(sp):
            sp.dma_start(CIN[:, :], cT).then_inc(in_loaded, 16)
            sp.dma_start(X[:, :], xT).then_inc(in_loaded, 16)
            sp.dma_start(PRM[:, :], prm).then_inc(par_loaded, 16)
            sp.dma_start(ROPE[:, :], rope).then_inc(par_loaded, 16)
            sp.dma_start(CST[:, :], consts).then_inc(par_loaded, 16)

            def load(n, s):
                sp.dma_start(RAW[:, s * SLAB:(s + 1) * SLAB], slab_of(stream, n)).then_inc(raw_loaded[s], 16)

            def load_mod(n, s):
                sp.dma_start(CD[:, s * SLAB:(s + 1) * SLAB], slab_of(modw, n)).then_inc(mod_loaded[s], 16)

            def slab_of(t, n):
                return t[n] if isinstance(n, int) else t[ds(n, 1)]

            for s in range(2):
                load_mod(s, s)
            with sp.Fori(1, MOD_FIRST // 2) as i:
                for s in range(2):
                    sp.wait_ge(mod_used[s], i)
                    load_mod(2 * i + s, s)
            for s in range(2):
                load(s, s)
            for l in range(DEPTH):
                for s in range(2):
                    sp.wait_ge(mod_used[s], MOD_FIRST // 2 if l == 0 else (l + 1) * NMOD // 2)
                sp.dma_start(CD[:, :], lruw[l]).then_inc(lru_loaded, 16)

                def loads(first, end, mods=0, use=0):
                    with sp.Fori(first, end) as i:
                        for s in range(2):
                            sp.wait_ge(lo_done[s], 2 * (i + 1))
                            load(2 * i + (2 + s), s)
                            for r in range(mods):
                                slot = r if mods == 2 else s
                                u = i + (use - first) if mods == 1 else 2 * i + (use - 2 * first + s)
                                sp.wait_ge(mod_used[slot], u)
                                load_mod(2 * u + slot, slot)

                at = pair_base(l, "c_in")
                for name in [k for ll, k in MOD_IN if ll == l]:
                    start = pair_base(l, name)
                    loads(at, start)
                    if name == "d_out":
                        sp.wait_ge(L[l]["ln_l"].sem, KC)
                    loads(start, start + dict(STAGES)[name] // 2, *MOD_IN[l, name])
                    at = start + dict(STAGES)[name] // 2
                loads(at, (l + 1) * LAYER_SLABS // 2 - (l == DEPTH - 1))
            sp.wait_ge(fin_v, 1 + KC)
            sp.dma_start(outT, CD[:, 0:KC * NX]).then_inc(out_stored, 16)
            sp.wait_ge(out_stored, 16)

        @block.gpsimd
        def _(pool):
            def low(m, s, h):
                pool.wait_ge(hi_done[s], 2 * m + (h + 1))
                a, b = s * SLAB + h * HALF, s * SLAB + (h + 1) * HALF
                nc.gpsimd.tensor_tensor(WL[:, a:b], RAW[:, a:b], WH[:, a:b].bitcast(F32), ALU.subtract)\
                    .then_inc(lo_done[s], 1)

            with pool.Fori(0, LAYER_SLABS // 2 + 1) as m:
                for s in range(2):
                    for h in range(2):
                        low(m, s, h)
            with pool.Fori(LAYER_SLABS // 2 + 1, LAYER_SLABS) as m:
                for s in range(2):
                    low(m, s, 0)

        @block.tensor
        def _(pe):
            def mm(out, lhs, rhs, start, stop):
                return nc.tensor.matmul(out, lhs, rhs, start=start, stop=stop)

            def begin(m, s):
                pe.wait_ge(lo_done[s], 2 * m + 2)
                pe.wait_ge(slab_out[s], m + 1)

            def products(s, t, z, w, k, nk=KC):
                zh, zl = z
                out = bank(2 * s + t, w)
                a = s * SLAB + k * 2 * P + t * P
                wh, wl = WH[:, a:a + P], WL[:, a:a + P]
                mm(out, wh, row(zh, k, w), k == 0, False)
                mm(out, wh, row(zl, k, w), False, False)
                return mm(out, wl, row(zh, k, w), False, k == nk - 1)

            def slab(m, s, ops, nk=KC, before=None, mods=()):
                begin(m, s)
                for t, (z, w) in enumerate(ops):
                    if before is not None and z is Z:
                        before()
                    for k in range(nk):
                        last = products(s, t, z, w, k, nk)
                    last.then_inc(tile_done[s], 1)
                    for slot, u in mods:
                        (mod_products, mod_columns)[t](slot, u)

            def stage(l, name, ops, nk=KC, before=None, pairs=None):
                b = pair_base(l, name)
                mods, use = MOD_IN.get((l, name), (0, 0))
                with pe.Fori(*(pairs or (0, dict(STAGES)[name] // 2))) as i:
                    for s in range(2):
                        slots = [(0, 2 * i + (use + s)), (1, 2 * i + (use + s))] if mods == 2 else [(s, i + use)] * mods
                        slab(i + b, s, ops, nk, before, slots)

            def mod_products(slot, u):
                pe.wait_ge(mod_loaded[slot], 16 * u + 16)
                for k in range(KC):
                    g = k % 4
                    w0 = slot * SLAB + k * 2 * P
                    last = nc.tensor.matmul(PS[32 * g:32 * g + 32, 5 + slot, 0:2 * P], SILC[:, 32 * k:32 * k + 32],
                                            CD[:, w0:w0 + 2 * P], start=k < 4, stop=k >= 4,
                                            tile_position=(0, 32 * g))
                last.then_inc(mod_used[slot], 1)

            def mod_columns(slot, u):
                pe.wait_ge(mod_copied[slot], u + 1)
                at = 8 * u + (4 * slot - mod_base[0])
                for t in range(2):
                    last = mm(PS[:, 4, ds(at + 2 * t, 2)] if not isinstance(at, int) else PS[:, 4, at + 2 * t:at + 2 * t + 2],
                              MROW[slot][:, t * P:(t + 1) * P], SEL, True, True)
                last.then_inc(mod_cols, 1)

            H, Z = (HH, HL), (ZH, ZL)
            mod_base = [0]
            pe.wait_ge(par_loaded, 48)
            pe.wait_ge(silu_c, 1)
            with pe.Fori(0, MOD_FIRST // 2) as i:
                for s in range(2):
                    mod_products(s, i)
                    mod_columns(s, i)
            for l in range(DEPTH):
                a = L[l]
                W = seqs_of(l) * NX

                def squares(nm, w):
                    for k in range(KC):
                        pe.wait_ge(a[nm + "_a"].sem, k + 1)
                        last = mm(bank(5, w), ONES, row(S, k, w), k == 0, k == KC - 1)
                    last.then_inc(a[nm + "_p"].sem, 1)

                squares("n1", NT)
                pe.wait_ge(a["n1_h"].sem, 2 * KC)
                pe.wait_ge(a["mod_v"].sem, a["mod_v"].at(0, "m1" if l == 0 else "m3"))

                b = pair_base(l, "c_in")
                with pe.Fori(0, KC // 2) as i:
                    for s in range(2):
                        slab(i + b, s, [(H, NT), (H, W)])
                        pe.wait_ge(a["ci_v"].sem, a["ci_v"].at(2 * i + s, "u3"))
                        for g in range(4):
                            last = mm(bank(4 + g), TMP[:, 5 * NT + g * P:5 * NT + (g + 1) * P], tmp(0), True, True)
                        last.then_inc(a["ci_p"].sem, 1)
                stage(l, "c_out", [(H, W), (Z, W)], before=lambda: all_out(pe, l, "c_out"))

                def rotate(st_a, st_p, n, s):
                    for t in range(2):
                        pe.wait_ge(st_a.sem, st_a.at(n, f"c{t}"))
                        mm(bank(4 + 2 * s + t, NX), ROT, tmp(4 + t, 0, NX), True, True).then_inc(st_p.sem, 1)

                b = pair_base(l, "kv")
                slab(b, 0, [(H, NT), (H, NT)])
                rotate(a["kv_a"], a["kv_p"], 0, 0)
                begin(b, 1)
                for c in range(NT // P):
                    out = PS[:, 2 + c // 2, (c % 2) * 2 * P:(c % 2 + 1) * 2 * P]
                    for k in range(KC):
                        w0 = SLAB + k * 2 * P
                        h0 = k * NT + c * P
                        mm(out, HH[:, h0:h0 + P], WH[:, w0:w0 + 2 * P], k == 0, False)
                        mm(out, HH[:, h0:h0 + P], WL[:, w0:w0 + 2 * P], False, False)
                        last = mm(out, HL[:, h0:h0 + P], WH[:, w0:w0 + 2 * P], False, k == KC - 1)
                    if c % 2:
                        last.then_inc(tile_done[1], 1)
                b = pair_base(l, "q")
                with pe.Fori(0, 2) as i:
                    for s in range(2):
                        slab(i + b, s, [(H, W), (H, W)])
                        rotate(a["q_a"], a["q_p"], 2 * i + s, s)

                b = pair_base(l, "d_in")
                units = 3 if l == 0 else 2
                dv, da, dp = a["di_v"], a["di_a"], a["di_p"]

                def scores(n, u, kv):
                    if u == 0:
                        pe.wait_ge(da.sem, da.at(n, "qs"))
                    if u < 2:
                        last = mm(bank(5), QS[:, u * P:(u + 1) * P], KT[kv], True, True)
                    else:
                        for q in range(2):
                            last = mm(bank(5, NC, q * NC), QS[:, NX + q * P:NX + (q + 1) * P],
                                      KT[kv][:, NX:NT], True, True)
                    last.then_inc(dp.sem, 1)

                def turn(n, u):
                    pe.wait_ge(dv.sem, dv.at(n, f"q{u}"))
                    for q in range(4):
                        last = nc.tensor.transpose(bank(6, P, q * P), PR[:, q * P:(q + 1) * P], IDENT)
                    last.then_inc(dp.sem, 1)

                def weigh(n, u, kv):
                    pe.wait_ge(da.sem, da.at(n, f"t{u}"))
                    if u < 2:
                        for q in range(4):
                            last = mm(bank(7, P, u * P), VT[kv][q], PT[:, q * P:(q + 1) * P], q == 0, q == 3)
                    else:
                        for q in range(2):
                            for r in range(2):
                                last = mm(bank(7, P, NX + q * P), VT[kv][2 + r],
                                          PT[:, (2 * q + r) * P:(2 * q + r + 1) * P], r == 0, r == 1)
                    last.then_inc(dp.sem, 1)

                all_out(pe, l, "d_in")
                cuts = [(2 * KC * u) // (units + 1) for u in range(units + 2)]
                for kv in range(KVH):
                    with pe.Fori(0, 2) as i:
                        for s in range(2):
                            n = i * 2 + (kv * 4 + s)
                            begin(i + (b + 2 * kv), s)
                            for u in range(units + 1):
                                if u > 0:
                                    scores(n, u - 1, kv)
                                for step in range(cuts[u], cuts[u + 1]):
                                    t, k = divmod(step, KC)
                                    last = products(s, t, H, W, k)
                                    if k == KC - 1:
                                        last.then_inc(tile_done[s], 1)
                                if u > 0:
                                    turn(n, u - 1)
                                    weigh(n, u - 1, kv)
                stage(l, "b_out", [(H, W), (Z, W)], before=lambda: all_out(pe, l, "b_out"))
                stage(l, "a_cu", [(H, W), (H, W)])
                stage(l, "a_b", [(H, W), (H, W)])
                lv, la, lp = a["ln_v"], a["ln_a"], a["ln_p"]
                all_out(pe, l, "a_out")
                for k in range(KC):
                    last = mm(bank(4, W), ONES, row(CD, k, W), k == 0, k == KC - 1)
                last.then_inc(lp.sem, 1)
                stage(l, "a_out", [(H, W), (Z, W)], pairs=(0, 2))
                pe.wait_ge(la.sem, la.at(0, f"q{KC - 1}"))
                for k in range(KC):
                    last = mm(seqs(bank(5, W), seqs_of(l)), ONES, padded(k, seqs_of(l)), k == 0, k == KC - 1)
                last.then_inc(lp.sem, 1)
                stage(l, "a_out", [(H, W), (Z, W)], pairs=(2, 4))
                stage(l, "d_out", [(H, W), (Z, W)], before=lambda: pe.wait_ge(a["ln_l"].sem, KC))
                stage(l, "w_out", [(Z, W), (Z, W)], before=lambda: pe.wait_ge(a["ws_v"].sem, KC))
                squares("n2", W)
                pe.wait_ge(a["n2_h"].sem, seqs_of(l) * KC)
                pe.wait_ge(a["mod_v"].sem, a["mod_v"].at(0, "m3"))
                mod_base[0] = 2 * NMOD * 2
                for f, nf in enumerate(FF_PARTS):
                    stage(l, f"ff_in{f}", [(H, W), (H, W)])
                    stage(l, f"ff_out{f}", [(Z, W), (Z, W)], nf, before=lambda f=f: all_out(pe, l, f"ff_out{f}"))
            for k in range(KC):
                pe.wait_ge(fin_a, k + 1)
                last = mm(bank(5, NX), ONES, row(S, k, NX), k == 0, k == KC - 1)
            last.then_inc(fin_p, 1)

        @block.scalar
        def _(act):
            def fn(out, in_, f, **kw):
                return nc.scalar.activation(out, in_, f, **kw)

            def high(m, s):
                act.wait_ge(raw_loaded[s], 16 * m + 16)
                for h in range(2):
                    x = slice(s * SLAB + h * HALF, s * SLAB + (h + 1) * HALF)
                    fn(WH[:, x], RAW[:, x], ACT.Copy).then_inc(hi_done[s], 1)

            def tiles(m, s, t=1):
                act.wait_ge(tile_done[s], 2 * m + (t + 1))

            def mod_rows(slot, u):
                act.wait_ge(mod_used[slot], u + 1)
                fn(MROW[slot], bank(5 + slot, NX), ACT.Copy).then_inc(mod_copied[slot], 1)

            def stage(l, name, body, high_first=True, some=None):
                b, pairs = pair_base(l, name), dict(STAGES)[name] // 2
                last = (l, name) == (DEPTH - 1, STAGES[-1][0])

                mods, use = MOD_IN.get((l, name), (0, 0))

                def one(i, s, more=True):
                    for slot, u in ([(0, 2 * i + (use + s)), (1, 2 * i + (use + s))] if mods == 2 else [(s, i + use)] * mods):
                        mod_rows(slot, u)
                    if high_first and more:
                        tiles(i + b, s)
                        high(i + (b + 1), s)
                    all_out(act, l, name)
                    body(2 * i + s, s, i + b)
                    if not high_first and more:
                        tiles(i + b, s)
                        high(i + (b + 1), s)

                with act.Fori(*(some or (0, pairs - last))) as i:
                    for s in range(2):
                        one(i, s)
                if last:
                    for s in range(2):
                        one(pairs - 1, s, more=False)

            act.wait_ge(in_loaded, 32)
            fn(SG[:, :], CIN[:, :], ACT.Sigmoid).then_inc(sigmoid_c, 1)
            act.wait_ge(par_loaded, 48)
            with act.Fori(0, MOD_FIRST // 2) as i:
                for s in range(2):
                    mod_rows(s, i)
            for s in range(2):
                high(0, s)
            for l in range(DEPTH):
                a = L[l]
                C = seqs_of(l)
                W = C * NX

                def norm(nm, shift, c_all, stage_after):
                    na, nv, np_ = a[nm + "_a"].sem, a[nm + "_v"].sem, a[nm + "_p"].sem
                    all_out(act, l, stage_after)
                    for k in range(KC):
                        fn(row(S, k, c_all * NX), row(X, k, c_all * NX), ACT.Square).then_inc(na, 1)
                    act.wait_ge(np_, 1)
                    fn(tmp(0, 0, c_all * NX), bank(5, c_all * NX), ACT.Sqrt, scale=1.0 / D, bias=EPSC).then_inc(na, 1)
                    for k in range(KC):
                        for c in range(c_all):
                            act.wait_ge(nv, 1 + k * c_all + c + 1)
                            fn(row(HH, k, NX, c * NX), row(S, k, NX, c * NX), ACT.Identity,
                               bias=MOD[:, c * 48 + shift + k:c * 48 + shift + k + 1]).then_inc(na, 1)

                if l > 0:
                    all_out(act, l, "c_in")
                ls = a["lam_a"].sem
                fn(LT[:, 0:16], par(l, "lam", 0, 16), ACT.Abs).then_inc(ls, 1)
                act.wait_ge(ls, 1)
                fn(LT[:, 16:32], LT[:, 0:16], ACT.Exp, scale=-1.0).then_inc(ls, 1)
                norm("n1", 0, 2, "c_in")

                av, aa = a["ci_v"], a["ci_a"]

                def c_in(n, s, m):
                    fn(padded(n, 2), seqs(bank(2 * s), 2), ACT.Copy).then_inc(aa.sem, 1)
                    if s == 0:
                        act.wait_ge(slab_out[1], m + 1)
                    else:
                        act.wait_ge(slab_out[0], m + 2)
                    fn(tmp(1, 0, W), bank(2 * s + 1, W), ACT.Square).then_inc(aa.sem, 1)
                    act.wait_ge(av.sem, av.at(n, "p1"))
                    fn(tmp(3, 0, W), tmp(2, 0, W), ACT.Tanh, scale=GELU_C).then_inc(aa.sem, 1)
                    act.wait_ge(a["ci_p"].sem, n + 1)
                    for d in range(2):
                        fn(row(S, 2 * d), bank(4 + 2 * d), ACT.Sigmoid, bias=par(l, "ba", n + 8 * d)).then_inc(aa.sem, 1)
                        fn(row(S, 2 * d + 1), bank(5 + 2 * d), ACT.Sigmoid, bias=par(l, "bx", n + 8 * d)).then_inc(aa.sem, 1)
                    act.wait_ge(aa.sem, aa.at(n, "i1"))
                    for d in range(2):
                        fn(row(S, 4 + d), row(S, 2 * d), ACT.Tanh, scale=lc(2, n, d)).then_inc(aa.sem, 1)
                    for d in range(2):
                        fn(row(S, 6 + d), row(S, 2 * d), ACT.Exp, scale=lc(0, n, d)).then_inc(aa.sem, 1)
                    for d in range(2):
                        act.wait_ge(aa.sem, aa.at(n, f"a{d}"))
                        fn(row(S, 2 * d), row(S, 2 * d), ACT.Exp, scale=lc(1, n, d)).then_inc(aa.sem, 1)
                    for d in range(2):
                        act.wait_ge(av.sem, av.at(n, f"w{d}"))
                        fn(row(S, 2 * d), row(S, 2 * d), ACT.Sqrt).then_inc(aa.sem, 1)
                    act.wait_ge(av.sem, av.at(n, "y"))
                    fn(row(ZH, n, W), tmp(2, 0, W), ACT.Copy).then_inc(aa.sem, 1)

                stage(l, "c_in", c_in)

                def gate(which):
                    def body(n, s, m):
                        fn(tmp(s, 0, W), bank(2 * s, W), ACT.Sigmoid).then_inc(a[which + "_a"].sem, 1)
                    return body

                stage(l, "c_out", gate("co"))

                b = pair_base(l, "kv")
                tiles(b, 0)
                high(b + 1, 0)
                all_out(act, l, "kv")
                ks = a["kv_a"].sem
                for t in range(2):
                    fn(tmp(4 + t, 0, NX), bank(t, NX), ACT.Copy).then_inc(ks, 1)
                for t in range(2):
                    fn(KT[t][:, NX:NT], bank(t, NC, NX), ACT.Copy).then_inc(ks, 1)
                tiles(b, 1)
                high(b + 1, 1)
                fn(tmp(2), bank(2), ACT.Copy).then_inc(ks, 1)

                def q_in(n, s, m):
                    qs = a["q_a"].sem
                    for t in range(2):
                        fn(tmp(4 + t, 0, NX), bank(2 * s + t, NX), ACT.Copy).then_inc(qs, 1)
                    if l == 0:
                        for t in range(2):
                            fn(row(CD, 2 * n + t, NC, NX), bank(2 * s + t, NC, NX), ACT.Copy).then_inc(qs, 1)

                stage(l, "q", q_in)

                dv, da, dp = a["di_v"], a["di_a"], a["di_p"]
                units = 3 if l == 0 else 2

                def d_in(n, s, m):
                    fn(QS[:, 0:W], row(CD, n, W), ACT.Copy).then_inc(da.sem, 1)
                    for u in range(units):
                        act.wait_ge(dv.sem, dv.at(n, f"n{u}"))
                        if u < 2:
                            fn(PR, bank(5), ACT.Exp, scale=SCALE, bias=SM[:, 4:5], accum_out=SM[:, 6:7]).then_inc(da.sem, 1)
                        else:
                            for q in range(2):
                                fn(PR[:, q * NC:(q + 1) * NC], bank(5, NC, q * NC), ACT.Exp, scale=SCALE,
                                   bias=SM[:, 4 + q:5 + q], accum_out=SM[:, 6 + q:7 + q]).then_inc(da.sem, 1)
                        act.wait_ge(dv.sem, dv.at(n, f"f{u}"))
                        q = 2 if u == 2 else 1
                        fn(SM[:, 8:8 + q], SM[:, 8:8 + q], ACT.Exp).then_inc(da.sem, 1)
                        act.wait_ge(dp.sem, dp.at(n, f"t{u}"))
                        fn(PT, bank(6), ACT.Copy).then_inc(da.sem, 1)
                    act.wait_ge(dp.sem, dp.at(n, f"o{units - 1}"))
                    fn(row(ZH, n, W), bank(7, W), ACT.Copy).then_inc(da.sem, 1)
                    tiles(m, s)
                    fn(padded(n, C), seqs(bank(2 * s + 1, W), C), ACT.Tanh, scale=0.5).then_inc(da.sem, 1)

                stage(l, "d_in", d_in, high_first=False)
                stage(l, "b_out", gate("bo"))

                def a_cu(n, s, m):
                    sa, sv = a["ac_a"], a["ac_v"]
                    fn(tmp(s, 0, W), bank(2 * s, W), ACT.Copy).then_inc(sa.sem, 1)
                    act.wait_ge(sv.sem, sv.at(n, "c2"))
                    fn(row(ZH, n, W), tmp(2 + s, 0, W), ACT.Copy).then_inc(sa.sem, 1)

                stage(l, "a_cu", a_cu)

                def a_b(n, s, m):
                    for t in range(2):
                        act.wait_ge(a["ab_v"].sem, a["ab_v"].at(n, f"p{t}"))
                        fn(row(ZH, 2 * n + t, W), tmp(2 * s + t, 0, W), ACT.Copy).then_inc(a["ab_a"].sem, 1)

                stage(l, "a_b", a_b)
                lv, la, lp = a["ln_v"], a["ln_a"], a["ln_p"]
                for k in range(KC):
                    act.wait_ge(lv.sem, lv.at(0, f"c{k}"))
                    fn(padded(k, C), seqs(row(CD, k, W), C), ACT.Square).then_inc(la.sem, 1)
                stage(l, "a_out", gate("ao"), some=(0, 2))
                act.wait_ge(lp.sem, lp.at(0, "var"))
                fn(tmp(5, 0, W), bank(5, W), ACT.Sqrt, scale=1.0 / D, bias=EPS4).then_inc(la.sem, 1)
                for k in range(KC):
                    act.wait_ge(lv.sem, lv.at(0, f"n{k}"))
                    fn(padded(k, C), seqs(row(CD, k, W), C), ACT.Sigmoid, bias=par(l, "ln_b", k)).then_inc(la.sem, 1)
                stage(l, "a_out", gate("ao"), some=(2, 4))
                all_out(act, l, "d_out")
                for k in range(KC):
                    act.wait_ge(lv.sem, lv.at(0, f"s{k}"))
                    fn(row(ZH, k, W), row(CD, k, W), ACT.Copy).then_inc(a["ln_h"].sem, 1)
                stage(l, "d_out", gate("do"))

                all_out(act, l, "w_out")
                for k in range(KC):
                    fn(row(ZH, k, W), row(S, k, W), ACT.Copy).then_inc(a["ws_a"].sem, 1)
                stage(l, "w_out", lambda n, s, m: None)
                norm("n2", 24, C, "ff_in0")
                for f in range(len(FF_PARTS)):
                    fa, fv = a[f"fi{f}_a"], a[f"fi{f}_v"]

                    def ff_in(n, s, m):
                        fn(tmp(s, 0, W), bank(2 * s, W), ACT.Sigmoid).then_inc(fa.sem, 1)
                        act.wait_ge(fv.sem, fv.at(n, "z"))
                        fn(row(ZH, n, W), tmp(4 + s, 0, W), ACT.Copy).then_inc(fa.sem, 1)

                    stage(l, f"ff_in{f}", ff_in)
                    stage(l, f"ff_out{f}", lambda n, s, m: None)
            for s in range(2):
                act.wait_ge(slab_out[s], DEPTH * LAYER_SLABS // 2 + 1)
            for k in range(KC):
                fn(row(S, k, NX), row(X, k, NX), ACT.Square).then_inc(fin_a, 1)
            act.wait_ge(fin_p, 1)
            fn(tmp(0, 0, NX), bank(5, NX), ACT.Sqrt, scale=1.0 / D, bias=EPSC).then_inc(fin_a, 1)

        @block.vector
        def _(dve):
            V = nc.vector

            def tt(out, x, y, op):
                return V.tensor_tensor(out, x, y, op)

            def stt(out, x, sc, y, op0, op1):
                return V.scalar_tensor_tensor(out, x, sc, y, op0, op1)

            def ts(out, x, s1, s2, op0, op1=None):
                return V.tensor_scalar(out, x, s1, s2, op0, op1) if op1 is not None else V.tensor_scalar(out, x, s1, None, op0)

            MUL, ADD, SUB, MAX = ALU.mult, ALU.add, ALU.subtract, ALU.max

            def stage(l, name, body, some=None):
                b, pairs = pair_base(l, name), dict(STAGES)[name] // 2
                last = (l, name) == (DEPTH - 1, STAGES[-1][0])

                def one(i, s, more=True):
                    dve.wait_ge(tile_done[s], 2 * (i + b) + 2)
                    body(2 * i + s, s, i + b)
                    if l == DEPTH - 1 and more:
                        low(i + (b + 1), s)

                with dve.Fori(*(some or (0, pairs - last))) as i:
                    for s in range(2):
                        one(i, s)
                if last:
                    for s in range(2):
                        one(pairs - 1, s, more=False)

            def low(m, s):
                dve.wait_ge(hi_done[s], 2 * m + 2)
                x = slice(s * SLAB + HALF, (s + 1) * SLAB)
                tt(WL[:, x], RAW[:, x], WH[:, x].bitcast(F32), SUB).then_inc(lo_done[s], 1)

            def z_low(n, w, src):
                return tt(row(ZL, n, w), src, row(ZH, n, w).bitcast(F32), SUB)

            V.memset(G[:, 0:GW * KC // 2], 0.0).then_inc(slab_out[0], 1)
            V.memset(G[:, GW * KC // 2:GW * KC], 0.0).then_inc(slab_out[1], 1)
            V.memset(EPSC, EPS).then_inc(eps_set, 1)
            V.memset(EPS4, 4 * EPS).then_inc(eps_set, 1)
            V.memset(SILC[:, :], 0.0).then_inc(eps_set, 1)
            dve.wait_ge(eps_set, 3)
            dve.wait_ge(sigmoid_c, 1)
            tt(SILC[:, :].rearrange("p (k c) -> p k c", c=32)[:, :, 0:2], CIN[:, :].rearrange("p (k c) -> p k c", c=2),
               SG[:, :].rearrange("p (k c) -> p k c", c=2), MUL).then_inc(silu_c, 1)
            dve.wait_ge(par_loaded, 48)
            for l in range(DEPTH):
                a = L[l]
                C = seqs_of(l)
                W = C * NX

                la, lv = a["lam_a"], a["lam_v"]
                k0, y, pos, z, z2 = (LT[:, 0:16], LT[:, 16:32], LT[:, 32:48], LT[:, 48:64], LT[:, 64:80])
                dve.wait_ge(la.sem, 2)
                ts(pos, par(l, "lam", 0, 16), -1.0, 0.0, MUL, MAX).then_inc(lv.sem, 1)
                ts(k0, y, 2.0, None, ADD).then_inc(lv.sem, 1)
                dve.wait_ge(lv.sem, lv.at(0, "den"))
                V.reciprocal(z, k0).then_inc(lv.sem, 1)
                dve.wait_ge(lv.sem, lv.at(0, "inv"))
                tt(z, z, y, MUL).then_inc(lv.sem, 1)
                dve.wait_ge(lv.sem, lv.at(0, "z"))
                tt(z2, z, z, MUL).then_inc(lv.sem, 1)
                dve.wait_ge(lv.sem, lv.at(0, "z2"))
                ts(k0, z2, 1.0 / 15, None, MUL).then_inc(lv.sem, 1)
                for j in range(6, 0, -1):
                    dve.wait_ge(lv.sem, lv.at(0, f"p{j}"))
                    stt(k0, k0, 1.0 / (2 * j + 1), z2, ADD, MUL).then_inc(lv.sem, 1)
                dve.wait_ge(lv.sem, lv.at(0, "p0"))
                stt(k0, k0, 1.0, z, ADD, MUL).then_inc(lv.sem, 1)
                dve.wait_ge(lv.sem, lv.at(0, "log"))
                stt(k0, k0, 2.0, pos, MUL, ADD).then_inc(lv.sem, 1)
                dve.wait_ge(lv.sem, lv.at(0, "sp"))
                for j, f in enumerate((-8.0, -16.0, 8.0)):
                    ts(LC[:, 16 * j:16 * j + 16], k0, f, None, MUL).then_inc(lv.sem, 1)
                dve.wait_ge(lv.sem, lv.at(0, "c2"))

                mv = a["mod_v"]

                def modulation(lo, hi, cols, names, which, g, off):
                    dve.wait_ge(mod_cols, cols)
                    for c in range(2):
                        tt(MOD[:, c * 48 + lo:c * 48 + hi], PS[:, 4, 0:96].rearrange("p (n c) -> p c n", c=2)[:, c, lo:hi],
                           par(l, "b_mod", lo, hi - lo), ADD).then_inc(mv.sem, 1)
                    dve.wait_ge(mv.sem, mv.at(0, names[0]))
                    for c in range(2):
                        stt(AMP[:, (2 * which + c) * KC:(2 * which + c + 1) * KC],
                            MOD[:, c * 48 + off:c * 48 + off + KC], 1.0, par(l, g, 0, KC), ADD, MUL).then_inc(mv.sem, 1)
                    dve.wait_ge(mv.sem, mv.at(0, names[1]))

                ts(BD2[:, :], par(l, "conv_d_b", 0, KC), 2.0, None, MUL).then_inc(mv.sem, 1)
                modulation(0, 16, MOD_FIRST if l == 0 else (l + 1) * NMOD, ("m1", "a1"), 0, "g_mix", 8)
                if l > 0:
                    modulation(16, 48, (l + 1) * NMOD, ("m3", "a3"), 1, "g_ffn", 32)

                def norm(nm, which, shift, c_all):
                    na, nv, nh = a[nm + "_a"].sem, a[nm + "_v"].sem, a[nm + "_h"].sem
                    dve.wait_ge(na, KC + 1)
                    V.reciprocal(tmp(1, 0, c_all * NX), tmp(0, 0, c_all * NX)).then_inc(nv, 1)
                    dve.wait_ge(nv, 1)

                    def scaled(k):
                        for c in range(c_all):
                            stt(row(S, k, NX, c * NX), row(X, k, NX, c * NX),
                                AMP[:, (2 * which + c) * KC + k:(2 * which + c) * KC + k + 1],
                                tmp(1, c * NX, (c + 1) * NX), MUL, MUL).then_inc(nv, 1)

                    def lows(k):
                        for c in range(c_all):
                            dve.wait_ge(na, KC + 1 + k * c_all + c + 1)
                            stt(row(HL, k, NX, c * NX), row(S, k, NX, c * NX),
                                MOD[:, c * 48 + shift + k:c * 48 + shift + k + 1],
                                row(HH, k, NX, c * NX).bitcast(F32), ADD, SUB).then_inc(nh, 1)

                    scaled(0)
                    for k in range(KC):
                        if k + 1 < KC:
                            scaled(k + 1)
                        lows(k)

                norm("n1", 0, 0, 2)

                def conv(out, src_at, n, c, name, taps, step, first_bias=None, some=None):
                    o = seqs(out, c)
                    for k in some or range(taps):
                        src, w = src_at(k - taps // 2), par(l, name, n + 8 * k)
                        if k == 0 and first_bias is not None:
                            ins = ts(o, src, w, first_bias, MUL, ADD)
                        elif k == 0:
                            ins = ts(o, src, w, None, MUL)
                        else:
                            ins = stt(o, src, w, o, MUL, ADD)
                        step(k, ins)

                av, aa, ap = a["ci_v"], a["ci_a"], a["ci_p"]

                def c_in(n, s, m):
                    rg = bank(2 * s + 1, W)
                    V.tensor_copy(tmp(5), row(CD, n)).then_inc(av.sem, 1)
                    dve.wait_ge(aa.sem, aa.at(n, "ru"))

                    def tap(k, ins):
                        ins.then_inc(av.sem, 1)
                        dve.wait_ge(av.sem, av.at(n, f"u{k}"))

                    conv(tmp(0), lambda d: padded(n, 2, d), n, 2, "conv_c", TAPS_C, tap, first_bias=par(l, "conv_c_b", n))
                    dve.wait_ge(aa.sem, aa.at(n, "sq"))
                    ts(tmp(2, 0, W), tmp(1, 0, W), 0.044715, 1.0, MUL, ADD).then_inc(av.sem, 1)
                    dve.wait_ge(av.sem, av.at(n, "p0"))
                    tt(tmp(2, 0, W), tmp(2, 0, W), rg, MUL).then_inc(av.sem, 1)
                    dve.wait_ge(aa.sem, aa.at(n, "th"))
                    stt(tmp(4, 0, W), tmp(3, 0, W), 1.0, rg, ADD, MUL).then_inc(av.sem, 1)
                    for d in range(2):
                        dve.wait_ge(aa.sem, aa.at(n, f"i{d}"))
                        tt(row(S, 2 * d + 1), row(S, 2 * d + 1), tmp(0), MUL).then_inc(av.sem, 1)
                        dve.wait_ge(aa.sem, aa.at(n, f"e{d}"))
                        stt(row(S, 2 * d), row(S, 2 * d), 1.0, row(S, 4 + d), ADD, MUL).then_inc(av.sem, 1)
                    for d in range(2):
                        dve.wait_ge(aa.sem, aa.at(n, f"s{d}"))
                        tt(row(S, 2 * d + 1), row(S, 2 * d + 1), row(S, 2 * d), MUL).then_inc(av.sem, 1)
                    dve.wait_ge(av.sem, av.at(n, "b1"))

                    def part(j, lo, hi, back):
                        v = S[:, j * NT + lo:j * NT + hi]
                        return v[:, ::-1] if back else v

                    for d in range(2):
                        h = 4 + d
                        end = h * NT + (NX if d else NT - 1)
                        V.tensor_tensor_scan(part(h, NX, NT, d), part(6 + d, NX, NT, d), part(2 * d + 1, NX, NT, d),
                                             0.0, MUL, ADD).then_inc(av.sem, 1)
                        dve.wait_ge(av.sem, av.at(n, f"hc{d}"))
                        V.tensor_tensor_scan(part(h, 0, NX, d), part(6 + d, 0, NX, d), part(2 * d + 1, 0, NX, d),
                                             S[:, end:end + 1], MUL, ADD).then_inc(av.sem, 1)
                    dve.wait_ge(av.sem, av.at(n, "hx1"))
                    tt(tmp(6, 0, W), row(S, 4, W), row(S, 5, W), ADD).then_inc(av.sem, 1)
                    dve.wait_ge(av.sem, av.at(n, "rec"))
                    stt(tmp(2, 0, W), tmp(6, 0, W), 0.5, tmp(4, 0, W), MUL, MUL).then_inc(av.sem, 1)
                    dve.wait_ge(aa.sem, aa.at(n, "zh"))
                    z_low(n, W, tmp(2, 0, W)).then_inc(slab_out[s], 1)

                dve.wait_ge(lru_loaded, 16 * (l + 1))
                stage(l, "c_in", c_in)

                def gated(which, first=False, before=None):
                    def body(n, s, m):
                        if before is not None:
                            before(n)
                        sa, sv = a[which + "_a"], a[which + "_v"]
                        dve.wait_ge(sa.sem, sa.at(n, "sg"))
                        if first:
                            tt(row(S, n, W), tmp(s, 0, W), bank(2 * s + 1, W), MUL).then_inc(slab_out[s], 1)
                        else:
                            tt(tmp(2 + s, 0, W), tmp(s, 0, W), bank(2 * s + 1, W), MUL).then_inc(sv.sem, 1)
                            dve.wait_ge(sv.sem, sv.at(n, "t"))
                            tt(row(S, n, W), row(S, n, W), tmp(2 + s, 0, W), ADD).then_inc(slab_out[s], 1)
                    return body

                stage(l, "c_out", gated("co", first=True))

                def rotated(sa, sv, sp_, n, s, out):
                    for t in range(2):
                        dve.wait_ge(sa.sem, sa.at(n, f"x{t}" if "x0" in sa.names else f"c{t}"))
                        tt(out(t), bank(2 * s + t, NX), COS, MUL).then_inc(sv.sem, 1)
                    for t in range(2):
                        dve.wait_ge(sp_.sem, sp_.at(n, f"r{t}"))
                        tt(tmp(6, t * NX, t * NX + NX), bank(4 + 2 * s + t, NX), SIN, MUL).then_inc(sv.sem, 1)
                        dve.wait_ge(sv.sem, sv.at(n, f"b{t}"))
                        tt(out(t), out(t), tmp(6, t * NX, t * NX + NX), ADD)\
                            .then_inc(*((slab_out[s], 1) if t else (sv.sem, 1)))

                b = pair_base(l, "kv")
                all_out(dve, l, "kv")
                dve.wait_ge(tile_done[0], 2 * b + 2)
                rotated(a["kv_a"], a["kv_v"], a["kv_p"], 0, 0, lambda t: KT[t][:, 0:NX])
                if l == DEPTH - 1:
                    low(b + 1, 0)
                dve.wait_ge(tile_done[1], 2 * b + 2)
                dve.wait_ge(a["kv_a"].sem, a["kv_a"].at(0, "v0"))
                V.tensor_copy(tmp(3), bank(3)).then_inc(slab_out[1], 1)
                if l == DEPTH - 1:
                    low(b + 1, 1)
                stage(l, "q", lambda n, s, m: rotated(a["q_a"], a["q_v"], a["q_p"], n, s,
                                                      lambda t: row(CD, 2 * n + t, NX)))

                dv, da, dp = a["di_v"], a["di_a"], a["di_p"]
                units = 3 if l == 0 else 2

                def d_in_slab(n, s, m):
                    sink = par(l, "sink", n)
                    for u in range(units):
                        q = 2 if u == 2 else 1
                        mx, mm_, nm, dn, es, d2, rd = (SM[:, 2 * j:2 * j + q] for j in range(7))

                        def step(ins, name):
                            ins.then_inc(dv.sem, 1)
                            dve.wait_ge(dv.sem, dv.at(n, name))

                        dve.wait_ge(dp.sem, dp.at(n, f"s{u}"))
                        if u < 2:
                            far = bank(5, P, (1 - u) * P)
                            step(tt(far, far, TRI[u], ADD), f"k{u}")
                            step(V.reduce_max(mx, bank(5), AX.X), f"m{u}")
                        else:
                            step(V.reduce_max(mx, seqs(bank(5), 2), AX.X), "m2")
                        step(ts(mm_, mx, SCALE, sink, MUL, MAX), f"s{u}")
                        ts(nm, mm_, -1.0, None, MUL).then_inc(dv.sem, 1)
                        ts(es, mm_, -1.0, sink, MUL, ADD).then_inc(dv.sem, 1)
                        dve.wait_ge(da.sem, da.at(n, f"e{u}"))
                        step(tt(d2, dn, es, ADD), f"d{u}")
                        step(V.reciprocal(rd, d2), f"r{u}")
                        if u < 2:
                            ts(PR, PR, SM[:, 12:13], None, MUL).then_inc(dv.sem, 1)
                        else:
                            for j in range(2):
                                h = PR[:, j * NC:(j + 1) * NC]
                                ts(h, h, SM[:, 12 + j:13 + j], None, MUL).then_inc(dv.sem, 1)
                    dve.wait_ge(da.sem, da.at(n, "zh"))
                    z_low(n, W, bank(7, W)).then_inc(dv.sem, 1)
                    dve.wait_ge(tile_done[s], 2 * m + 2)
                    dve.wait_ge(da.sem, da.at(n, "th"))
                    stt(padded(n, C), padded(n, C), 1.0, seqs(bank(2 * s, W), C), ADD, MUL).then_inc(slab_out[s], 1)

                b = pair_base(l, "d_in")
                with dve.Fori(0, dict(STAGES)["d_in"] // 2) as i:
                    for s in range(2):
                        d_in_slab(2 * i + s, s, i + b)
                        if l == DEPTH - 1:
                            low(i + (b + 1), s)

                def conv_d(stage_, sv, name, n, j=None):
                    j = n if j is None else j

                    def tap(k, ins):
                        ins.then_inc(sv.sem, 1)
                        dve.wait_ge(sv.sem, sv.at(n, name(k)))

                    conv(row(CD, j, W), lambda d: padded(j, C, d), j, C, "conv_d", TAPS_D, tap,
                         first_bias=BD2[:, ds(j, 1)], some=D_TAPS[stage_])

                all_out(dve, l, "b_out")
                stage(l, "b_out", gated("bo", before=lambda n: conv_d("b_out", a["bo_v"], lambda k: f"k{k}", n)))
                V.memset(PADA[:, :], 0.0).then_inc(a["pad_v"].sem, 1)
                dve.wait_ge(a["pad_v"].sem, 1)

                def a_cu(n, s, m):
                    sa, sv = a["ac_a"], a["ac_v"]

                    def src(d):
                        return PADA[:, s * GW:(s + 1) * GW].rearrange("p (c t) -> p c t", c=2)[:, 0:C, PAD + d:PAD + d + NX]

                    dve.wait_ge(sa.sem, sa.at(n, "c"))
                    tt(src(0), seqs(tmp(s, 0, W), C), seqs(bank(2 * s + 1, W), C), MUL).then_inc(sv.sem, 1)
                    dve.wait_ge(sv.sem, sv.at(n, "g"))

                    def tap(k, ins):
                        ins.then_inc(sv.sem, 1)
                        dve.wait_ge(sv.sem, sv.at(n, f"c{k}"))

                    conv(tmp(2 + s, 0, W), src, n, C, "conv_a", TAPS_A, tap)
                    conv_d("a_cu", sv, lambda k: f"k{k}", n)
                    dve.wait_ge(sa.sem, sa.at(n, "zh"))
                    z_low(n, W, tmp(2 + s, 0, W)).then_inc(slab_out[s], 1)

                stage(l, "a_cu", a_cu)

                def a_b(n, s, m):
                    sa, sv = a["ab_a"], a["ab_v"]
                    for t in range(2):
                        tt(tmp(2 * s + t, 0, W), row(ZH, 2 * n + t, W).bitcast(F32), row(ZL, 2 * n + t, W).bitcast(F32), ADD)\
                            .then_inc(sv.sem, 1)
                    for t in range(2):
                        dve.wait_ge(sv.sem, sv.at(n, f"e{t}"))
                        tt(tmp(2 * s + t, 0, W), bank(2 * s + t, W), tmp(2 * s + t, 0, W), MUL).then_inc(sv.sem, 1)
                    for k in D_TAPS["a_b"]:
                        for t in range(2):
                            j = 2 * n + t
                            if k > D_TAPS["a_b"][0]:
                                dve.wait_ge(sv.sem, sv.at(n, f"k{k - 1}_{t}"))
                            o = seqs(row(CD, j, W), C)
                            stt(o, padded(j, C, k - TAPS_D // 2), par(l, "conv_d", j + 8 * k), o, MUL, ADD).then_inc(sv.sem, 1)
                    for t in range(2):
                        dve.wait_ge(sa.sem, sa.at(n, f"z{t}"))
                        z_low(2 * n + t, W, tmp(2 * s + t, 0, W)).then_inc(*((slab_out[s], 1) if t else (sv.sem, 1)))

                all_out(dve, l, "a_b")
                stage(l, "a_b", a_b)

                lv, la, lp = a["ln_v"], a["ln_a"], a["ln_p"]
                all_out(dve, l, "a_out")
                dve.wait_ge(lp.sem, lp.at(0, "mean"))
                ts(tmp(4, 0, W), bank(4, W), 1.0 / D, None, MUL).then_inc(lv.sem, 1)
                dve.wait_ge(lv.sem, lv.at(0, "mu"))
                for k in range(KC):
                    tt(row(CD, k, W), row(CD, k, W), tmp(4, 0, W), SUB).then_inc(lv.sem, 1)
                stage(l, "a_out", gated("ao"), some=(0, 2))
                dve.wait_ge(la.sem, la.at(0, "rms"))
                V.reciprocal(tmp(6, 0, W), tmp(5, 0, W)).then_inc(lv.sem, 1)
                dve.wait_ge(lv.sem, lv.at(0, "rstd"))

                def ln_gate(k):
                    dve.wait_ge(la.sem, la.at(0, f"g{k}"))
                    stt(seqs(row(CD, k, W), C), seqs(row(CD, k, W), C), par(l, "ln_b", k), padded(k, C), ADD, MUL)\
                        .then_inc(lv.sem, 1)

                for k in range(KC):
                    stt(row(CD, k, W), row(CD, k, W), par(l, "ln_g", k), tmp(6, 0, W), MUL, MUL).then_inc(lv.sem, 1)
                    if k > 0:
                        ln_gate(k - 1)
                ln_gate(KC - 1)
                stage(l, "a_out", gated("ao"), some=(2, 4))
                for k in range(KC):
                    dve.wait_ge(a["ln_h"].sem, k + 1)
                    z_low(k, W, row(CD, k, W)).then_inc(a["ln_l"].sem, 1)
                stage(l, "d_out", gated("do"))

                all_out(dve, l, "w_out")
                for k in range(KC):
                    dve.wait_ge(a["ws_a"].sem, k + 1)
                    z_low(k, W, row(S, k, W)).then_inc(a["ws_v"].sem, 1)

                def residual(which, gt):
                    def body(n, s, m):
                        for t in range(2):
                            for c in range(C):
                                x = row(X, 2 * n + t, NX, c * NX)
                                g = MOD[:, ds(2 * n + (t + gt + 48 * c), 1)] if not isinstance(n, int) else \
                                    MOD[:, 2 * n + t + gt + 48 * c:2 * n + t + gt + 48 * c + 1]
                                stt(x, bank(2 * s + t, NX, c * NX), g, x, MUL, ADD)\
                                    .then_inc(*((slab_out[s], 1) if (t, c) == (1, C - 1) else (a[which + "_v"].sem, 1)))
                    return body

                if l == 0:
                    modulation(16, 48, NMOD, ("m3", "a3"), 1, "g_ffn", 32)
                stage(l, "w_out", residual("wo", 16))
                norm("n2", 1, 24, C)
                for f in range(len(FF_PARTS)):
                    fa, fv = a[f"fi{f}_a"], a[f"fi{f}_v"]

                    def ff_in(n, s, m):
                        dve.wait_ge(fa.sem, fa.at(n, "sg"))
                        tt(tmp(2 + s, 0, W), tmp(s, 0, W), bank(2 * s, W), MUL).then_inc(fv.sem, 1)
                        dve.wait_ge(fv.sem, fv.at(n, "p"))
                        tt(tmp(4 + s, 0, W), tmp(2 + s, 0, W), bank(2 * s + 1, W), MUL).then_inc(fv.sem, 1)
                        dve.wait_ge(fa.sem, fa.at(n, "zh"))
                        z_low(n, W, tmp(4 + s, 0, W)).then_inc(slab_out[s], 1)

                    stage(l, f"ff_in{f}", ff_in)
                    all_out(dve, l, f"ff_out{f}")
                    stage(l, f"ff_out{f}", residual(f"fo{f}", 40))
                    if (l, f) != (DEPTH - 1, len(FF_PARTS) - 1):
                        all_out(dve, l, f"ff_in{f + 1}") if f + 1 < len(FF_PARTS) else all_out(dve, l + 1, "c_in")
            dve.wait_ge(fin_a, KC + 1)
            V.reciprocal(tmp(1, 0, NX), tmp(0, 0, NX)).then_inc(fin_v, 1)
            dve.wait_ge(fin_v, 1)
            for k in range(KC):
                stt(CD[:, k * NX:(k + 1) * NX], row(X, k, NX), par(0, "g_final", k), tmp(1, 0, NX), MUL, MUL)\
                    .then_inc(fin_v, 1)


def slab_tiles(w, c0, c1=None, r0=0):
    cols = [c0, c0 + P if c1 is None else c1]
    rows = min(w.shape[0] - r0, D)
    out = np.zeros((P, KC, 2, P), np.float32)
    for t, c in enumerate(cols):
        out[:, :rows // P, t, :] = w[r0:r0 + rows, c:c + P].reshape(rows // P, P, P).transpose(1, 0, 2)
    return out.reshape(P, SLAB)


def layer_stream(w_in, w_a, w_b, w_c, w_d, w_out, w_fi, w_fo):
    at = dict(zip(("a_b", "a_c", "a_u", "q", "k", "v", "r_g", "r_u", "d_v", "d_g", "gl"),
                  np.cumsum([0, D, D, D, D, 256, 256, D, D, D, D])))
    ff = FF_TILES * P
    s = []

    def two(x, y):
        s.extend(slab_tiles(w_in, at[x] + j * P, at[y] + j * P) for j in range(KC))

    def branch(w, n):
        for j in range(KC):
            c = at["gl"] + n * D + j * P
            g, y = (slab_tiles(x, a, a).reshape(P, KC, 2, P)[:, :, 0] for x, a in ((w_in, c), (w, j * P)))
            s.append(np.stack([g, y], axis=2).reshape(P, SLAB))

    two("r_u", "r_g")
    branch(w_c, 2)
    s.append(slab_tiles(w_in, at["k"]))
    s.append(slab_tiles(w_in, at["v"]))
    s.extend(slab_tiles(w_in, at["q"] + 2 * j * P) for j in range(KC // 2))
    two("d_v", "d_g")
    branch(w_b, 1)
    two("a_c", "a_u")
    s.extend(slab_tiles(w_in, at["a_b"] + 2 * j * P) for j in range(KC // 2))
    branch(w_a, 0)
    branch(w_d, 3)
    s.extend(slab_tiles(w_out, 2 * j * P) for j in range(KC // 2))
    first = 0
    for n in FF_PARTS:
        s.extend(slab_tiles(w_fi, (first + j) * P, ff + (first + j) * P) for j in range(n))
        s.extend(slab_tiles(w_fo[first * P:(first + n) * P], 2 * j * P) for j in range(KC // 2))
        first += n
    return s


def constants():
    half = HD // 2
    inv = (10000.0 ** (-np.arange(0, half, 2, dtype=np.float32) / half)).astype(np.float32)
    tok = np.arange(NX)
    row_, col = (tok // 64).astype(np.float32), (tok % 64).astype(np.float32)
    ar, ac = row_[:, None] * inv, col[:, None] * inv
    ang = np.concatenate([ar, ar, ac, ac], axis=-1).astype(np.float32)
    q = HD // 4
    sign = np.repeat(np.array([-1, 1, -1, 1], np.float32), q)
    rope = np.concatenate([np.cos(ang).T, (np.sin(ang) * sign).T], axis=1).astype(np.float32)
    swap = np.concatenate([np.arange(q) + q, np.arange(q), np.arange(q) + 3 * q, np.arange(q) + 2 * q])
    rot = np.zeros((P, P), np.float32)
    rot[swap, np.arange(P)] = 1.0
    i, j = np.arange(P)[:, None], np.arange(P)[None, :]
    tri0 = np.where(j <= i, 0.0, NEG).astype(np.float32)
    tri1 = np.where(j >= i, 0.0, NEG).astype(np.float32)
    sel = np.zeros((P, 2), np.float32)
    for g in range(4):
        sel[32 * g, 0] = sel[32 * g + 1, 1] = 1.0
    return rope, np.concatenate([np.eye(P, dtype=np.float32), np.ones((P, P), np.float32), rot, tri0, tri1, sel], axis=1)


def columns(v):
    return np.asarray(v).reshape(-1, P).T


def kernel(**inputs):
    import concourse.bacc as bacc
    from concourse.bass_utils import run_bass_kernel_spmd

    w = {k: np.asarray(v) for k, v in inputs.items()}
    stream, modw, lruw, prm = [], [], [], []
    for l in range(DEPTH):
        stream += layer_stream(*(w[k][l] for k in ("w_in", "w_a_out", "w_b_out", "w_c_out", "w_d_out", "w_out",
                                                   "w_ffn_in", "w_ffn_out")))
        modw += [slab_tiles(w["w_mod"][l], 2 * j * P) for j in range(NMOD)]
        gates = np.stack([w["lru_wa"][l, 0], w["lru_wx"][l, 0], w["lru_wa"][l, 1], w["lru_wx"][l, 1]])
        lruw.append(gates.transpose(2, 1, 0, 3).reshape(P, KC * NT))
        prm.append(np.concatenate(
            [columns(w[k][l]) for k in ("b_mod", "g_mix", "g_ffn", "conv_a", "conv_c", "conv_c_b", "lru_ba", "lru_bx",
                                        "lru_lam", "conv_d", "conv_d_b", "ln_d_g", "ln_d_b")]
            + [columns(w["g_final"]), np.broadcast_to(w["sink"][l], (P, HEADS))], axis=1))
    tokens = np.concatenate([w["x"][0], w["ctx"][0]], axis=0)
    xT = tokens.T.reshape(KC, P, NT).transpose(1, 0, 2).reshape(P, KC * NT)
    cT = np.stack([w["c"][0], w["c_ctx"]], axis=-1).reshape(KC, P, 2).transpose(1, 0, 2).reshape(P, 2 * KC)
    rope, consts = constants()
    arrays = {"stream": np.stack(stream), "modw": np.stack(modw), "lruw": np.stack(lruw), "xT": xT, "cT": cT,
              "prm": np.concatenate(prm, axis=1), "rope": rope, "consts": consts}
    arrays = {k: np.ascontiguousarray(v) for k, v in arrays.items()}

    nc = bacc.Bacc("TRN2", target_bir_lowering=False, num_devices=1)
    args = [nc.dram_tensor("in_" + k, v.shape, F32, kind="ExternalInput").ap() for k, v in arrays.items()]
    out = nc.dram_tensor("outT", (P, KC * NX), F32, kind="ExternalOutput").ap()
    build(nc, *args, out)
    r = run_bass_kernel_spmd(nc, [{"in_" + k: v for k, v in arrays.items()}], core_ids=[0])
    y = np.asarray(r.results[0]["outT"]).reshape(P, KC, NX)
    return y.transpose(2, 1, 0).reshape(1, NX, D)
```

```python
from contextlib import ExitStack

import numpy as np
import concourse.bass as bass
from concourse import mybir

P = 128
F32 = mybir.dt.float32
F32R = mybir.dt.float32r
ALU = mybir.AluOpType
ACT = mybir.ActivationFunctionType
AX = mybir.AxisListType
ds = bass.ds

DEPTH = 2
D = 1024
KC = D // P
NX = 256
NC = 256
NT = NX + NC
HEADS, KVH, HD = 8, 2, 128
SCALE = float(HD) ** -0.5
EPS = 1e-6
TAPS_A, TAPS_C, TAPS_D = 3, 4, 31
FF_TILES = 22
FF_PARTS = (8, 8, 6)
PAD = 15
SEG = NX + 2 * PAD
GW = 2 * SEG
SLAB = KC * 2 * P
HALF = SLAB // 2
NMOD = 6 * KC // 2
MOD_FIRST = 2 * KC // 2
MOD_IN = {(0, "d_out"): (2, MOD_FIRST // 2, 2), (0, "w_out"): (2, MOD_FIRST // 2 + 4, 0), (0, "ff_in0"): (2, NMOD // 2, 0),
          (0, "ff_in1"): (1, NMOD // 2 + KC, 0)}
D_TAPS = {"b_out": range(0, 14), "a_cu": range(14, 24), "a_b": range(24, TAPS_D)}
POOL_WHOLE = ("c_in", "kv", "q", "d_in", "b_out", "a_cu", "a_b")
GELU_C = 0.7978845608028654
NEG = -1e30

_cols, _at = {}, 0
for _name, _n in (("b_mod", 48), ("g_mix", 8), ("g_ffn", 8), ("conv_a", 24), ("conv_c", 32), ("conv_c_b", 8),
                  ("ba", 16), ("bx", 16), ("lam", 16), ("conv_d", 248), ("conv_d_b", 8), ("ln_g", 8), ("ln_b", 8),
                  ("g_final", 8), ("sink", 8)):
    _cols[_name] = _at
    _at += _n
NPRM = _at

STAGES = [("c_in", 8), ("kv", 2), ("q", 4), ("c_out", 8), ("d_in", 8), ("b_out", 8), ("a_cu", 8), ("a_b", 4),
          ("a_out", 8), ("d_out", 8), ("w_out", 4)]
for _f, _n in enumerate(FF_PARTS):
    STAGES += [(f"ff_in{_f}", _n), (f"ff_out{_f}", 4)]
LAYER_SLABS = sum(n for _, n in STAGES)


def pair_base(layer, stage):
    n = layer * LAYER_SLABS
    for name, k in STAGES:
        if name == stage:
            return n // 2
        n += k
    raise KeyError(stage)


ATTENTION = [[("t0", 6), ("t1", 9), ("o0", 9), ("t2", 13), ("o1", 13), ("o2", 16)],
             [("t0", 12), ("t1", 14), ("o0", 16), ("o1", 16)]]


class Steps:

    def __init__(self, sem, names):
        self.sem = sem
        self.names = names.split()

    def at(self, n, name):
        return n * len(self.names) + self.names.index(name) + 1


def build(nc, stream, modw, lruw, xT, cT, prm, rope, consts, outT):
    with ExitStack() as ctx:
        def sb(name, n, dt=F32):
            return ctx.enter_context(nc.sbuf_tensor(name, [P, n], dt))

        def sem(name):
            return ctx.enter_context(nc.semaphore(name))

        X = sb("X", KC * NT)
        HH = sb("HH", KC * NT, F32R)
        HL = sb("HL", KC * NT, F32R)
        ZH = sb("ZH", KC * NT, F32R)
        ZL = sb("ZL", KC * NT, F32R)
        S = sb("S", KC * NT)
        G = sb("G", KC * GW)
        CD = sb("CD", KC * NT)
        PADA = sb("PADA", 2 * GW)
        RAW = sb("RAW", 2 * SLAB)
        WH = sb("WH", 2 * SLAB, F32R)
        WL = sb("WL", 2 * SLAB, F32R)
        TMP = sb("TMP", 7 * NT)
        PRM = sb("PRM", DEPTH * NPRM)
        ROPE = sb("ROPE", 2 * NX)
        CST = sb("CST", 5 * P + 2)
        MOD = sb("MOD", 2 * 48)
        AMP = sb("AMP", 2 * 2 * KC)
        CIN = sb("CIN", 2 * KC)
        SILC = sb("SILC", 32 * KC)
        SG = sb("SG", 2 * KC)
        LC = sb("LC", 3 * 16)
        LT = sb("LT", 5 * 16)
        EPST = sb("EPST", 2)
        WARM = sb("WARM", 1)
        BD2 = sb("BD2", KC)
        SM = sb("SM", 3 * 14)
        PS = ctx.enter_context(nc.psum_tensor("PS", [P, 8, 512], F32))

        EPSC, EPS4 = EPST[:, 0:1], EPST[:, 1:2]
        IDENT, ONES, ROT = CST[:, 0:P], CST[:, P:2 * P], CST[:, 2 * P:3 * P]
        TRI = [CST[:, 3 * P:4 * P], CST[:, 4 * P:5 * P]]
        SEL = CST[:, 5 * P:5 * P + 2]
        COS, SIN = ROPE[:, 0:NX], ROPE[:, NX:2 * NX]

        def tmp(i, a=0, b=NT):
            return TMP[:, i * NT + a:i * NT + b]

        KT = [tmp(0), tmp(1)]
        VT = [[TMP[:, (2 + c // 2) * NT + (c % 2) * 256 + kv * P:(2 + c // 2) * NT + (c % 2) * 256 + kv * P + P]
               for c in range(4)] for kv in range(KVH)]
        PR = [tmp(4), PADA[:, 0:NT]]
        PT = [tmp(5), PADA[:, NT:2 * NT]]

        QS = [[tmp(6, q * P, q * P + P) for q in range(4)],
              [G[:, (KC - 1) * GW + (q // 2) * SEG + PAD + (q % 2) * P:(KC - 1) * GW + (q // 2) * SEG + PAD + (q % 2) * P + P]
               for q in range(4)]]

        MROW = [tmp(6, 0, NX), tmp(6, NX, NT)]

        def par(l, name, i=0, n=1):
            return PRM[:, ds(i + (l * NPRM + _cols[name]), n)] if not isinstance(i, int) else \
                PRM[:, l * NPRM + _cols[name] + i:l * NPRM + _cols[name] + i + n]

        def row(t, j, w=NT, a=0):
            return t[:, j * NT + a:j * NT + a + w] if isinstance(j, int) else t[:, ds(j * NT + a, w)]

        def lc(j, n, d):
            return LC[:, ds(n + (16 * j + 8 * d), 1)]

        def bank(b, w=NT, a=0):
            return PS[:, b, a:a + w]

        def seqs(ap, c):
            return ap.rearrange("p (c t) -> p c t", c=c)

        def padded(j, c, shift=0):
            base = G[:, j * GW:j * GW + GW] if isinstance(j, int) else G[:, ds(j * GW, GW)]
            return base.rearrange("p (c t) -> p c t", c=2)[:, 0:c, PAD + shift:PAD + shift + NX]

        raw_loaded = [sem(f"raw_loaded{s}") for s in range(2)]
        hi_done = [sem(f"hi_done{s}") for s in range(2)]
        lo_done = [sem(f"lo_done{s}") for s in range(2)]
        tile_done = [sem(f"tile_done{s}") for s in range(2)]
        slab_out = [sem(f"slab_out{s}") for s in range(2)]
        mod_loaded = [sem(f"mod_loaded{s}") for s in range(2)]
        mod_used = [sem(f"mod_used{s}") for s in range(2)]
        mod_copied = [sem(f"mod_copied{s}") for s in range(2)]
        mod_cols = sem("mod_cols")
        in_loaded, par_loaded, lru_loaded = sem("in_loaded"), sem("par_loaded"), sem("lru_loaded")
        x_loaded = sem("x_loaded")
        table_set = sem("table_set")
        out_stored = sem("out_stored")
        eps_set, sigmoid_c, silu_c = sem("eps_set"), sem("sigmoid_c"), sem("silu_c")

        def stage_sems(l):
            a = {}

            def st(name, names=""):
                a[name] = Steps(sem(f"{name}_{l}"), names)

            st("lam_a", "abs exp")
            st("lam_v", "pos den inv z z2 p6 p5 p4 p3 p2 p1 p0 log sp c0 c1 c2")
            st("mod_v", "b2 m0 m1 a0 a1 m2 m3 m4 m5 a2 a3")
            for nm in ("n1", "n2"):
                for eng in "apvh":
                    st(f"{nm}_{eng}")
            st("cf_a", "ru sq th")
            st("cf_v", "wc u0 u1 u2 u3 p0 p1")
            st("ci_a", "r0 r1 i0 i1 t0 t1 a0 a1 e0 e1 s0 s1")
            st("ci_v", "iu0 iu1 w0 w1 b0 b1 hc0 hx0 hc1 hx1 rec y")
            st("ci_h", "zh")
            st("ci_l", "zl")
            st("ci_p", "gates")
            st("ac_a", "c zh")
            st("ac_v", "g c0 c1 c2")
            for nm in D_TAPS:
                st(f"cd_{nm}", " ".join(f"k{k}_{t}" for k in D_TAPS[nm] for t in range(2)))
            st("ab_a", "z0 z1")
            st("ab_v", "e0 e1 p0 p1 l0")
            for nm in ("co", "ao", "bo", "do"):
                st(f"{nm}_a", "sg")
            st("co_v")
            st("ao_v", "t")
            st("do_v", "t")
            st("bo_v", "s")
            st("kv_a", "c0 x0 x1 v0")
            st("kv_v", "a0 a1 b0 s0 b1 s1")
            st("kv_p", "r0 r1")
            st("q_a", "c0 c1 x0 x1" if l == 0 else "c0 c1")
            st("q_v", "a0 b0 s0 b1 s1")
            st("q_p", "r0 r1")
            ctx_unit = l == 0
            st("di_qs")
            st("di_a", "p0 e0 p1 e1 t0 " + ("p2a p2 e2 " if ctx_unit else "") + "t1 " + ("t2 " if ctx_unit else "") + "zh th")
            st("di_v", "k0 m0 s0 n0 f0 k1 m1 s1 n1 f1 " + ("m2 s2 n2 f2 " if ctx_unit else "") + "d0 r0 q0 d1 r1 q1 "
               + ("d2 r2 q2a q2 " if ctx_unit else "") + "zl")
            st("di_s", " ".join(f"s{u}" for u in range(2 + ctx_unit)))
            st("di_p", " ".join(x for x, _ in ATTENTION[l] if x[0] in "to"))
            tiles = range(KC)
            st("ln_v", " ".join(["mu"] + [f"c{k}" for k in tiles] + ["rstd", "n0"]
                                + [f"n{k} s{k - 1}" for k in tiles if k > 0] + [f"s{KC - 1}"]))
            st("ln_a", " ".join([f"q{k}" for k in tiles] + ["rms"] + [f"g{k}" for k in tiles]))
            st("ln_p", "mean var")
            st("ln_h")
            st("ln_l")
            st("pad_v")
            st("ws_a")
            st("ws_v")
            st("wo_v", "x0 x1 x2" if l == 0 else "x0")
            for f in range(len(FF_PARTS)):
                st(f"fi{f}_a", "sg zh")
                st(f"fi{f}_v", "p z")
                st(f"fo{f}_v", "x0 x1 x2" if l == 0 else "x0")
            return a

        L = [stage_sems(l) for l in range(DEPTH)]
        fin_a, fin_p, fin_v = sem("fin_a"), sem("fin_p"), sem("fin_v")

        block = ctx.enter_context(nc.Block())

        def all_out(e, l, stage):
            for s in range(2):
                e.wait_ge(slab_out[s], pair_base(l, stage) + 1)

        def read(e, l, stage):
            for s in range(2):
                e.wait_ge(tile_done[s], 2 * pair_base(l, stage))

        def out_of(e, l, stage, n):
            e.wait_ge(slab_out[n % 2], pair_base(l, stage) + n // 2 + 2)

        def seqs_of(l):
            return 2 if l == 0 else 1

        @block.sync
        def _(sp):
            sp.dma_start(CIN[:, :], cT).then_inc(in_loaded, 16)
            sp.dma_start(CST[:, :], consts).then_inc(par_loaded, 16)
            sp.dma_start(PRM[:, :], prm).then_inc(par_loaded, 16)

            def load(n, s):
                sp.dma_start(RAW[:, s * SLAB:(s + 1) * SLAB], slab_of(stream, n)).then_inc(raw_loaded[s], 16)

            def load_mod(n, s):
                sp.dma_start(CD[:, s * SLAB:(s + 1) * SLAB], slab_of(modw, n)).then_inc(mod_loaded[s], 16)

            def slab_of(t, n):
                return t[n] if isinstance(n, int) else t[ds(n, 1)]

            for s in range(2):
                load_mod(s, s)
            sp.dma_start(X[:, :], xT).then_inc(x_loaded, 16)
            sp.dma_start(ROPE[:, :], rope).then_inc(x_loaded, 16)
            with sp.Fori(1, MOD_FIRST // 2) as i:
                for s in range(2):
                    sp.wait_ge(mod_used[s], i)
                    load_mod(2 * i + s, s)
            for s in range(2):
                load(s, s)
            for l in range(DEPTH):
                for s in range(2):
                    sp.wait_ge(mod_used[s], MOD_FIRST // 2 if l == 0 else (l + 1) * NMOD // 2)
                sp.dma_start(CD[:, :], lruw[l]).then_inc(lru_loaded, 16)

                def loads(first, end, mods=0, use=0):
                    with sp.Fori(first, end) as i:
                        for s in range(2):
                            sp.wait_ge(lo_done[s], 2 * (i + 1))
                            load(2 * i + (2 + s), s)
                            for r in range(mods):
                                slot = r if mods == 2 else s
                                u = i + (use - first) if mods == 1 else 2 * i + (use - 2 * first + s)
                                sp.wait_ge(mod_used[slot], u)
                                load_mod(2 * u + slot, slot)

                at = pair_base(l, "c_in")
                for name in [k for ll, k in MOD_IN if ll == l]:
                    mods, use, skip = MOD_IN[l, name]
                    end = pair_base(l, name) + dict(STAGES)[name] // 2
                    start = pair_base(l, name) + skip
                    if start > at:
                        loads(at, start)
                    if name == "d_out":
                        sp.wait_ge(L[l]["ln_l"].sem, KC)
                    loads(start, end, mods, use)
                    at = end
                loads(at, (l + 1) * LAYER_SLABS // 2 - (l == DEPTH - 1))
            sp.wait_ge(fin_v, 1 + KC)
            sp.dma_start(outT, CD[:, 0:KC * NX]).then_inc(out_stored, 16)
            sp.wait_ge(out_stored, 16)

        @block.gpsimd
        def _(pool):
            def low(m, s, h):
                pool.wait_ge(hi_done[s], 2 * m + (h + 1))
                a, b = s * SLAB + h * HALF, s * SLAB + (h + 1) * HALF
                nc.gpsimd.tensor_tensor(WL[:, a:b], RAW[:, a:b], WH[:, a:b].bitcast(F32), ALU.subtract)\
                    .then_inc(lo_done[s], 1)

            runs = [(0, LAYER_SLABS // 2 + 1, 2)]
            for name, n in STAGES:
                first, halves = pair_base(1, name) + 1, 2 if name in POOL_WHOLE else 1
                if halves == runs[-1][2]:
                    first = runs.pop()[0]
                runs.append((first, pair_base(1, name) + 1 + n // 2, halves))
            runs[-1] = (runs[-1][0], DEPTH * LAYER_SLABS // 2, runs[-1][2])
            for first, end, halves in runs:
                with pool.Fori(first, end) as m:
                    for s in range(2):
                        for h in range(halves):
                            low(m, s, h)

        @block.tensor
        def _(pe):
            def mm(out, lhs, rhs, start, stop):
                return nc.tensor.matmul(out, lhs, rhs, start=start, stop=stop)

            def begin(m, s):
                pe.wait_ge(lo_done[s], 2 * m + 2)
                pe.wait_ge(slab_out[s], m + 1)

            def products(s, t, z, w, k, nk=KC):
                zh, zl = z
                out = bank(2 * s + t, w)
                a = s * SLAB + k * 2 * P + t * P
                wh, wl = WH[:, a:a + P], WL[:, a:a + P]
                mm(out, wh, row(zh, k, w), k == 0, False)
                mm(out, wh, row(zl, k, w), False, False)
                return mm(out, wl, row(zh, k, w), False, k == nk - 1)

            def slab(m, s, ops, nk=KC, before=None, mods=(), ready=None):
                begin(m, s)
                for t, (z, w) in enumerate(ops):
                    for k in range(nk):
                        if before is not None and z is Z and (t == 0 or ops[0][0] is not Z):
                            before(k)
                        if ready is not None and t == 0:
                            pe.wait_ge(ready[0], (k + 1) * ready[1])
                        last = products(s, t, z, w, k, nk)
                    last.then_inc(tile_done[s], 1)
                    for slot, u in mods:
                        (mod_products, mod_columns)[t](slot, u)

            def stage(l, name, ops, nk=KC, before=None, pairs=None, ready=None):
                b = pair_base(l, name)
                first, end = pairs or (0, dict(STAGES)[name] // 2)
                mods, use, skip = MOD_IN.get((l, name), (0, 0, 0))

                def pair(i, start):
                    for s in range(2):
                        slots = []
                        if start >= skip:
                            slots = [(0, 2 * i + (use - 2 * skip + s)), (1, 2 * i + (use - 2 * skip + s))] if mods == 2 \
                                else [(s, i + (use - skip))] * mods
                        slab(i + b, s, ops, nk, before if start == 0 else None, slots, ready if start == 0 else None)

                if first == 0:
                    pair(0, 0)
                    first = 1
                for lo, hi in [(first, skip), (skip, end)] if skip > first else [(first, end)]:
                    if hi > lo:
                        with pe.Fori(lo, hi) as i:
                            pair(i, lo)

            def mod_products(slot, u):
                pe.wait_ge(mod_loaded[slot], 16 * u + 16)
                for k in range(KC):
                    g = k % 4
                    w0 = slot * SLAB + k * 2 * P
                    last = nc.tensor.matmul(PS[32 * g:32 * g + 32, 5 + slot, 0:2 * P], SILC[:, 32 * k:32 * k + 32],
                                            CD[:, w0:w0 + 2 * P], start=k < 4, stop=k >= 4,
                                            tile_position=(0, 32 * g))
                last.then_inc(mod_used[slot], 1)

            def mod_columns(slot, u):
                pe.wait_ge(mod_copied[slot], u + 1)
                at = 8 * u + (4 * slot - mod_base[0])
                for t in range(2):
                    last = mm(PS[:, 4, ds(at + 2 * t, 2)] if not isinstance(at, int) else PS[:, 4, at + 2 * t:at + 2 * t + 2],
                              MROW[slot][:, t * P:(t + 1) * P], SEL, True, True)
                last.then_inc(mod_cols, 1)

            H, Z = (HH, HL), (ZH, ZL)
            mod_base = [0]
            pe.wait_ge(par_loaded, 32)

            def squares(l, nm, w):
                for k in range(KC):
                    pe.wait_ge(L[l][nm + "_a"].sem, k + 1)
                    last = mm(bank(7, w), ONES, row(S, k, w), k == 0, k == KC - 1)
                last.then_inc(L[l][nm + "_p"].sem, 1)

            pe.wait_ge(silu_c, 1)
            for s in range(2):
                mod_products(s, 0)
                mod_columns(s, 0)
            squares(0, "n1", NT)
            with pe.Fori(1, MOD_FIRST // 2) as i:
                for s in range(2):
                    mod_products(s, i)
                    mod_columns(s, i)
            for l in range(DEPTH):
                a = L[l]
                W = seqs_of(l) * NX
                if l > 0:
                    squares(l, "n1", NT)
                pe.wait_ge(a["mod_v"].sem, a["mod_v"].at(0, "m1" if l == 0 else "m5"))

                b = pair_base(l, "c_in")

                def ru_rg(i, s, ready=None):
                    slab(i + b, s, [(H, NT), (H, W)], ready=ready)

                def gates(n, s):
                    pe.wait_ge(a["cf_v"].sem, a["cf_v"].at(n, "u3"))
                    if not isinstance(n, int) or n > 0:
                        pe.wait_ge(a["ci_a"].sem, a["ci_a"].at(n - 1, "i1"))
                    for g in range(4):
                        last = mm(bank(4 + g), TMP[:, (5 + s) * NT + g * P:(5 + s) * NT + (g + 1) * P], tmp(s), True, True)
                    last.then_inc(a["ci_p"].sem, 1)

                ru_rg(0, 0, (a["n1_h"].sem, 2))
                ru_rg(0, 1)
                gates(0, 0)
                with pe.Fori(1, KC // 2) as i:
                    ru_rg(i, 0)
                    gates(2 * i - 1, 1)
                    ru_rg(i, 1)
                    gates(2 * i, 0)

                def rotate(st_a, st_p, n, s):
                    for t in range(2):
                        if f"c{t}" in st_a.names:
                            pe.wait_ge(st_a.sem, st_a.at(n, f"c{t}"))
                        else:
                            out_of(pe, l, "kv", 0)
                        mm(bank(4 + 2 * s + t, NX), ROT, tmp(4 + t, s * NX, (s + 1) * NX), True, True).then_inc(st_p.sem, 1)

                b = pair_base(l, "kv")
                slab(b, 0, [(H, NT), (H, NT)])
                gates(KC - 1, 1)
                begin(b, 1)
                for c in range(NT // P):
                    out = PS[:, 2 + c // 2, (c % 2) * 2 * P:(c % 2 + 1) * 2 * P]
                    for k in range(KC):
                        w0 = SLAB + k * 2 * P
                        h0 = k * NT + c * P
                        mm(out, HH[:, h0:h0 + P], WH[:, w0:w0 + 2 * P], k == 0, False)
                        mm(out, HH[:, h0:h0 + P], WL[:, w0:w0 + 2 * P], False, False)
                        last = mm(out, HL[:, h0:h0 + P], WH[:, w0:w0 + 2 * P], False, k == KC - 1)
                    if c % 2:
                        last.then_inc(tile_done[1], 1)
                rotate(a["kv_a"], a["kv_p"], 0, 0)
                b = pair_base(l, "q")
                slab(b, 0, [(H, W), (H, W)])
                for n in range(1, 4):
                    slab(b + n // 2, n % 2, [(H, W), (H, W)])
                    rotate(a["q_a"], a["q_p"], n - 1, (n - 1) % 2)
                pe.wait_ge(a["q_v"].sem, a["q_v"].at(1, "b1"))
                rotate(a["q_a"], a["q_p"], 3, 1)
                stage(l, "c_out", [(H, W), (Z, W)], before=lambda k: pe.wait_ge(a["ci_l"].sem, k + 1))

                b = pair_base(l, "d_in")
                units = 3 if l == 0 else 2
                dv, da, dp = a["di_v"], a["di_a"], a["di_p"]

                def scores(n, u, kv, s):
                    if u == 0:
                        pe.wait_ge(a["di_qs"].sem, n + 1)
                    if u < 2:
                        last = mm(bank(4 + u), QS[s][u], KT[kv], True, True)
                    else:
                        for q in range(2):
                            last = mm(bank(6, NC, q * NC), QS[s][2 + q],
                                      KT[kv][:, NX:NT], True, True)
                    last.then_inc(a["di_s"].sem, 1)

                def turn(n, u):
                    pe.wait_ge(dv.sem, dv.at(n, f"q{u}"))
                    for q in range(4):
                        last = nc.tensor.transpose(bank(4 + u, P, q * P), PR[u % 2][:, q * P:(q + 1) * P], IDENT)
                    last.then_inc(dp.sem, 1)

                def weigh(n, u, kv):
                    pe.wait_ge(da.sem, da.at(n, f"t{u}"))
                    if u < 2:
                        for q in range(4):
                            last = mm(bank(7, P, u * P), VT[kv][q], PT[u][:, q * P:(q + 1) * P], q == 0, q == 3)
                    else:
                        for q in range(2):
                            for r in range(2):
                                last = mm(bank(7, P, NX + q * P), VT[kv][2 + r],
                                          PT[0][:, (2 * q + r) * P:(2 * q + r + 1) * P], r == 0, r == 1)
                    last.then_inc(dp.sem, 1)

                all_out(pe, l, "d_in")
                for kv in range(KVH):
                    with pe.Fori(0, 2) as i:
                        for s in range(2):
                            n = i * 2 + (kv * 4 + s)
                            for u in range(units):
                                scores(n, u, kv, s)
                            begin(i + (b + 2 * kv), s)
                            done = 0
                            for x, steps in ATTENTION[l] + [("", 2 * KC)]:
                                for done in range(done, steps):
                                    t, k = divmod(done, KC)
                                    last = products(s, t, H, W, k)
                                    if k == KC - 1:
                                        last.then_inc(tile_done[s], 1)
                                done = steps
                                if x:
                                    turn(n, int(x[1])) if x[0] == "t" else weigh(n, int(x[1]), kv)
                stage(l, "b_out", [(H, W), (Z, W)], before=lambda k: out_of(pe, l, "d_in", k))
                stage(l, "a_cu", [(H, W), (H, W)])
                stage(l, "a_b", [(H, W), (H, W)])
                lv, la, lp = a["ln_v"], a["ln_a"], a["ln_p"]
                stage(l, "a_out", [(H, W), (Z, W)], before=lambda k: out_of(pe, l, "a_b", k // 2), pairs=(0, 1))
                cd = a["cd_a_b"]
                pe.wait_ge(cd.sem, cd.at(KC // 2 - 1, cd.names[-1]))
                for k in range(KC):
                    last = mm(bank(4, W), ONES, row(CD, k, W), k == 0, k == KC - 1)
                last.then_inc(lp.sem, 1)
                stage(l, "a_out", [(H, W), (Z, W)], pairs=(1, 2))
                pe.wait_ge(la.sem, la.at(0, f"q{KC - 1}"))
                for k in range(KC):
                    last = mm(seqs(bank(5, W), seqs_of(l)), ONES, padded(k, seqs_of(l)), k == 0, k == KC - 1)
                last.then_inc(lp.sem, 1)
                stage(l, "a_out", [(H, W), (Z, W)], pairs=(2, 4))
                stage(l, "d_out", [(H, W), (Z, W)], before=lambda k: pe.wait_ge(a["ln_l"].sem, k + 1))
                pe.wait_ge(a["mod_v"].sem, a["mod_v"].at(0, "m3"))
                stage(l, "w_out", [(Z, W), (Z, W)], before=lambda k: pe.wait_ge(a["ws_v"].sem, k + 1))
                squares(l, "n2", W)
                pe.wait_ge(a["mod_v"].sem, a["mod_v"].at(0, "m5"))
                mod_base[0] = 2 * NMOD * 2
                for f, nf in enumerate(FF_PARTS):
                    stage(l, f"ff_in{f}", [(H, W), (H, W)], ready=(a["n2_h"].sem, seqs_of(l)) if f == 0 else None)
                    stage(l, f"ff_out{f}", [(Z, W), (Z, W)], nf, before=lambda k, f=f: out_of(pe, l, f"ff_in{f}", k))
            for k in range(KC):
                pe.wait_ge(fin_a, k + 1)
                last = mm(bank(5, NX), ONES, row(S, k, NX), k == 0, k == KC - 1)
            last.then_inc(fin_p, 1)

        @block.scalar
        def _(act):
            def fn(out, in_, f, **kw):
                return nc.scalar.activation(out, in_, f, **kw)

            def high(m, s):
                act.wait_ge(raw_loaded[s], 16 * m + 16)
                for h in range(2):
                    x = slice(s * SLAB + h * HALF, s * SLAB + (h + 1) * HALF)
                    fn(WH[:, x], RAW[:, x], ACT.Copy).then_inc(hi_done[s], 1)

            def tiles(m, s, t=1):
                act.wait_ge(tile_done[s], 2 * m + (t + 1))

            warmed = [0]

            def table(f):
                if warmed[0]:
                    act.wait_ge(table_set, warmed[0])
                fn(WARM[:, :], EPSC, f).then_inc(table_set, 1)
                warmed[0] += 1

            def mod_rows(slot, u):
                act.wait_ge(mod_used[slot], u + 1)
                fn(MROW[slot], bank(5 + slot, NX), ACT.Copy).then_inc(mod_copied[slot], 1)

            def stage(l, name, body, high_first=True, some=None):
                b, pairs = pair_base(l, name), dict(STAGES)[name] // 2
                last = (l, name) == (DEPTH - 1, STAGES[-1][0])

                mods, use, skip = MOD_IN.get((l, name), (0, 0, 0))

                def one(i, s, more=True, start=0):
                    if start >= skip:
                        for slot, u in ([(0, 2 * i + (use - 2 * skip + s)), (1, 2 * i + (use - 2 * skip + s))] if mods == 2
                                        else [(s, i + (use - skip))] * mods):
                            mod_rows(slot, u)
                    if high_first and more:
                        tiles(i + b, s)
                        high(i + (b + 1), s)
                    all_out(act, l, name)
                    body(2 * i + s, s, i + b)
                    if not high_first and more:
                        tiles(i + b, s)
                        high(i + (b + 1), s)

                lo, hi = some or (0, pairs - last)
                for start, end in [(lo, skip), (skip, hi)] if skip > lo else [(lo, hi)]:
                    with act.Fori(start, end) as i:
                        for s in range(2):
                            one(i, s, start=start)
                if last:
                    for s in range(2):
                        one(pairs - 1, s, more=False)

            def norm_root(l, nm, c_all, stage_after):
                na, np_ = L[l][nm + "_a"].sem, L[l][nm + "_p"].sem
                all_out(act, l, stage_after)
                for k in range(KC):
                    fn(row(S, k, c_all * NX), row(X, k, c_all * NX), ACT.Square).then_inc(na, 1)
                act.wait_ge(np_, 1)
                fn(tmp(0, 0, c_all * NX), bank(7, c_all * NX), ACT.Sqrt, scale=1.0 / D, bias=EPSC).then_inc(na, 1)

            def norm_high(l, nm, shift, c_all):
                na, nv = L[l][nm + "_a"].sem, L[l][nm + "_v"].sem
                for k in range(KC):
                    for c in range(c_all):
                        act.wait_ge(nv, 1 + k * c_all + c + 1)
                        fn(row(HH, k, NX, c * NX), row(S, k, NX, c * NX), ACT.Identity,
                           bias=MOD[:, c * 48 + shift + k:c * 48 + shift + k + 1]).then_inc(na, 1)

            def decay(l):
                if l > 0:
                    all_out(act, l, "c_in")
                ls = L[l]["lam_a"].sem
                fn(LT[:, 0:16], par(l, "lam", 0, 16), ACT.Abs).then_inc(ls, 1)
                act.wait_ge(ls, 1)
                fn(LT[:, 16:32], LT[:, 0:16], ACT.Exp, scale=-1.0).then_inc(ls, 1)

            act.wait_ge(in_loaded, 16)
            fn(SG[:, :], CIN[:, :], ACT.Sigmoid).then_inc(sigmoid_c, 1)
            act.wait_ge(par_loaded, 32)
            decay(0)
            for s in range(2):
                mod_rows(s, 0)
            act.wait_ge(x_loaded, 32)
            norm_root(0, "n1", 2, "c_in")
            with act.Fori(1, MOD_FIRST // 2) as i:
                for s in range(2):
                    mod_rows(s, i)
            for s in range(2):
                high(0, s)
            for l in range(DEPTH):
                a = L[l]
                C = seqs_of(l)
                W = C * NX
                if l > 0:
                    decay(l)
                    norm_root(l, "n1", 2, "c_in")
                norm_high(l, "n1", 0, 2)

                av, aa = a["ci_v"], a["ci_a"]

                ks = a["kv_a"]
                b = pair_base(l, "c_in")
                fa, fv = a["cf_a"], a["cf_v"]

                def front(n, s, m, first=False):
                    act.wait_ge(tile_done[s], 2 * m + 1)
                    fn(padded(n, 2), seqs(bank(2 * s), 2), ACT.Copy).then_inc(fa.sem, 1)
                    tiles(m, s)
                    act.wait_ge(slab_out[1 - s], m + (1 + s))
                    fn(tmp(4, 0, W), bank(2 * s + 1, W), ACT.Square).then_inc(fa.sem, 1)
                    high(m + 1, s)
                    if not first:
                        z_high(n - 2)

                def gelu(n, s):
                    act.wait_ge(fv.sem, fv.at(n, "p1"))
                    fn(tmp(4, 0, W), tmp(2 + s, 0, W), ACT.Tanh, scale=GELU_C).then_inc(fa.sem, 1)

                def z_high(n):
                    act.wait_ge(av.sem, av.at(n, "y"))
                    fn(row(ZH, n, W), row(S, 5, W), ACT.Copy).then_inc(a["ci_h"].sem, 1)

                def back(n, s, first=False, last=False):
                    act.wait_ge(a["ci_p"].sem, n + 1)
                    if not first:
                        act.wait_ge(av.sem, av.at(n - 1, "b1"))
                    for d in range(2):
                        fn(row(S, 2 * d), bank(4 + 2 * d), ACT.Sigmoid, bias=par(l, "ba", n + 8 * d)).then_inc(aa.sem, 1)
                    for d in range(2):
                        fn(row(S, 2 * d + 1), bank(5 + 2 * d), ACT.Sigmoid, bias=par(l, "bx", n + 8 * d)).then_inc(aa.sem, 1)
                    if not first:
                        act.wait_ge(a["ci_l"].sem, n)
                    if last:
                        tiles(b + KC // 2, 0)
                        act.wait_ge(slab_out[1], b + KC // 2 + 1)
                        fn(tmp(4), bank(0), ACT.Copy).then_inc(ks.sem, 1)
                        fn(tmp(5), bank(1), ACT.Copy).then_inc(slab_out[0], 1)
                    for d in range(2):
                        act.wait_ge(aa.sem, aa.at(n, f"r{d}"))
                        fn(row(S, 4 + d), row(S, 2 * d), ACT.Tanh, scale=lc(2, n, d)).then_inc(aa.sem, 1)
                    if not last:
                        gelu(n + 1, 1 - s)
                    for d in range(2):
                        fn(row(S, 6 + d), row(S, 2 * d), ACT.Exp, scale=lc(0, n, d)).then_inc(aa.sem, 1)
                    for d in range(2):
                        act.wait_ge(aa.sem, aa.at(n, f"a{d}"))
                        fn(row(S, 2 * d), row(S, 2 * d), ACT.Exp, scale=lc(1, n, d)).then_inc(aa.sem, 1)
                    for d in range(2):
                        act.wait_ge(av.sem, av.at(n, f"w{d}"))
                        fn(row(S, 2 * d), row(S, 2 * d), ACT.Sqrt).then_inc(aa.sem, 1)

                front(0, 0, b, first=True)
                gelu(0, 0)
                front(1, 1, b, first=True)
                back(0, 0, first=True)
                with act.Fori(1, KC // 2) as i:
                    front(2 * i, 0, i + b)
                    back(2 * i - 1, 1)
                    front(2 * i + 1, 1, i + b)
                    back(2 * i, 0)
                z_high(KC - 2)
                tiles(b + KC // 2, 0)
                high(b + KC // 2 + 1, 0)
                back(KC - 1, 1, last=True)

                def gate(which, at=0):
                    def body(n, s, m):
                        fn(tmp(at + s, 0, W), bank(2 * s, W), ACT.Sigmoid).then_inc(a[which + "_a"].sem, 1)
                    return body

                b = pair_base(l, "kv")
                tiles(b, 1)
                high(b + 1, 1)
                z_high(KC - 1)
                act.wait_ge(a["ci_l"].sem, KC)
                act.wait_ge(ks.sem, ks.at(0, "c0"))
                out_of(act, l, "kv", 0)
                for t in range(2):
                    fn(KT[t][:, NX:NT], tmp(4 + t, NX, NT), ACT.Copy).then_inc(ks.sem, 1)
                fn(tmp(2), bank(2), ACT.Copy).then_inc(ks.sem, 1)

                def q_in(n, s, m):
                    qs = a["q_a"].sem
                    for t in range(2):
                        fn(tmp(4 + t, s * NX, (s + 1) * NX), bank(2 * s + t, NX), ACT.Copy).then_inc(qs, 1)
                    if l == 0:
                        for t in range(2):
                            fn(row(CD, 2 * n + t, NC, NX), bank(2 * s + t, NC, NX), ACT.Copy).then_inc(qs, 1)

                b = pair_base(l, "q")
                act.wait_ge(a["kv_p"].sem, 2)
                act.wait_ge(a["kv_v"].sem, a["kv_v"].at(0, "a1"))
                with act.Fori(0, 2) as i:
                    for s in range(2):
                        tiles(i + b, s)
                        q_in(2 * i + s, s, i + b)
                        high(i + (b + 1), s)
                table(ACT.Sigmoid)
                stage(l, "c_out", gate("co", 4))

                dv, da, dp = a["di_v"], a["di_a"], a["di_p"]
                units = 3 if l == 0 else 2

                def stage_q(n, s):
                    out = padded(KC - 1, C) if s else seqs(tmp(6, 0, W), C)
                    fn(out, seqs(row(CD, n, W), C), ACT.Copy).then_inc(a["di_qs"].sem, 1)

                def d_in(n, s, m, more=True):
                    def probs(u):
                        sm = 14 * u
                        act.wait_ge(dv.sem, dv.at(n, f"n{u}"))
                        if u < 2:
                            fn(PR[u], bank(4 + u), ACT.Exp, scale=SCALE, bias=SM[:, sm + 4:sm + 5],
                               accum_out=SM[:, sm + 6:sm + 7]).then_inc(da.sem, 1)
                        else:
                            for q in range(2):
                                fn(PR[0][:, q * NC:(q + 1) * NC], bank(6, NC, q * NC), ACT.Exp, scale=SCALE,
                                   bias=SM[:, sm + 4 + q:sm + 5 + q], accum_out=SM[:, sm + 6 + q:sm + 7 + q]).then_inc(da.sem, 1)
                        act.wait_ge(dv.sem, dv.at(n, f"f{u}"))
                        q = 2 if u == 2 else 1
                        fn(SM[:, sm + 8:sm + 8 + q], SM[:, sm + 8:sm + 8 + q], ACT.Exp).then_inc(da.sem, 1)

                    def turned(u):
                        act.wait_ge(dp.sem, dp.at(n, f"t{u}"))
                        if u == 2:
                            act.wait_ge(dp.sem, dp.at(n, "o0"))
                        fn(PT[u % 2], bank(4 + u), ACT.Copy).then_inc(da.sem, 1)

                    probs(0)
                    probs(1)
                    if more:
                        stage_q(n + 1, 1 - s)
                    turned(0)
                    if units == 3:
                        probs(2)
                    turned(1)
                    if units == 3:
                        turned(2)
                    if l > 0:
                        tiles(m, s)
                        high(m + 1, s)
                    act.wait_ge(dp.sem, dp.at(n, f"o{units - 1}"))
                    fn(row(ZH, n, W), bank(7, W), ACT.Copy).then_inc(da.sem, 1)
                    tiles(m, s)
                    fn(padded(n, C), seqs(bank(2 * s + 1, W), C), ACT.Tanh, scale=0.5).then_inc(da.sem, 1)
                    if l == 0:
                        high(m + 1, s)

                all_out(act, l, "d_in")
                b = pair_base(l, "d_in")
                stage_q(0, 0)
                with act.Fori(0, KC // 2 - 1) as i:
                    for s in range(2):
                        d_in(2 * i + s, s, i + b)
                for s in range(2):
                    d_in(KC - 2 + s, s, b + KC // 2 - 1, more=s == 0)
                table(ACT.Sigmoid)
                stage(l, "b_out", gate("bo"))

                def a_cu(n, s, m):
                    sa, sv = a["ac_a"], a["ac_v"]
                    fn(tmp(s, 0, W), bank(2 * s, W), ACT.Copy).then_inc(sa.sem, 1)
                    act.wait_ge(sv.sem, sv.at(n, "c2"))
                    fn(row(ZH, n, W), tmp(2 + s, 0, W), ACT.Copy).then_inc(sa.sem, 1)

                stage(l, "a_cu", a_cu)

                def a_b(n, s, m):
                    for t in range(2):
                        act.wait_ge(a["ab_v"].sem, a["ab_v"].at(n, f"p{t}"))
                        fn(row(ZH, 2 * n + t, W), tmp(2 * s + t, 0, W), ACT.Copy).then_inc(a["ab_a"].sem, 1)

                stage(l, "a_b", a_b)
                lv, la, lp = a["ln_v"], a["ln_a"], a["ln_p"]
                stage(l, "a_out", gate("ao"), some=(0, 1))
                for k in range(KC):
                    act.wait_ge(lv.sem, lv.at(0, f"c{k}"))
                    fn(padded(k, C), seqs(row(CD, k, W), C), ACT.Square).then_inc(la.sem, 1)
                table(ACT.Sigmoid)
                stage(l, "a_out", gate("ao"), some=(1, 2))
                act.wait_ge(lp.sem, lp.at(0, "var"))
                fn(tmp(5, 0, W), bank(5, W), ACT.Sqrt, scale=1.0 / D, bias=EPS4).then_inc(la.sem, 1)
                for k in range(KC):
                    act.wait_ge(lv.sem, lv.at(0, f"n{k}"))
                    fn(padded(k, C), seqs(row(CD, k, W), C), ACT.Sigmoid, bias=par(l, "ln_b", k)).then_inc(la.sem, 1)
                table(ACT.Sigmoid)
                stage(l, "a_out", gate("ao"), some=(2, 4))
                read(act, l, "d_out")
                for k in range(KC):
                    act.wait_ge(lv.sem, lv.at(0, f"s{k}"))
                    fn(row(ZH, k, W), row(CD, k, W), ACT.Copy).then_inc(a["ln_h"].sem, 1)
                stage(l, "d_out", gate("do"))

                read(act, l, "w_out")
                for k in range(KC):
                    out_of(act, l, "d_out", k)
                    fn(row(ZH, k, W), row(S, k, W), ACT.Copy).then_inc(a["ws_a"].sem, 1)
                stage(l, "w_out", lambda n, s, m: None)
                norm_root(l, "n2", C, "ff_in0")
                table(ACT.Sigmoid)
                norm_high(l, "n2", 24, C)
                for f in range(len(FF_PARTS)):
                    fa, fv = a[f"fi{f}_a"], a[f"fi{f}_v"]

                    def ff_in(n, s, m):
                        fn(tmp(s, 0, W), bank(2 * s, W), ACT.Sigmoid).then_inc(fa.sem, 1)
                        act.wait_ge(fv.sem, fv.at(n, "z"))
                        fn(row(ZH, n, W), tmp(4 + s, 0, W), ACT.Copy).then_inc(fa.sem, 1)

                    stage(l, f"ff_in{f}", ff_in)
                    stage(l, f"ff_out{f}", lambda n, s, m: None)
            for s in range(2):
                act.wait_ge(slab_out[s], DEPTH * LAYER_SLABS // 2 + 1)
            for k in range(KC):
                fn(row(S, k, NX), row(X, k, NX), ACT.Square).then_inc(fin_a, 1)
            act.wait_ge(fin_p, 1)
            fn(tmp(0, 0, NX), bank(5, NX), ACT.Sqrt, scale=1.0 / D, bias=EPSC).then_inc(fin_a, 1)

        @block.vector
        def _(dve):
            V = nc.vector

            def tt(out, x, y, op):
                return V.tensor_tensor(out, x, y, op)

            def stt(out, x, sc, y, op0, op1):
                return V.scalar_tensor_tensor(out, x, sc, y, op0, op1)

            def ts(out, x, s1, s2, op0, op1=None):
                return V.tensor_scalar(out, x, s1, s2, op0, op1) if op1 is not None else V.tensor_scalar(out, x, s1, None, op0)

            MUL, ADD, SUB, MAX = ALU.mult, ALU.add, ALU.subtract, ALU.max

            def stage(l, name, body, some=None):
                b, pairs = pair_base(l, name), dict(STAGES)[name] // 2
                last = (l, name) == (DEPTH - 1, STAGES[-1][0])

                def one(i, s, more=True):
                    dve.wait_ge(tile_done[s], 2 * (i + b) + 2)
                    body(2 * i + s, s, i + b)
                    if l == DEPTH - 1 and more and name not in POOL_WHOLE:
                        low(i + (b + 1), s)

                with dve.Fori(*(some or (0, pairs - last))) as i:
                    for s in range(2):
                        one(i, s)
                if last:
                    for s in range(2):
                        one(pairs - 1, s, more=False)

            def low(m, s):
                dve.wait_ge(hi_done[s], 2 * m + 2)
                x = slice(s * SLAB + HALF, (s + 1) * SLAB)
                tt(WL[:, x], RAW[:, x], WH[:, x].bitcast(F32), SUB).then_inc(lo_done[s], 1)

            def z_low(n, w, src):
                return tt(row(ZL, n, w), src, row(ZH, n, w).bitcast(F32), SUB)

            V.memset(G[:, 0:GW * KC // 2], 0.0).then_inc(slab_out[0], 1)
            V.memset(G[:, GW * KC // 2:GW * KC], 0.0).then_inc(slab_out[1], 1)
            V.memset(EPSC, EPS).then_inc(eps_set, 1)
            V.memset(EPS4, 4 * EPS).then_inc(eps_set, 1)
            V.memset(SILC[:, :], 0.0).then_inc(eps_set, 1)
            dve.wait_ge(eps_set, 3)
            dve.wait_ge(sigmoid_c, 1)
            tt(SILC[:, :].rearrange("p (k c) -> p k c", c=32)[:, :, 0:2], CIN[:, :].rearrange("p (k c) -> p k c", c=2),
               SG[:, :].rearrange("p (k c) -> p k c", c=2), MUL).then_inc(silu_c, 1)
            dve.wait_ge(par_loaded, 32)
            for l in range(DEPTH):
                a = L[l]
                C = seqs_of(l)
                W = C * NX

                la, lv = a["lam_a"], a["lam_v"]
                k0, y, pos, z, z2 = (LT[:, 0:16], LT[:, 16:32], LT[:, 32:48], LT[:, 48:64], LT[:, 64:80])
                dve.wait_ge(la.sem, 2)
                ts(pos, par(l, "lam", 0, 16), -1.0, 0.0, MUL, MAX).then_inc(lv.sem, 1)
                ts(k0, y, 2.0, None, ADD).then_inc(lv.sem, 1)
                dve.wait_ge(lv.sem, lv.at(0, "den"))
                V.reciprocal(z, k0).then_inc(lv.sem, 1)
                dve.wait_ge(lv.sem, lv.at(0, "inv"))
                tt(z, z, y, MUL).then_inc(lv.sem, 1)
                dve.wait_ge(lv.sem, lv.at(0, "z"))
                tt(z2, z, z, MUL).then_inc(lv.sem, 1)
                dve.wait_ge(lv.sem, lv.at(0, "z2"))
                ts(k0, z2, 1.0 / 15, None, MUL).then_inc(lv.sem, 1)
                for j in range(6, 0, -1):
                    dve.wait_ge(lv.sem, lv.at(0, f"p{j}"))
                    stt(k0, k0, 1.0 / (2 * j + 1), z2, ADD, MUL).then_inc(lv.sem, 1)
                dve.wait_ge(lv.sem, lv.at(0, "p0"))
                stt(k0, k0, 1.0, z, ADD, MUL).then_inc(lv.sem, 1)
                dve.wait_ge(lv.sem, lv.at(0, "log"))
                stt(k0, k0, 2.0, pos, MUL, ADD).then_inc(lv.sem, 1)
                dve.wait_ge(lv.sem, lv.at(0, "sp"))
                for j, f in enumerate((-8.0, -16.0, 8.0)):
                    ts(LC[:, 16 * j:16 * j + 16], k0, f, None, MUL).then_inc(lv.sem, 1)
                dve.wait_ge(lv.sem, lv.at(0, "c2"))

                mv = a["mod_v"]

                def modulation(lo, hi, cols, names, which, g, off):
                    dve.wait_ge(mod_cols, cols)
                    for c in range(2):
                        tt(MOD[:, c * 48 + lo:c * 48 + hi], PS[:, 4, 0:96].rearrange("p (n c) -> p c n", c=2)[:, c, lo:hi],
                           par(l, "b_mod", lo, hi - lo), ADD).then_inc(mv.sem, 1)
                    dve.wait_ge(mv.sem, mv.at(0, names[0]))
                    for c in range(2 if names[1] else 0):
                        stt(AMP[:, (2 * which + c) * KC:(2 * which + c + 1) * KC],
                            MOD[:, c * 48 + off:c * 48 + off + KC], 1.0, par(l, g, 0, KC), ADD, MUL).then_inc(mv.sem, 1)
                    if names[1]:
                        dve.wait_ge(mv.sem, mv.at(0, names[1]))

                ts(BD2[:, :], par(l, "conv_d_b", 0, KC), 2.0, None, MUL).then_inc(mv.sem, 1)
                def inverse_root(nm, c_all):
                    na, nv = a[nm + "_a"].sem, a[nm + "_v"].sem
                    dve.wait_ge(na, KC + 1)
                    V.reciprocal(tmp(1, 0, c_all * NX), tmp(0, 0, c_all * NX)).then_inc(nv, 1)
                    dve.wait_ge(nv, 1)

                if l == 0:
                    dve.wait_ge(x_loaded, 32)
                    inverse_root("n1", 2)
                modulation(0, 16, MOD_FIRST if l == 0 else (l + 1) * NMOD, ("m1", "a1"), 0, "g_mix", 8)
                if l > 0:
                    modulation(16, 32, (l + 1) * NMOD, ("m3", None), 1, "g_ffn", 32)
                    modulation(32, 48, (l + 1) * NMOD, ("m5", "a3"), 1, "g_ffn", 32)

                def norm(nm, which, shift, c_all):
                    na, nv, nh = a[nm + "_a"].sem, a[nm + "_v"].sem, a[nm + "_h"].sem

                    def scaled(k):
                        for c in range(c_all):
                            stt(row(S, k, NX, c * NX), row(X, k, NX, c * NX),
                                AMP[:, (2 * which + c) * KC + k:(2 * which + c) * KC + k + 1],
                                tmp(1, c * NX, (c + 1) * NX), MUL, MUL).then_inc(nv, 1)

                    def lows(k):
                        for c in range(c_all):
                            dve.wait_ge(na, KC + 1 + k * c_all + c + 1)
                            stt(row(HL, k, NX, c * NX), row(S, k, NX, c * NX),
                                MOD[:, c * 48 + shift + k:c * 48 + shift + k + 1],
                                row(HH, k, NX, c * NX).bitcast(F32), ADD, SUB).then_inc(nh, 1)

                    scaled(0)
                    for k in range(KC):
                        if k + 1 < KC:
                            scaled(k + 1)
                        lows(k)

                if l > 0:
                    inverse_root("n1", 2)
                norm("n1", 0, 0, 2)

                def conv(out, src_at, n, c, name, taps, step, first_bias=None, some=None):
                    o = seqs(out, c)
                    for k in some or range(taps):
                        src, w = src_at(k - taps // 2), par(l, name, n + 8 * k)
                        if k == 0 and first_bias is not None:
                            ins = ts(o, src, w, first_bias, MUL, ADD)
                        elif k == 0:
                            ins = ts(o, src, w, None, MUL)
                        else:
                            ins = stt(o, src, w, o, MUL, ADD)
                        step(k, ins)

                av, aa = a["ci_v"], a["ci_a"]
                fa, fv = a["cf_a"], a["cf_v"]

                def front(n, s, first=False):
                    rg, ge = bank(2 * s + 1, W), tmp(2 + s, 0, W)
                    V.tensor_copy(tmp(5 + s), row(CD, n)).then_inc(fv.sem, 1)
                    if not first:
                        z_out(n - 2)
                    dve.wait_ge(fa.sem, fa.at(n, "ru"))

                    def tap(k, ins):
                        ins.then_inc(fv.sem, 1)
                        dve.wait_ge(fv.sem, fv.at(n, f"u{k}"))

                    conv(tmp(s), lambda d: padded(n, 2, d), n, 2, "conv_c", TAPS_C, tap, first_bias=par(l, "conv_c_b", n))
                    dve.wait_ge(fa.sem, fa.at(n, "sq"))
                    ts(ge, tmp(4, 0, W), 0.044715, 1.0, MUL, ADD).then_inc(fv.sem, 1)
                    dve.wait_ge(fv.sem, fv.at(n, "p0"))
                    tt(ge, ge, rg, MUL).then_inc(fv.sem, 1)

                def gelu(n, s):
                    dve.wait_ge(fa.sem, fa.at(n, "th"))
                    stt(tmp(2 + s, 0, W), tmp(4, 0, W), 1.0, bank(2 * s + 1, W), ADD, MUL).then_inc(slab_out[s], 1)

                def part(j, lo, hi, back):
                    v = S[:, j * NT + lo:j * NT + hi]
                    return v[:, ::-1] if back else v

                def z_out(n):
                    dve.wait_ge(a["ci_h"].sem, n + 1)
                    z_low(n, W, row(S, 5, W)).then_inc(a["ci_l"].sem, 1)

                def back(n, s, m, last=False):
                    for d in range(2):
                        dve.wait_ge(aa.sem, aa.at(n, f"i{d}"))
                        tt(row(S, 2 * d + 1), row(S, 2 * d + 1), tmp(s), MUL).then_inc(av.sem, 1)
                    if not last:
                        gelu(n + 1, 1 - s)
                    for d in range(2):
                        dve.wait_ge(aa.sem, aa.at(n, f"e{d}"))
                        stt(row(S, 2 * d), row(S, 2 * d), 1.0, row(S, 4 + d), ADD, MUL).then_inc(av.sem, 1)
                    for d in range(2):
                        dve.wait_ge(aa.sem, aa.at(n, f"s{d}"))
                        tt(row(S, 2 * d + 1), row(S, 2 * d + 1), row(S, 2 * d), MUL).then_inc(av.sem, 1)
                    dve.wait_ge(av.sem, av.at(n, "b1"))
                    for d in range(2):
                        h = 4 + d
                        end = h * NT + (NX if d else NT - 1)
                        V.tensor_tensor_scan(part(h, NX, NT, d), part(6 + d, NX, NT, d), part(2 * d + 1, NX, NT, d),
                                             0.0, MUL, ADD).then_inc(av.sem, 1)
                        dve.wait_ge(av.sem, av.at(n, f"hc{d}"))
                        V.tensor_tensor_scan(part(h, 0, NX, d), part(6 + d, 0, NX, d), part(2 * d + 1, 0, NX, d),
                                             S[:, end:end + 1], MUL, ADD).then_inc(av.sem, 1)
                    dve.wait_ge(av.sem, av.at(n, "hx1"))
                    tt(row(S, 4, W), row(S, 4, W), row(S, 5, W), ADD).then_inc(av.sem, 1)
                    dve.wait_ge(av.sem, av.at(n, "rec"))
                    dve.wait_ge(slab_out[s], m + 2)
                    stt(row(S, 5, W), row(S, 4, W), 0.5, tmp(2 + s, 0, W), MUL, MUL).then_inc(av.sem, 1)

                dve.wait_ge(lru_loaded, 16 * (l + 1))
                b = pair_base(l, "c_in")
                front(0, 0, first=True)
                gelu(0, 0)
                front(1, 1, first=True)
                back(0, 0, b)
                with dve.Fori(1, KC // 2) as i:
                    front(2 * i, 0)
                    back(2 * i - 1, 1, i + (b - 1))
                    front(2 * i + 1, 1)
                    back(2 * i, 0, i + b)
                z_out(KC - 2)
                back(KC - 1, 1, b + KC // 2 - 1, last=True)
                z_out(KC - 1)

                def gated(which, first=False, at=0):
                    def body(n, s, m):
                        sa, sv = a[which + "_a"], a[which + "_v"]
                        dve.wait_ge(sa.sem, sa.at(n, "sg"))
                        if first:
                            tt(row(S, n, W), tmp(at + s, 0, W), bank(2 * s + 1, W), MUL).then_inc(slab_out[s], 1)
                        else:
                            tt(tmp(2 + s, 0, W), tmp(s, 0, W), bank(2 * s + 1, W), MUL).then_inc(sv.sem, 1)
                            dve.wait_ge(sv.sem, sv.at(n, "t"))
                            tt(row(S, n, W), row(S, n, W), tmp(2 + s, 0, W), ADD).then_inc(slab_out[s], 1)
                    return body

                def rotated(sa, sv, sp_, n, s, out):
                    for t in range(2):
                        dve.wait_ge(sa.sem, sa.at(n, f"x{t}" if "x0" in sa.names else f"c{t}"))
                        tt(out(t), bank(2 * s + t, NX), COS, MUL).then_inc(*((slab_out[s], 1) if t else (sv.sem, 1)))
                    turned(sv, sp_, n, s, out)

                def turned(sv, sp_, n, s, out):
                    for t in range(2):
                        dve.wait_ge(sp_.sem, sp_.at(n, f"r{t}"))
                        tt(tmp(6, t * NX, t * NX + NX), bank(4 + 2 * s + t, NX), SIN, MUL).then_inc(sv.sem, 1)
                        dve.wait_ge(sv.sem, sv.at(n, f"b{t}"))
                        tt(out(t), out(t), tmp(6, t * NX, t * NX + NX), ADD).then_inc(sv.sem, 1)

                b = pair_base(l, "kv")
                kv = a["kv_v"]
                for t in range(2):
                    if t == 0:
                        dve.wait_ge(a["kv_a"].sem, a["kv_a"].at(0, "c0"))
                    else:
                        out_of(dve, l, "kv", 0)
                    tt(KT[t][:, 0:NX], tmp(4 + t, 0, NX), COS, MUL).then_inc(kv.sem, 1)
                turned(kv, a["kv_p"], 0, 0, lambda t: KT[t][:, 0:NX])
                dve.wait_ge(tile_done[1], 2 * b + 2)
                dve.wait_ge(a["kv_a"].sem, a["kv_a"].at(0, "v0"))
                V.tensor_copy(tmp(3), bank(3)).then_inc(slab_out[1], 1)

                def q_in(n, s, m):
                    rotated(a["q_a"], a["q_v"], a["q_p"], n, s, lambda t: row(CD, 2 * n + t, NX))

                stage(l, "q", q_in)
                stage(l, "c_out", gated("co", first=True, at=4))

                dv, da = a["di_v"], a["di_a"]
                units = 3 if l == 0 else 2

                def d_in_slab(n, s, m):
                    sink = par(l, "sink", n)

                    def scalars(u):
                        q = 2 if u == 2 else 1
                        return (SM[:, 14 * u + 2 * j:14 * u + 2 * j + q] for j in range(7))

                    def step(ins, name):
                        ins.then_inc(dv.sem, 1)
                        dve.wait_ge(dv.sem, dv.at(n, name))

                    for u in range(units):
                        mx, mm_, nm, _, es, _, _ = scalars(u)
                        dve.wait_ge(a["di_s"].sem, a["di_s"].at(n, f"s{u}"))
                        if u < 2:
                            far = bank(4 + u, P, (1 - u) * P)
                            step(tt(far, far, TRI[u], ADD), f"k{u}")
                            step(V.reduce_max(mx, bank(4 + u), AX.X), f"m{u}")
                        else:
                            step(V.reduce_max(mx, seqs(bank(6), 2), AX.X), "m2")
                        step(ts(mm_, mx, SCALE, sink, MUL, MAX), f"s{u}")
                        ts(nm, mm_, -1.0, None, MUL).then_inc(dv.sem, 1)
                        ts(es, mm_, -1.0, sink, MUL, ADD).then_inc(dv.sem, 1)
                    for u in range(units):
                        _, _, _, dn, es, d2, rd = scalars(u)
                        dve.wait_ge(da.sem, da.at(n, f"e{u}"))
                        step(tt(d2, dn, es, ADD), f"d{u}")
                        step(V.reciprocal(rd, d2), f"r{u}")
                        if u < 2:
                            ts(PR[u], PR[u], rd, None, MUL).then_inc(dv.sem, 1)
                        else:
                            for j in range(2):
                                h = PR[0][:, j * NC:(j + 1) * NC]
                                ts(h, h, SM[:, 14 * u + 12 + j:14 * u + 13 + j], None, MUL).then_inc(dv.sem, 1)
                    dve.wait_ge(da.sem, da.at(n, "zh"))
                    z_low(n, W, bank(7, W)).then_inc(dv.sem, 1)
                    dve.wait_ge(tile_done[s], 2 * m + 2)
                    dve.wait_ge(da.sem, da.at(n, "th"))
                    stt(padded(n, C), padded(n, C), 1.0, seqs(bank(2 * s, W), C), ADD, MUL).then_inc(slab_out[s], 1)

                b = pair_base(l, "d_in")
                with dve.Fori(0, KC // 2) as i:
                    for s in range(2):
                        d_in_slab(2 * i + s, s, i + b)

                def conv_d(name, i, taps):
                    sv = a[f"cd_{name}"]
                    for k in taps:
                        for t in range(2):
                            j = 2 * i + t
                            o, w = seqs(row(CD, j, W), C), par(l, "conv_d", j + 8 * k)
                            if k > D_TAPS[name][0]:
                                dve.wait_ge(sv.sem, sv.at(i, f"k{k - 1}_{t}"))
                            if k == 0:
                                ins = ts(o, padded(j, C, -(TAPS_D // 2)), w, BD2[:, ds(j, 1)], MUL, ADD)
                            else:
                                ins = stt(o, padded(j, C, k - TAPS_D // 2), w, o, MUL, ADD)
                            ins.then_inc(sv.sem, 1)

                def half(name, s):
                    taps = D_TAPS[name]
                    return taps[:len(taps) // 2] if s == 0 else taps[len(taps) // 2:]

                all_out(dve, l, "b_out")
                b = pair_base(l, "b_out")
                with dve.Fori(0, KC // 2) as i:
                    for s in range(2):
                        n = 2 * i + s
                        conv_d("b_out", i, half("b_out", s)[:-2])
                        dve.wait_ge(tile_done[s], 2 * (i + b) + 2)
                        dve.wait_ge(a["bo_a"].sem, n + 1)
                        tt(tmp(2 + s, 0, W), tmp(s, 0, W), bank(2 * s + 1, W), MUL).then_inc(slab_out[s], 1)
                        conv_d("b_out", i, half("b_out", s)[-2:])
                        dve.wait_ge(slab_out[s], i + (b + 2))
                        tt(row(S, n, W), row(S, n, W), tmp(2 + s, 0, W), ADD).then_inc(a["bo_v"].sem, 1)
                V.memset(PADA[:, :], 0.0).then_inc(a["pad_v"].sem, 1)
                dve.wait_ge(a["pad_v"].sem, 1)

                b = pair_base(l, "a_cu")
                with dve.Fori(0, KC // 2) as i:
                    for s in range(2):
                        n = 2 * i + s
                        sa, sv = a["ac_a"], a["ac_v"]
                        taps = half("a_cu", s)
                        seq = PADA[:, s * GW:(s + 1) * GW].rearrange("p (c t) -> p c t", c=2)

                        dve.wait_ge(tile_done[s], 2 * (i + b) + 2)
                        dve.wait_ge(sa.sem, sa.at(n, "c"))
                        tt(seq[:, 0:C, PAD:PAD + NX], seqs(tmp(s, 0, W), C), seqs(bank(2 * s + 1, W), C), MUL)\
                            .then_inc(sv.sem, 1)
                        conv_d("a_cu", i, taps[0:1])
                        for k in range(TAPS_A):
                            dve.wait_ge(sv.sem, sv.at(n, f"c{k - 1}" if k else "g"))
                            o = seqs(tmp(2 + s, 0, W), C)
                            src, w = seq[:, 0:C, PAD + k - TAPS_A // 2:PAD + k - TAPS_A // 2 + NX], par(l, "conv_a", n + 8 * k)
                            (stt(o, src, w, o, MUL, ADD) if k else ts(o, src, w, None, MUL)).then_inc(sv.sem, 1)
                            conv_d("a_cu", i, taps[1 + k:2 + k])
                        conv_d("a_cu", i, taps[1 + TAPS_A:])
                        dve.wait_ge(sa.sem, sa.at(n, "zh"))
                        z_low(n, W, tmp(2 + s, 0, W)).then_inc(slab_out[s], 1)

                def a_b(n, s, m):
                    sa, sv = a["ab_a"], a["ab_v"]
                    taps = D_TAPS["a_b"]
                    for t in range(2):
                        tt(tmp(2 * s + t, 0, W), row(ZH, 2 * n + t, W).bitcast(F32), row(ZL, 2 * n + t, W).bitcast(F32), ADD)\
                            .then_inc(sv.sem, 1)
                    for t in range(2):
                        dve.wait_ge(sv.sem, sv.at(n, f"e{t}"))
                        tt(tmp(2 * s + t, 0, W), bank(2 * s + t, W), tmp(2 * s + t, 0, W), MUL).then_inc(sv.sem, 1)
                    conv_d("a_b", n, taps[:2])
                    for t in range(2):
                        dve.wait_ge(sa.sem, sa.at(n, f"z{t}"))
                        z_low(2 * n + t, W, tmp(2 * s + t, 0, W)).then_inc(*((slab_out[s], 1) if t else (sv.sem, 1)))
                    conv_d("a_b", n, taps[2:])

                all_out(dve, l, "a_b")
                stage(l, "a_b", a_b)

                lv, la, lp = a["ln_v"], a["ln_a"], a["ln_p"]
                stage(l, "a_out", gated("ao"), some=(0, 1))
                dve.wait_ge(lp.sem, lp.at(0, "mean"))
                ts(tmp(4, 0, W), bank(4, W), 1.0 / D, None, MUL).then_inc(lv.sem, 1)
                dve.wait_ge(lv.sem, lv.at(0, "mu"))
                for k in range(KC):
                    tt(row(CD, k, W), row(CD, k, W), tmp(4, 0, W), SUB).then_inc(lv.sem, 1)
                stage(l, "a_out", gated("ao"), some=(1, 2))
                dve.wait_ge(la.sem, la.at(0, "rms"))
                V.reciprocal(tmp(6, 0, W), tmp(5, 0, W)).then_inc(lv.sem, 1)
                dve.wait_ge(lv.sem, lv.at(0, "rstd"))

                def ln_gate(k):
                    dve.wait_ge(la.sem, la.at(0, f"g{k}"))
                    stt(seqs(row(CD, k, W), C), seqs(row(CD, k, W), C), par(l, "ln_b", k), padded(k, C), ADD, MUL)\
                        .then_inc(lv.sem, 1)

                for k in range(KC):
                    stt(row(CD, k, W), row(CD, k, W), par(l, "ln_g", k), tmp(6, 0, W), MUL, MUL).then_inc(lv.sem, 1)
                    if k > 0:
                        ln_gate(k - 1)
                ln_gate(KC - 1)
                stage(l, "a_out", gated("ao"), some=(2, 4))
                for k in range(KC):
                    dve.wait_ge(a["ln_h"].sem, k + 1)
                    z_low(k, W, row(CD, k, W)).then_inc(a["ln_l"].sem, 1)
                stage(l, "d_out", gated("do"))

                if l == 0:
                    modulation(16, 32, MOD_FIRST + 8, ("m3", None), 1, "g_ffn", 32)
                for k in range(KC):
                    dve.wait_ge(a["ws_a"].sem, k + 1)
                    z_low(k, W, row(S, k, W)).then_inc(a["ws_v"].sem, 1)

                def residual(which, gt):
                    def body(n, s, m):
                        for t in range(2):
                            for c in range(C):
                                x = row(X, 2 * n + t, NX, c * NX)
                                g = MOD[:, ds(2 * n + (t + gt + 48 * c), 1)] if not isinstance(n, int) else \
                                    MOD[:, 2 * n + t + gt + 48 * c:2 * n + t + gt + 48 * c + 1]
                                stt(x, bank(2 * s + t, NX, c * NX), g, x, MUL, ADD)\
                                    .then_inc(*((slab_out[s], 1) if (t, c) == (1, C - 1) else (a[which + "_v"].sem, 1)))
                    return body

                stage(l, "w_out", residual("wo", 16))
                if l == 0:
                    modulation(32, 48, NMOD, ("m5", "a3"), 1, "g_ffn", 32)
                inverse_root("n2", C)
                norm("n2", 1, 24, C)
                for f in range(len(FF_PARTS)):
                    fa, fv = a[f"fi{f}_a"], a[f"fi{f}_v"]

                    def ff_in(n, s, m):
                        dve.wait_ge(fa.sem, fa.at(n, "sg"))
                        tt(tmp(2 + s, 0, W), tmp(s, 0, W), bank(2 * s, W), MUL).then_inc(fv.sem, 1)
                        dve.wait_ge(fv.sem, fv.at(n, "p"))
                        tt(tmp(4 + s, 0, W), tmp(2 + s, 0, W), bank(2 * s + 1, W), MUL).then_inc(fv.sem, 1)
                        dve.wait_ge(fa.sem, fa.at(n, "zh"))
                        z_low(n, W, tmp(4 + s, 0, W)).then_inc(slab_out[s], 1)

                    stage(l, f"ff_in{f}", ff_in)
                    all_out(dve, l, f"ff_out{f}")
                    stage(l, f"ff_out{f}", residual(f"fo{f}", 40))
                    if (l, f) != (DEPTH - 1, len(FF_PARTS) - 1):
                        all_out(dve, l, f"ff_in{f + 1}") if f + 1 < len(FF_PARTS) else all_out(dve, l + 1, "c_in")
            dve.wait_ge(fin_a, KC + 1)
            V.reciprocal(tmp(1, 0, NX), tmp(0, 0, NX)).then_inc(fin_v, 1)
            dve.wait_ge(fin_v, 1)
            for k in range(KC):
                stt(CD[:, k * NX:(k + 1) * NX], row(X, k, NX), par(0, "g_final", k), tmp(1, 0, NX), MUL, MUL)\
                    .then_inc(fin_v, 1)


def slab_tiles(w, c0, c1=None, r0=0):
    cols = [c0, c0 + P if c1 is None else c1]
    rows = min(w.shape[0] - r0, D)
    out = np.zeros((P, KC, 2, P), np.float32)
    for t, c in enumerate(cols):
        out[:, :rows // P, t, :] = w[r0:r0 + rows, c:c + P].reshape(rows // P, P, P).transpose(1, 0, 2)
    return out.reshape(P, SLAB)


def layer_stream(w_in, w_a, w_b, w_c, w_d, w_out, w_fi, w_fo):
    at = dict(zip(("a_b", "a_c", "a_u", "q", "k", "v", "r_g", "r_u", "d_v", "d_g", "gl"),
                  np.cumsum([0, D, D, D, D, 256, 256, D, D, D, D])))
    ff = FF_TILES * P
    s = []

    def two(x, y):
        s.extend(slab_tiles(w_in, at[x] + j * P, at[y] + j * P) for j in range(KC))

    def branch(w, n):
        for j in range(KC):
            c = at["gl"] + n * D + j * P
            g, y = (slab_tiles(x, a, a).reshape(P, KC, 2, P)[:, :, 0] for x, a in ((w_in, c), (w, j * P)))
            s.append(np.stack([g, y], axis=2).reshape(P, SLAB))

    two("r_u", "r_g")
    s.append(slab_tiles(w_in, at["k"]))
    s.append(slab_tiles(w_in, at["v"]))
    s.extend(slab_tiles(w_in, at["q"] + 2 * j * P) for j in range(KC // 2))
    branch(w_c, 2)
    two("d_v", "d_g")
    branch(w_b, 1)
    two("a_c", "a_u")
    s.extend(slab_tiles(w_in, at["a_b"] + 2 * j * P) for j in range(KC // 2))
    branch(w_a, 0)
    branch(w_d, 3)
    s.extend(slab_tiles(w_out, 2 * j * P) for j in range(KC // 2))
    first = 0
    for n in FF_PARTS:
        s.extend(slab_tiles(w_fi, (first + j) * P, ff + (first + j) * P) for j in range(n))
        s.extend(slab_tiles(w_fo[first * P:(first + n) * P], 2 * j * P) for j in range(KC // 2))
        first += n
    return s


def constants():
    half = HD // 2
    inv = (10000.0 ** (-np.arange(0, half, 2, dtype=np.float32) / half)).astype(np.float32)
    tok = np.arange(NX)
    row_, col = (tok // 64).astype(np.float32), (tok % 64).astype(np.float32)
    ar, ac = row_[:, None] * inv, col[:, None] * inv
    ang = np.concatenate([ar, ar, ac, ac], axis=-1).astype(np.float32)
    q = HD // 4
    sign = np.repeat(np.array([-1, 1, -1, 1], np.float32), q)
    rope = np.concatenate([np.cos(ang).T, (np.sin(ang) * sign).T], axis=1).astype(np.float32)
    swap = np.concatenate([np.arange(q) + q, np.arange(q), np.arange(q) + 3 * q, np.arange(q) + 2 * q])
    rot = np.zeros((P, P), np.float32)
    rot[swap, np.arange(P)] = 1.0
    i, j = np.arange(P)[:, None], np.arange(P)[None, :]
    tri0 = np.where(j <= i, 0.0, NEG).astype(np.float32)
    tri1 = np.where(j >= i, 0.0, NEG).astype(np.float32)
    sel = np.zeros((P, 2), np.float32)
    for g in range(4):
        sel[32 * g, 0] = sel[32 * g + 1, 1] = 1.0
    return rope, np.concatenate([np.eye(P, dtype=np.float32), np.ones((P, P), np.float32), rot, tri0, tri1, sel], axis=1)


def columns(v):
    return np.asarray(v).reshape(-1, P).T


def kernel(**inputs):
    import concourse.bacc as bacc
    from concourse.bass_utils import run_bass_kernel_spmd

    w = {k: np.asarray(v) for k, v in inputs.items()}
    stream, modw, lruw, prm = [], [], [], []
    for l in range(DEPTH):
        stream += layer_stream(*(w[k][l] for k in ("w_in", "w_a_out", "w_b_out", "w_c_out", "w_d_out", "w_out",
                                                   "w_ffn_in", "w_ffn_out")))
        modw += [slab_tiles(w["w_mod"][l], 2 * j * P) for j in range(NMOD)]
        gates = np.stack([w["lru_wa"][l, 0], w["lru_wx"][l, 0], w["lru_wa"][l, 1], w["lru_wx"][l, 1]])
        lruw.append(gates.transpose(2, 1, 0, 3).reshape(P, KC * NT))
        prm.append(np.concatenate(
            [columns(w[k][l]) for k in ("b_mod", "g_mix", "g_ffn", "conv_a", "conv_c", "conv_c_b", "lru_ba", "lru_bx",
                                        "lru_lam", "conv_d", "conv_d_b", "ln_d_g", "ln_d_b")]
            + [columns(w["g_final"]), np.broadcast_to(w["sink"][l], (P, HEADS))], axis=1))
    tokens = np.concatenate([w["x"][0], w["ctx"][0]], axis=0)
    xT = tokens.T.reshape(KC, P, NT).transpose(1, 0, 2).reshape(P, KC * NT)
    cT = np.stack([w["c"][0], w["c_ctx"]], axis=-1).reshape(KC, P, 2).transpose(1, 0, 2).reshape(P, 2 * KC)
    rope, consts = constants()
    arrays = {"stream": np.stack(stream), "modw": np.stack(modw), "lruw": np.stack(lruw), "xT": xT, "cT": cT,
              "prm": np.concatenate(prm, axis=1), "rope": rope, "consts": consts}
    arrays = {k: np.ascontiguousarray(v) for k, v in arrays.items()}

    nc = bacc.Bacc("TRN2", target_bir_lowering=False, num_devices=1)
    args = [nc.dram_tensor("in_" + k, v.shape, F32, kind="ExternalInput").ap() for k, v in arrays.items()]
    out = nc.dram_tensor("outT", (P, KC * NX), F32, kind="ExternalOutput").ap()
    build(nc, *args, out)
    r = run_bass_kernel_spmd(nc, [{"in_" + k: v for k, v in arrays.items()}], core_ids=[0])
    y = np.asarray(r.results[0]["outT"]).reshape(P, KC, NX)
    return y.transpose(2, 1, 0).reshape(1, NX, D)
```
